# Optimizing a Trainium2 kernel written in Bass

```python
import math
import jax, jax.numpy as jnp
from jax import lax
import numpy as np

D_MODEL = 1024
BATCH = 1
SEQ = 256
DEPTH = 1

HEAD_DIM = 64
RWKV_HEADS = 12
RWKV_WIDTH = RWKV_HEADS * HEAD_DIM
DECAY_LORA = 64
ICLR_LORA = 64
GATE_LORA = 128
ATTN_GROUPS = ((128, 1), (512, 4), (2048, 16))
HEADS_PER_GROUP = 4
ATTN_HEADS = HEADS_PER_GROUP * len(ATTN_GROUPS)
ATTN_WIDTH = ATTN_HEADS * HEAD_DIM
ATTN_OUT_WIDTH = HEADS_PER_GROUP * HEAD_DIM
ATTN_BLOCK = 128
ROPE_THETA = 10000.0
D_FF = -(-8 * D_MODEL // (3 * 256)) * 256
SHIFT_WIDTH = 3 * RWKV_WIDTH + DECAY_LORA + ICLR_LORA + GATE_LORA
IN_WIDTH = SHIFT_WIDTH + 3 * ATTN_WIDTH + 2 * D_MODEL
NORM_EPS = 1e-6
GN_EPS = 64e-5


def _split(t, sizes):
    idx = np.cumsum(sizes)[:-1].tolist()
    return jnp.split(t, idx, axis=-1)

def rms_norm(x, g):
    xf = x.astype(jnp.float32)
    y = xf * lax.rsqrt(jnp.mean(xf * xf, axis=-1, keepdims=True) + NORM_EPS)
    return (y * g.astype(jnp.float32)).astype(x.dtype)

def modulate(h, shift, scale):
    return h * (1.0 + scale[:, None, :]) + shift[:, None, :]

def token_shift(p):
    return jnp.pad(p, ((0, 0), (1, 0), (0, 0)))[:, :-1]

def apply_rope(t, pos):
    half = t.shape[-1] // 2
    inv_freq = ROPE_THETA ** (-jnp.arange(half, dtype=jnp.float32) / half)
    ang = pos.astype(jnp.float32)[:, None] * inv_freq[None, :]
    cos, sin = jnp.cos(ang), jnp.sin(ang)
    tf = t.astype(jnp.float32)
    t1, t2 = tf[..., :half], tf[..., half:]
    return jnp.concatenate([t1 * cos - t2 * sin, t2 * cos + t1 * sin], axis=-1).astype(t.dtype)

def rwkv7_recurrence(r, w, k, v, kk, a):
    B, S, H, N = r.shape

    def step(state, inp):
        r_t, w_t, k_t, v_t, kk_t, a_t = inp
        sa = -jnp.einsum('bhvk,bhk->bhv', state, kk_t)
        state = (state * w_t[:, :, None, :]
                 + sa[..., None] * (kk_t * a_t)[:, :, None, :]
                 + v_t[..., None] * k_t[:, :, None, :])
        y = jnp.einsum('bhvk,bhk->bhv', state, r_t)
        return state, y

    xs = tuple(jnp.moveaxis(t.astype(jnp.float32), 1, 0) for t in (r, w, k, v, kk, a))
    init = jnp.zeros((B, H, N, N), jnp.float32)
    _, ys = lax.scan(step, init, xs)
    return jnp.moveaxis(ys, 0, 1)

def rwkv7_mix(pr, pk, pv, pw, pa, pg, w0, w2, a0, a2, g2, k_k, k_a, r_k, lnx_w, lnx_b, w_a):
    B, S, _ = pr.shape
    f32 = jnp.float32
    heads = lambda t: t.reshape(B, S, RWKV_HEADS, HEAD_DIM)
    wf = (w0 + jnp.tanh(pw) @ w2).astype(f32)
    decay = jnp.exp(-jnp.exp(-jax.nn.softplus(-wf) - 0.5))
    a = jax.nn.sigmoid((a0 + pa @ a2).astype(f32))
    gate = (jax.nn.sigmoid(pg) @ g2).astype(f32)
    kk = heads((pk * k_k).astype(f32))
    kk = kk / jnp.maximum(jnp.linalg.norm(kk, axis=-1, keepdims=True), 1e-12)
    k = pk.astype(f32) * (1.0 + (a - 1.0) * k_a.astype(f32))
    rf, vf = heads(pr.astype(f32)), heads(pv.astype(f32))
    y = rwkv7_recurrence(rf, heads(decay), heads(k), vf, kk, heads(a))
    mean = jnp.mean(y, axis=-1, keepdims=True)
    var = jnp.mean(jnp.square(y - mean), axis=-1, keepdims=True)
    yn = ((y - mean) * lax.rsqrt(var + GN_EPS)).reshape(B, S, RWKV_WIDTH)
    yn = yn * lnx_w.astype(f32) + lnx_b.astype(f32)
    bonus = (jnp.sum(rf * heads(k) * r_k.astype(f32), axis=-1, keepdims=True) * vf).reshape(B, S, RWKV_WIDTH)
    return ((yn + bonus) * gate).astype(pr.dtype) @ w_a

def dilated_window_attn(q, k, v, window, dilation):
    B, H, S, hd = q.shape
    span = window // dilation
    n_prev = -(-span // ATTN_BLOCK)
    chunk = dilation * ATTN_BLOCK
    s_pad = -(-S // chunk) * chunk
    L = s_pad // dilation
    nb = L // ATTN_BLOCK

    def to_blocks(t):
        t = jnp.pad(t, ((0, 0), (0, 0), (0, s_pad - S), (0, 0)))
        t = t.reshape(B, H, L, dilation, hd).transpose(0, 1, 3, 2, 4)
        return t.reshape(B, H, dilation, nb, ATTN_BLOCK, hd)

    def with_prev(t):
        padded = jnp.pad(t, ((0, 0), (0, 0), (0, 0), (n_prev, 0), (0, 0), (0, 0)))
        return jnp.concatenate([padded[:, :, :, i:i + nb] for i in range(n_prev + 1)], axis=4)

    qb, kb, vb = to_blocks(q), to_blocks(k), to_blocks(v)
    kc, vc = with_prev(kb), with_prev(vb)
    s = jnp.einsum('bhrnqd,bhrnkd->bhrnqk', qb, kc, preferred_element_type=jnp.float32)
    s = s * (HEAD_DIM ** -0.5)
    n_keys = (n_prev + 1) * ATTN_BLOCK
    qi = jnp.arange(ATTN_BLOCK)[:, None]
    kj = jnp.arange(n_keys)[None, :]
    dist = qi + n_prev * ATTN_BLOCK - kj
    key_pos = jnp.arange(nb)[:, None, None] * ATTN_BLOCK + kj[None] - n_prev * ATTN_BLOCK
    valid = (dist >= 0) & (dist <= span) & (key_pos >= 0)
    s = jnp.where(valid, s, -jnp.inf)
    lse = jax.nn.logsumexp(s, axis=-1)
    p = jnp.exp(s - lse[..., None])
    o = jnp.einsum('bhrnqk,bhrnkd->bhrnqd', p, vc.astype(jnp.float32))
    o = o.reshape(B, H, dilation, L, hd).transpose(0, 1, 3, 2, 4).reshape(B, H, s_pad, hd)[:, :, :S]
    lse = lse.reshape(B, H, dilation, L).transpose(0, 1, 3, 2).reshape(B, H, s_pad)[:, :, :S]
    return o, lse

def dilated_attention_mix(pq, pk, pv, w_b):
    B, S, _ = pq.shape
    heads = lambda t: t.reshape(B, S, ATTN_HEADS, HEAD_DIM).transpose(0, 2, 1, 3)
    pos = jnp.arange(S)
    q, k, v = apply_rope(heads(pq), pos), apply_rope(heads(pk), pos), heads(pv)
    outs, lses = [], []
    for g, (window, dilation) in enumerate(ATTN_GROUPS):
        sl = slice(g * HEADS_PER_GROUP, (g + 1) * HEADS_PER_GROUP)
        o, l = dilated_window_attn(q[:, sl], k[:, sl], v[:, sl], window, dilation)
        outs.append(o)
        lses.append(l)
    outs = jnp.stack(outs)
    wts = jax.nn.softmax(jnp.stack(lses), axis=0)
    o = jnp.sum(wts[..., None] * outs, axis=0)
    o = o.transpose(0, 2, 1, 3).reshape(B, S, ATTN_OUT_WIDTH).astype(pq.dtype)
    return o @ w_b

def first_inputs(seed: int = 0) -> dict:
    key = jax.random.key(seed)
    ks = iter(jax.random.split(key, 32))
    f32 = jnp.float32
    nrm = lambda shape, sc: jax.random.normal(next(ks), shape, f32) * sc
    L, D, RW = DEPTH, D_MODEL, RWKV_WIDTH
    return {
        "x": nrm((BATCH, SEQ, D), 1.0),
        "c": nrm((BATCH, D), 1.0),
        "w_ada": nrm((L, D, 6 * D), 0.5 * D ** -0.5),
        "b_ada": nrm((L, 6 * D), 0.02),
        "g_pre_mix": 1.0 + nrm((L, D), 0.05),
        "g_post_mix": 1.0 + nrm((L, D), 0.05),
        "w_in": nrm((L, D, IN_WIDTH), D ** -0.5),
        "mu_shift": jax.random.uniform(next(ks), (L, SHIFT_WIDTH), f32, 0.0, 1.0),
        "w0": jax.random.uniform(next(ks), (L, RW), f32, -5.0, -0.5),
        "w2": nrm((L, DECAY_LORA, RW), 0.1 * DECAY_LORA ** -0.5),
        "a0": nrm((L, RW), 0.5),
        "a2": nrm((L, ICLR_LORA, RW), 0.5 * ICLR_LORA ** -0.5),
        "g2": nrm((L, GATE_LORA, RW), GATE_LORA ** -0.5),
        "k_k": 0.85 + nrm((L, RW), 0.05),
        "k_a": 1.0 + nrm((L, RW), 0.05),
        "r_k": nrm((L, RWKV_HEADS, HEAD_DIM), 0.1),
        "lnx_w": 1.0 + nrm((L, RW), 0.05),
        "lnx_b": nrm((L, RW), 0.02),
        "w_a": nrm((L, RW, D), RW ** -0.5),
        "w_b": nrm((L, ATTN_OUT_WIDTH, D), ATTN_OUT_WIDTH ** -0.5),
        "w_out": nrm((L, D, D), D ** -0.5),
        "g_pre_ffn": 1.0 + nrm((L, D), 0.05),
        "g_post_ffn": 1.0 + nrm((L, D), 0.05),
        "w_ffn_in": nrm((L, D, 2 * D_FF), D ** -0.5),
        "w_ffn_out": nrm((L, D_FF, D), D_FF ** -0.5),
    }

def first_block(x, c, w_ada, b_ada, g_pre_mix, g_post_mix, w_in, mu_shift, w0, w2, a0, a2, g2,
              k_k, k_a, r_k, lnx_w, lnx_b, w_a, w_b, w_out, g_pre_ffn, g_post_ffn,
              w_ffn_in, w_ffn_out):
    for i in range(DEPTH):
        mod = jax.nn.silu(c) @ w_ada[i] + b_ada[i]
        shift_m, scale_m, gate_m, shift_f, scale_f, gate_f = jnp.split(mod, 6, axis=-1)

        h = modulate(rms_norm(x, g_pre_mix[i]), shift_m, scale_m)
        p = h @ w_in[i]
        p_shift, pq, pk_att, pv_att, p_ga, p_gb = _split(
            p, [SHIFT_WIDTH, ATTN_WIDTH, ATTN_WIDTH, ATTN_WIDTH, D_MODEL, D_MODEL])
        p_shift = p_shift + mu_shift[i] * (token_shift(p_shift) - p_shift)
        pr, pk, pv, pw, pa, pg = _split(
            p_shift, [RWKV_WIDTH, RWKV_WIDTH, RWKV_WIDTH, DECAY_LORA, ICLR_LORA, GATE_LORA])
        y_a = rwkv7_mix(pr, pk, pv, pw, pa, pg, w0[i], w2[i], a0[i], a2[i], g2[i],
                        k_k[i], k_a[i], r_k[i], lnx_w[i], lnx_b[i], w_a[i])
        y_b = dilated_attention_mix(pq, pk_att, pv_att, w_b[i])
        merged = jax.nn.sigmoid(p_ga) * y_a + jax.nn.sigmoid(p_gb) * y_b
        x = x + gate_m[:, None, :] * rms_norm(merged @ w_out[i], g_post_mix[i])

        h = modulate(rms_norm(x, g_pre_ffn[i]), shift_f, scale_f)
        u, gt = jnp.split(h @ w_ffn_in[i], 2, axis=-1)
        f = (jax.nn.silu(u) * gt) @ w_ffn_out[i]
        x = x + gate_f[:, None, :] * rms_norm(f, g_post_ffn[i])
    return x


DEPTH_2 = 2

N_META = 16
BLOCK = 128
N_PAD = BLOCK - N_META
FOX_HEADS = 8
FOX_HEAD_DIM = D_MODEL // 16
FOX_WIDTH = FOX_HEADS * FOX_HEAD_DIM
GLA_HEADS = 4
GLA_WIDTH = D_MODEL // 2
GLA_DV = GLA_WIDTH // GLA_HEADS
GLA_DK = GLA_DV // 2
GLA_KWIDTH = GLA_HEADS * GLA_DK
GLA_GATE_RANK = 16
GLA_GATE_TEMP = 16.0
D_FF_2 = ((8 * D_MODEL // 3 + 127) // 128) * 128
RMS_EPS = 1e-6
SPLIT_SIZES = (FOX_WIDTH, FOX_WIDTH, FOX_WIDTH, FOX_HEADS, GLA_KWIDTH, GLA_KWIDTH, GLA_WIDTH, GLA_GATE_RANK, GLA_WIDTH, D_MODEL, D_MODEL)
N_IN = 3 * FOX_WIDTH + FOX_HEADS + 2 * GLA_KWIDTH + 2 * GLA_WIDTH + GLA_GATE_RANK + 2 * D_MODEL


def rmsnorm(x, gain):
    xf = x.astype(jnp.float32)
    y = xf * lax.rsqrt(jnp.mean(xf * xf, axis=-1, keepdims=True) + RMS_EPS)
    return (y * gain.astype(jnp.float32)).astype(x.dtype)

def swiglu(h, w_gu, w_down):
    gate, up = jnp.split(h @ w_gu, 2, axis=-1)
    return (jax.nn.silu(gate) * up) @ w_down

def to_heads(t, n_heads):
    b, l, _ = t.shape
    return t.reshape(b, l, n_heads, -1).transpose(0, 2, 1, 3)

def from_heads(t):
    b, h, l, d = t.shape
    return t.transpose(0, 2, 1, 3).reshape(b, l, h * d)

def fox_attention(q, k, v, log_f, key_valid):
    lp = q.shape[2]
    cum = jnp.cumsum(log_f, axis=-1)
    scale = FOX_HEAD_DIM ** -0.5
    outs = []
    for start in range(0, lp, BLOCK):
        end = start + BLOCK
        s = jnp.einsum('bhqd,bhkd->bhqk', q[:, :, start:end], k[:, :, :end]).astype(jnp.float32) * scale
        s = s + cum[:, :, start:end, None] - cum[:, :, None, :end]
        qpos = jnp.arange(start, end)[:, None]
        kpos = jnp.arange(end)[None, :]
        allowed = (kpos <= qpos) & (key_valid[None, :end] | (kpos == qpos))
        p = jax.nn.softmax(jnp.where(allowed, s, -jnp.inf), axis=-1)
        outs.append(jnp.einsum('bhqk,bhkd->bhqd', p.astype(v.dtype), v[:, :, :end]))
    return jnp.concatenate(outs, axis=2)

def gla_chunked(q, k, v, log_a):
    b, h, lp, dk = q.shape
    dv = v.shape[-1]
    n = lp // BLOCK

    def to_chunks(t):
        return jnp.moveaxis(t.reshape(b, h, n, BLOCK, t.shape[-1]), 2, 0)

    causal = jnp.tril(jnp.ones((BLOCK, BLOCK), dtype=bool))[:, :, None]

    def step(state, inp):
        qi, ki, vi, ai = inp
        cb = jnp.cumsum(ai, axis=2)
        qf, kf, vf = qi.astype(jnp.float32), ki.astype(jnp.float32), vi.astype(jnp.float32)
        inter = jnp.einsum('bhtk,bhkv->bhtv', qf * jnp.exp(cb), state)
        diff = cb[:, :, :, None, :] - cb[:, :, None, :, :]
        decay = jnp.exp(jnp.where(causal, diff, -jnp.inf))
        att = jnp.einsum('bhtk,bhsk,bhtsk->bhts', qf, kf, decay)
        intra = jnp.einsum('bhts,bhsv->bhtv', att, vf)
        last = cb[:, :, -1:, :]
        new_state = jnp.exp(last[:, :, 0, :, None]) * state + jnp.einsum('bhsk,bhsv->bhkv', kf * jnp.exp(last - cb), vf)
        return new_state, (inter + intra).astype(vi.dtype)

    s0 = jnp.zeros((b, h, dk, dv), jnp.float32)
    _, o = lax.scan(step, s0, (to_chunks(q), to_chunks(k), to_chunks(v), to_chunks(log_a)))
    return jnp.moveaxis(o, 0, 2).reshape(b, h, lp, dv)

def token_mixer(h, key_valid, w_in, w_alpha_up, b_alpha, b_f, g_gla_out, w_fox_o, w_gla_o, w_out):
    valid = key_valid.astype(jnp.float32)[None, :, None]
    points = np.cumsum(SPLIT_SIZES)[:-1].tolist()
    fq, fk, fv, ff, gq, gk, gv, ga, gr, g_merge_a, g_merge_b = jnp.split(h @ w_in, points, axis=-1)
    log_f = jax.nn.log_sigmoid(ff.astype(jnp.float32) + b_f.astype(jnp.float32)) * valid
    o_fox = fox_attention(to_heads(fq, FOX_HEADS), to_heads(fk, FOX_HEADS), to_heads(fv, FOX_HEADS),
                          log_f.transpose(0, 2, 1), key_valid)
    log_a = jax.nn.log_sigmoid((ga @ w_alpha_up).astype(jnp.float32) + b_alpha.astype(jnp.float32)) * (valid / GLA_GATE_TEMP)
    gk = gk * valid.astype(gk.dtype)
    o_gla = gla_chunked(to_heads(gq * (GLA_DK ** -0.5), GLA_HEADS), to_heads(gk, GLA_HEADS),
                        to_heads(gv, GLA_HEADS), to_heads(log_a, GLA_HEADS))
    o_gla = rmsnorm(o_gla, g_gla_out.reshape(GLA_HEADS, 1, GLA_DV))
    o_gla = from_heads(o_gla) * jax.nn.silu(gr)
    y = jax.nn.sigmoid(g_merge_a) * (from_heads(o_fox) @ w_fox_o) + jax.nn.sigmoid(g_merge_b) * (o_gla @ w_gla_o)
    return y @ w_out

def second_inputs(seed: int = 0) -> dict:
    key = jax.random.key(seed)
    ks = jax.random.split(key, 21)

    def nrm(k, shape, scale):
        return jax.random.normal(k, shape, jnp.float32) * scale

    def gain(k):
        return 1.0 + nrm(k, (DEPTH_2, D_MODEL), 0.02)

    return {
        "x": nrm(ks[0], (BATCH, SEQ, D_MODEL), 1.0),
        "meta_tokens": nrm(ks[1], (N_META, D_MODEL), 1.0),
        "w_in": nrm(ks[2], (DEPTH_2, D_MODEL, N_IN), D_MODEL ** -0.5),
        "w_alpha_up": nrm(ks[3], (DEPTH_2, GLA_GATE_RANK, GLA_KWIDTH), GLA_GATE_RANK ** -0.5),
        "b_alpha": nrm(ks[4], (DEPTH_2, GLA_KWIDTH), 0.1),
        "b_f": 2.0 + nrm(ks[5], (DEPTH_2, FOX_HEADS), 0.1),
        "g_gla_out": 1.0 + nrm(ks[6], (DEPTH_2, GLA_WIDTH), 0.02),
        "w_fox_o": nrm(ks[7], (DEPTH_2, FOX_WIDTH, D_MODEL), FOX_WIDTH ** -0.5),
        "w_gla_o": nrm(ks[8], (DEPTH_2, GLA_WIDTH, D_MODEL), GLA_WIDTH ** -0.5),
        "w_out": nrm(ks[9], (DEPTH_2, D_MODEL, D_MODEL), D_MODEL ** -0.5),
        "w_ffn1_gu": nrm(ks[10], (DEPTH_2, D_MODEL, 2 * D_FF_2), D_MODEL ** -0.5),
        "w_ffn1_down": nrm(ks[11], (DEPTH_2, D_FF_2, D_MODEL), D_FF_2 ** -0.5),
        "w_ffn2_gu": nrm(ks[12], (DEPTH_2, D_MODEL, 2 * D_FF_2), D_MODEL ** -0.5),
        "w_ffn2_down": nrm(ks[13], (DEPTH_2, D_FF_2, D_MODEL), D_FF_2 ** -0.5),
        "g_pre_ffn1": gain(ks[14]),
        "g_post_ffn1": gain(ks[15]),
        "g_pre_mix": gain(ks[16]),
        "g_post_mix": gain(ks[17]),
        "g_pre_ffn2": gain(ks[18]),
        "g_post_ffn2": gain(ks[19]),
    }

def second_block(x, meta_tokens, w_in, w_alpha_up, b_alpha, b_f, g_gla_out, w_fox_o, w_gla_o, w_out,
              w_ffn1_gu, w_ffn1_down, w_ffn2_gu, w_ffn2_down,
              g_pre_ffn1, g_post_ffn1, g_pre_mix, g_post_mix, g_pre_ffn2, g_post_ffn2):
    b = x.shape[0]
    pad = jnp.zeros((b, N_PAD, D_MODEL), x.dtype)
    meta = jnp.broadcast_to(meta_tokens.astype(x.dtype)[None], (b, N_META, D_MODEL))
    h = jnp.concatenate([pad, meta, x], axis=1)
    key_valid = jnp.arange(h.shape[1]) >= N_PAD
    for l in range(DEPTH_2):
        h = h + 0.5 * rmsnorm(swiglu(rmsnorm(h, g_pre_ffn1[l]), w_ffn1_gu[l], w_ffn1_down[l]), g_post_ffn1[l])
        mix = token_mixer(rmsnorm(h, g_pre_mix[l]), key_valid, w_in[l], w_alpha_up[l], b_alpha[l], b_f[l],
                          g_gla_out[l], w_fox_o[l], w_gla_o[l], w_out[l])
        h = h + rmsnorm(mix, g_post_mix[l])
        h = h + 0.5 * rmsnorm(swiglu(rmsnorm(h, g_pre_ffn2[l]), w_ffn2_gu[l], w_ffn2_down[l]), g_post_ffn2[l])
    return h[:, BLOCK:]


def setup_inputs(seed=0):
    out = dict(first_inputs(seed))
    for name, value in second_inputs(seed + 1).items():
        if name != "x":
            out[name + "_2"] = value
    return out


def reference(
    x, c, w_ada, b_ada, g_pre_mix, g_post_mix, w_in, mu_shift, w0, w2, a0, a2, g2, k_k, k_a,
    r_k, lnx_w, lnx_b, w_a, w_b, w_out, g_pre_ffn, g_post_ffn, w_ffn_in, w_ffn_out,
    meta_tokens_2, w_in_2, w_alpha_up_2, b_alpha_2, b_f_2, g_gla_out_2, w_fox_o_2, w_gla_o_2,
    w_out_2, w_ffn1_gu_2, w_ffn1_down_2, w_ffn2_gu_2, w_ffn2_down_2, g_pre_ffn1_2,
    g_post_ffn1_2, g_pre_mix_2, g_post_mix_2, g_pre_ffn2_2, g_post_ffn2_2,
):
    x = first_block(
        x, c, w_ada, b_ada, g_pre_mix, g_post_mix, w_in, mu_shift, w0, w2, a0, a2, g2, k_k, k_a,
        r_k, lnx_w, lnx_b, w_a, w_b, w_out, g_pre_ffn, g_post_ffn, w_ffn_in, w_ffn_out,
    )
    return second_block(
        x, meta_tokens_2, w_in_2, w_alpha_up_2, b_alpha_2, b_f_2, g_gla_out_2, w_fox_o_2,
        w_gla_o_2, w_out_2, w_ffn1_gu_2, w_ffn1_down_2, w_ffn2_gu_2, w_ffn2_down_2,
        g_pre_ffn1_2, g_post_ffn1_2, g_pre_mix_2, g_post_mix_2, g_pre_ffn2_2, g_post_ffn2_2,
    )


_drawn_inputs = setup_inputs


def setup_inputs(seed=0):
    import zlib

    import numpy as np

    out = dict(_drawn_inputs(seed))
    spreads = {}
    factors = {'w2': 8.0,
     'lnx_b': 4.845,
     'g_gla_out_2': 11.777,
     'g_post_ffn1_2': 3.055,
     'g_pre_ffn2_2': 4.045,
     'g_post_ffn2_2': 5.836,
     'b_f_2': 46.968,
     'g_post_mix_2': 3.161}
    for name, (base, spread) in spreads.items():
        noise = np.random.default_rng([zlib.crc32(name.encode()), seed]).standard_normal(out[name].shape)
        drawn = base * np.exp(spread * noise) if base else spread * noise
        out[name] = __import__('jax').numpy.asarray(drawn.astype(out[name].dtype))
    for name, factor in factors.items():
        out[name] = (out[name] * factor).astype(out[name].dtype)
    return out
```

```python
from contextlib import ExitStack

import numpy as np
import concourse.bass as bass
from concourse import mybir

F32 = mybir.dt.float32
F32R = mybir.dt.float32r
ALU = mybir.AluOpType
ACT = mybir.ActivationFunctionType
AX = mybir.AxisListType.X

P = 128
D = 1024
KT = D // P
SEQ = 256
META = 16
TOK = META + SEQ
HD = 64
EPS = 1e-6
NEG = -1e30

RW = 768
RT = RW // P
SHIFT_TILES = 20
GN_EPS = 64e-5
DECAY = float(np.exp(-0.5))
CHUNK = 64
NCH = SEQ // CHUNK
FF = 2816
FT = FF // P
GROUPS = ((128, 1), (512, 4), (2048, 16))

LAYERS = 2
FOX_PAIRS = 4
GLA_C = 68
GLA_N = TOK // GLA_C
BLOCKS = ((0, 16), (16, 144), (144, 272))

GU_K, DOWN_K, IN_K, AB_K, OUT_K = 16, FT, 16, 8, 16
ADA_FIRST, ADA_LAST = 8, 16
IN1, AB, OUT, GU, DOWN = 27, 8, 4, 22, 8
SINGLES, IN2 = 3, 19
M_AB1 = IN1
M_OUT1 = M_AB1 + AB
M_GU1 = M_OUT1 + OUT
M_DOWN1 = M_GU1 + GU
M_LAYER = M_DOWN1 + DOWN
L_GUA, L_DOWNA = 0, GU
L_SINGLE = GU + DOWN
L_IN = L_SINGLE + SINGLES
L_AB = L_IN + IN2
L_OUT = L_AB + AB
L_GUB = L_OUT + OUT
L_DOWNB = L_GUB + GU
L_PANELS = L_DOWNB + DOWN
assert L_PANELS % 2 == 0

T_R, T_K, T_V, T_WA, T_G = 0, 6, 12, 18, 19
T_FQ, T_FK, T_FV, T_GQ, T_GK, T_GV, T_GR, T_GA, T_GB = 0, 4, 8, 12, 14, 16, 20, 24, 32


def vector_table():
    at, cols = {}, 0
    for name, n in (("c", 8), ("b_ada", 48), ("g_pre_mix", 8), ("g_post_mix", 8), ("mu", 20), ("w0", 6), ("a0", 6),
                    ("k_k", 6), ("k_a", 6), ("r_k", 6), ("lnx_w", 6), ("lnx_b", 6), ("g_pre_ffn", 8),
                    ("g_post_ffn", 8)):
        at[name] = (cols, n)
        cols += n
    first = cols
    for name, n in (("pre1", 8), ("post1", 8), ("pre_mix", 8), ("post_mix", 8), ("pre2", 8), ("post2", 8),
                    ("b_alpha", 2), ("b_f", 1), ("g_gla", 4)):
        at[name] = (cols, n)
        cols += n
    per_layer = cols - first
    return at, cols + per_layer * (LAYERS - 1), per_layer


VEC, VEC_COLS, VEC_LAYER = vector_table()
CONST = {}
_at = 0
for _name, _n in (("ident", 128), ("rot", 128), ("mask_att", 768), ("mask_fox", 272), ("up_strict", 64),
                  ("lo_strict", 64), ("up_incl", 64), ("i2", 64), ("pair_ones", 128),
                  ("cos", 256), ("sin", 256), ("gla_mask", 68), ("eye8", 8)):
    CONST[_name] = (_at, _n)
    _at += _n
CONST_COLS = _at


def constants():
    c = np.zeros((P, CONST_COLS), np.float32)

    def put(name, a):
        at, n = CONST[name]
        c[:a.shape[0], at:at + n] = a.reshape(a.shape[0], n)

    i = np.arange(P)
    put("ident", np.eye(P))
    rot = np.zeros((P, P))
    for m in range(P):
        h, o = divmod(m, HD)
        if o < HD // 2:
            rot[h * HD + o + HD // 2, m] = -1.0
        else:
            rot[h * HD + o - HD // 2, m] = 1.0
    put("rot", rot)
    q, k = i[:, None], i[None, :]
    masks = np.zeros((P, 3, 2, P))
    for g, (window, dil) in enumerate(GROUPS):
        before, diag = q + P - k, q - k
        masks[:, g, 0] = np.where((before % dil == 0) & (before <= window), 0.0, NEG)
        masks[:, g, 1] = np.where((diag % dil == 0) & (diag >= 0) & (diag <= window), 0.0, NEG)
    put("mask_att", masks)
    put("mask_fox", np.concatenate([np.zeros((P, 144)), np.where(q >= k, 0.0, NEG)], 1))
    same = (q // CHUNK) == (k // CHUNK)
    s, t = (i % CHUNK)[:, None], np.arange(CHUNK)[None, :]
    put("up_strict", np.where(s < t, 1.0, 0.0))
    put("lo_strict", np.where(s > t, 1.0, 0.0))
    put("up_incl", np.where(s <= t, 1.0, 0.0))
    put("i2", np.where(s == t, 1.0, 0.0))
    put("pair_ones", np.where(same, 1.0, 0.0))
    half = HD // 2
    inv = (10000.0 ** (-np.arange(half, dtype=np.float32) / half)).astype(np.float32)
    ang = np.arange(SEQ, dtype=np.float32)[None, :] * inv[i % half][:, None]
    put("cos", np.cos(ang))
    put("sin", np.sin(ang))
    g = np.arange(GLA_C)
    put("gla_mask", np.where(g[:, None] <= g[None, :], 1.0, 0.0))
    put("eye8", np.eye(8))
    return c


class Panel:

    def __init__(self, half, par, lead):
        self.half, self.par, self.lead = half, par, lead

    @classmethod
    def of(cls, m, loop=0):
        return cls(m // 2 + loop, m % 2, ADA_FIRST if m < IN1 else ADA_FIRST + ADA_LAST)

    def ahead2(self):
        return Panel(self.half + 1, self.par, self.lead)

    def count(self, extra):
        return self.half * 2 + (self.par + extra)

    def landed(self):
        return (self.half + (self.lead // 2 + 1)) * 16


def section(eng, start, count, fn, loop=0, after=(None, None)):
    pairs = (count - 2) // 2
    if pairs > 0:
        with eng.Fori(0, pairs) as i:
            for b in range(2):
                fn(i * 2 + b, Panel.of(start + b, loop + i), "same")
    for t in range(2 * max(pairs, 0), count):
        left = count - 1 - t
        fn(t, Panel.of(start + t, loop), "same" if left >= 2 else after[1 - left])


class Kernel:
    pass


def allocate(k, nc, ctx):
    where = [16512]

    def at(name, shape, dt=F32, offset=None):
        size = 4 * int(np.prod(shape[1:]))
        here = where[0] if offset is None else offset
        t = nc.alloc_sbuf_tensor_at(name, shape, dt, offset=here)
        here += -(-size // 32) * 32
        if offset is None:
            where[0] = here
        return t, here

    def fixed(name, shape, dt=F32):
        return at(name, shape, dt)[0]

    def chain(start, *items):
        out = []
        for name, shape, *dt in items:
            t, start = at(name, shape, dt[0] if dt else F32, offset=start)
            out.append(t)
        return out, start

    k.land = fixed("land", [P, 2, FT * P])
    k.w_hi = fixed("w_hi", [P, 2, FT * P], F32R)
    k.w_lo = fixed("w_lo", [P, 2, FT * P], F32R)
    k.x = fixed("x", [P, KT, TOK])
    k.const = fixed("const", [P, CONST_COLS])
    k.vec = fixed("vec", [P, VEC_COLS])
    k.ssum = fixed("ssum", [P, TOK])
    k.root = fixed("root", [P, TOK])
    k.rstd = fixed("rstd", [P, TOK])
    norm_at = where[0]
    k.sq = fixed("sq", [P, 2, TOK])
    k.sq_post = fixed("sq_post", [P, 4, TOK])
    k.upd = fixed("upd", [P, 2, TOK])
    norm_end = where[0]
    k.mean_ones = fixed("mean_ones", [P, P])
    k.mod = fixed("mod", [P, 48])
    k.fold = fixed("fold", [P, 4, KT])
    k.csil = fixed("csil", [P, KT])
    k.eps = fixed("eps", [P, 2])
    h_at = where[0]
    k.h_hi = fixed("h_hi", [P, KT, TOK], F32R)
    k.h_lo = fixed("h_lo", [P, KT, TOK], F32R)
    k.f = fixed("f", [P, KT, TOK])
    h_end = where[0]
    arena = where[0]
    top = 229344

    (k.a_hi, k.a_lo, k.sig, k.t_ff, k.a_ff), end = chain(
        arena, ("a_hi", [P, FT, TOK], F32R), ("a_lo", [P, FT, TOK], F32R), ("sig", [P, 2, TOK]),
        ("t_ff", [P, 2, TOK]), ("a_ff", [P, 2, TOK]))
    assert end <= top, end

    (k.p_in, k.gates, k.c1), qkv_at = chain(
        arena, ("p_in", [P, SHIFT_TILES, SEQ + 1]), ("gates", [P, 16, SEQ]), ("c1", [P, RT, SEQ]))
    (k.qkv,), late = chain(qkv_at, ("qkv", [P, 18, SEQ]))
    (k.qs, k.kz), end = chain(h_at, ("qs", [P, 3, SEQ]), ("kz", [P, 3, 2, SEQ]),)
    (k.vs, k.vz, k.rt1, k.rt2), end = chain(
        end, ("vs", [P, 3, SEQ]), ("vz", [P, 3, 2, 2, P]), ("rt1", [P, SEQ]), ("rt2", [P, SEQ]))
    assert end <= h_end, (end, h_end)
    (k.s_att, k.p_att, k.pt_att, k.st_att, k.yb), end = chain(
        late, ("s_att", [P, 3, SEQ]), ("p_att", [P, 3, SEQ]), ("pt_att", [P, 6, P]), ("st_att", [P, 4]),
        ("yb", [P, 2, SEQ]))
    assert end <= top, (end, top)
    (k.bon, k.gate, k.tmp), end = chain(
        qkv_at, ("bon", [P, RT, SEQ]), ("gate", [P, RT, SEQ]), ("tmp", [P, RT, SEQ]))
    assert end <= late
    (k.beta, k.kap), rest = chain(late, ("beta", [P, RT, SEQ]), ("kap", [P, RT, SEQ]))
    (k.sw, k.kk, k.reset, k.w2p, k.a2p), end2 = chain(
        h_at, ("sw", [P, RT, SEQ]), ("kk", [P, RT, SEQ]), ("reset", [P, SEQ]), ("w2p", [P, RW]), ("a2p", [P, RW]))
    (k.g2,), end2 = chain(end2, ("g2", [P, RW]))
    assert end2 <= h_end
    (k.pc, k.yb_keep), rest = chain(rest, ("pc", [P, RT, NCH]), ("yb_keep", [P, 2, SEQ]))
    bd = [P, NCH, P]
    st = [P, NCH, CHUNK]
    names = (("al_bd", bd), ("be_bd", bd), ("ka_bd", bd), ("v_bd", bd), ("xr", bd), ("x_st", st),
             ("x_bd", bd), ("xt_bd", bd), ("rt_bd", bd), ("akt_bd", bd))
    place = h_at
    made = {}
    for name, shape in names:
        (made[name],), place = chain(place, (name, shape))
    assert place <= h_end, (place, h_end)
    place = rest
    for name, shape in (("qbt", st), ("qkt", st), ("au", bd), ("bet_bd", bd), ("bet_st", st), ("kat_bd", bd),
                        ("vt_bd", bd)):
        (made[name],), place = chain(place, (name, shape))
    assert place <= top, (place, top)
    place = qkv_at + 2 * 4 * RT * SEQ
    for name, shape in (("w_bd", bd), ("u_bd", bd), ("f_st", st), ("n_st", st)):
        (made[name],), place = chain(place, (name, shape))
    assert place <= late, (place, late)
    place = norm_at
    for name, shape in (("vt_st", st), ("u_st", st), ("m_bd", bd), ("s_st", [P, CHUNK]), ("s_bd", [P, 3, P])):
        (made[name],), place = chain(place, (name, shape))
    assert place <= norm_end, (place, norm_end)
    k.m = made
    (k.y1_hi, k.y1_lo), end = chain(arena, ("y1_hi", [P, KT, SEQ], F32R), ("y1_lo", [P, KT, SEQ], F32R))
    assert end <= arena + 4 * SHIFT_TILES * (SEQ + 1)

    (k.p2, k.y_hi, k.y_lo), mix_at = chain(
        arena, ("p2", [P, 40, TOK]), ("y_hi", [P, KT, TOK], F32R), ("y_lo", [P, KT, TOK], F32R))
    (k.small, k.wal, k.gcum), end = chain(mix_at, ("small", [P, TOK]), ("wal", [P, 256]), ("gcum", [P, 2, TOK]))
    (k.gst, k.cum, k.lf), end = chain(end, ("gst", [P, 2, 3, GLA_N]), ("cum", [P, TOK]), ("lf", [P, TOK]))
    k.mix_rest = end
    (k.e1, k.e2), end = chain(end, ("e1", [P, 2, TOK]), ("e2", [P, 2, TOK]))
    (k.minus8,), end = chain(end, ("minus8", [8, P]))
    assert end <= top, (end, top)
    (k.fqs, k.fkz, k.fvs, k.fvz, k.fs, k.fp, k.fpt, k.cumz), end = chain(
        h_at, ("fqs", [P, TOK]), ("fkz", [P, 2, TOK]), ("fvs", [P, TOK]), ("fvz", [P, 3, 2, P]),
        ("fs", [P, TOK]), ("fp", [P, TOK]), ("fpt", [P, 3, P]), ("cumz", [8, 8, TOK]))
    assert end <= h_end, (end, h_end)
    (k.fstat, k.fy), end = chain(
        k.mix_rest, ("fstat", [P, 4]), ("fy", [P, TOK]))
    assert end <= top
    (k.gkz, k.gks, k.gvs, k.gvt, k.gat, k.gkt, k.gs, k.gsm, k.go), end = chain(
        h_at, ("gkz", [P, 2, TOK]), ("gks", [P, TOK]), ("gvs", [P, 2, TOK]), ("gvt", [GLA_C, GLA_N, 2, P]),
        ("gat", [GLA_C, GLA_N, 2, GLA_C]), ("gkt", [GLA_C, GLA_N, P]), ("gs", [P, P]), ("gsm", [P, 3, 2, P]),
        ("go", [P, 2, TOK]))
    assert end <= h_end, (end, h_end)
    (k.gsq, k.gr_, k.gy), end = chain(k.mix_rest, ("gsq", [P, 2, TOK]), ("gr_", [P, 2, TOK]), ("gy", [P, TOK]))
    assert end <= top, (end, top)

    k.acc = ctx.enter_context(nc.psum_tensor("acc", [P, 4, 512], F32))
    k.mb = ctx.enter_context(nc.psum_tensor("mb", [P, 4, 512], F32))
    k.stat = k.mb[:, 3, 0:TOK]


def semaphores(k, sem):
    k.landed = (sem("landed0"), sem("landed1"))
    k.ada_done = sem("ada_done")
    k.hi_ready = sem("hi_ready")
    k.lo_ready = sem("lo_ready")
    k.panel_done = sem("panel_done")
    k.acc_free = sem("acc_free")
    k.x_loaded = sem("x_loaded")
    k.vec_loaded = sem("vec_loaded")
    k.lora_loaded = sem("lora_loaded")
    k.const_ready = sem("const_ready")
    k.csig = sem("csig")
    k.stored = sem("stored")
    k.sq_ready = sem("sq_ready")
    k.sq_used = sem("sq_used")
    k.sq_post_ready = sem("sq_post_ready")
    k.sums_ready = sem("sums_ready")
    k.stat_done = sem("stat_done")
    k.root_ready = sem("root_ready")
    k.n_ready = sem("n_ready")
    k.hh_ready = sem("hh_ready")
    k.hl_ready = sem("hl_ready")
    k.x_ready = sem("x_ready")
    k.sig_ready = sem("sig_ready")
    k.ah_ready = sem("ah_ready")
    k.al_ready = sem("al_ready")
    k.stage = sem("stage")
    k.pin_ready = sem("pin_ready")
    k.gla_zero = sem("gla_zero")
    k.gates_ready = sem("gates_ready")
    k.merged = sem("merged")
    k.yh_ready = sem("yh_ready")
    k.yl_ready = sem("yl_ready")
    k.t_ready = sem("t_ready")
    k.rot_done = sem("rot_done")
    k.q_copied = sem("q_copied")
    k.att_ready = sem("att_ready")
    k.v_tok = sem("v_tok")
    k.v_evac = sem("v_evac")
    k.scored = sem("scored")
    k.masked = sem("masked")
    k.p_ready = sem("p_ready")
    k.p_norm = sem("p_norm")
    k.p_tr = sem("p_tr")
    k.pt_ready = sem("pt_ready")
    k.pv_done = sem("pv_done")
    k.pv_evac = sem("pv_evac")
    k.wg_ready = sem("wg_ready")
    k.lora_mm = sem("lora_mm")
    k.lora_evac = sem("lora_evac")
    k.kk_sq = sem("kk_sq")
    k.kk_sum = sem("kk_sum")
    k.kk_root = sem("kk_root")
    k.c_ready = sem("c_ready")
    k.exp_ready = sem("exp_ready")
    k.arr_ready = sem("arr_ready")
    k.bon_in = sem("bon_in")
    k.bon_sum = sem("bon_sum")
    k.bd_pool = sem("bd_pool")
    k.bd_act = sem("bd_act")
    k.xbd_ready = sem("xbd_ready")
    k.round_act = sem("round_act")
    k.tok_act = sem("tok_act")
    k.max_ready = sem("max_ready")
    k.gram = sem("gram")
    k.gram_evac = sem("gram_evac")
    k.tok_mm = sem("tok_mm")
    k.tok_evac = sem("tok_evac")
    k.round_mm = sem("round_mm")
    k.round_evac = sem("round_evac")
    k.rt_copied = sem("rt_copied")
    k.u0_mm = sem("u0_mm")
    k.u0_evac = sem("u0_evac")
    k.wu_mm = sem("wu_mm")
    k.wu_evac = sem("wu_evac")
    k.mfn_mm = sem("mfn_mm")
    k.mfn_evac = sem("mfn_evac")
    k.chain_mm = sem("chain_mm")
    k.chain_evac = sem("chain_evac")
    k.y_mm = sem("y_mm")
    k.y_evac = sem("y_evac")
    k.gn_in = sem("gn_in")
    k.gn_sum = sem("gn_sum")
    k.gn_root = sem("gn_root")
    k.gn_sq = sem("gn_sq")
    k.dec_in = sem("dec_in")
    k.dec_exp = sem("dec_exp")
    k.dec_abs = sem("dec_abs")
    k.dec_mm = sem("dec_mm")
    k.gz_ready = sem("gz_ready")
    k.gexp_ready = sem("gexp_ready")
    k.gla_copy = sem("gla_copy")
    k.gla_tok = sem("gla_tok")
    k.gla_tok_evac = sem("gla_tok_evac")
    k.gla_att = sem("gla_att")
    k.gla_att_evac = sem("gla_att_evac")
    k.gla_state = sem("gla_state")
    k.gla_state_evac = sem("gla_state_evac")
    k.gla_o = sem("gla_o")
    k.gla_sq = sem("gla_sq")
    k.gla_mean = sem("gla_mean")
    k.gla_root = sem("gla_root")
    k.gla_y = sem("gla_y")
    k.wh_y = sem("wh_y")
    k.gyh_ready = sem("gyh_ready")
    k.y_ready = sem("y_ready")
    k.csil_ready = sem("csil_ready")
    k.settled = sem("settled")
    k.fox_copy = sem("fox_copy")
    k.fox_tok = sem("fox_tok")
    k.fox_tok_evac = sem("fox_tok_evac")
    k.fox_sc = sem("fox_sc")
    k.fox_masked = sem("fox_masked")
    k.fox_p = sem("fox_p")
    k.fox_norm = sem("fox_norm")
    k.fox_tr = sem("fox_tr")
    k.fox_pt = sem("fox_pt")
    k.fox_pv = sem("fox_pv")
    k.fox_y = sem("fox_y")


def stage_end(k, eng, n):
    eng.drain().then_inc(k.stage, 1)
    eng.wait_ge(k.stage, n * 4)
    settle(k, eng)


def settle(k, eng):
    eng.sem_inc(k.settled, 1)


def const(k, name, rows=slice(0, P)):
    at, n = CONST[name]
    return k.const[rows, at:at + n]


def vec(k, name, t=0, layer=None, n=1, rows=slice(0, P)):
    at = VEC[name][0]
    if layer is None:
        return k.vec[rows, bass.ds(at + t, n)]
    return k.vec[rows, bass.ds(layer * VEC_LAYER + (at + t), n)]



def load(k, sp, par, half, dram, size):
    sp.dma_start(k.land[:, par, 0:size * P], dram).then_inc(k.landed[par], 16)


def load_section(k, sp, start, count, dram, size, loop=0):
    def one(i, p, _):
        sp.wait_ge(k.lo_ready, p.count(1))
        load(k, sp, p.par, p.half, dram(i), size)
    section(sp, start, count, one, loop)


def load_ada(k, sp, first, count, par0, dram):
    def one(i, b):
        sp.wait_ge(k.ada_done, i + (first + 1))
        load(k, sp, (par0 + b) % 2, None, dram(i), ADA_K)
    with sp.Fori(0, count // 2) as i:
        for b in range(2):
            one(i * 2 + b, b)


ADA_K = 16


def flat(ap, i):
    return ap[bass.ds(i, 1), :, :].rearrange("a p n -> p (a n)")


def program_sync(k, sp, d):
    W = slice(META, TOK)
    sp.dma_start(k.vec[:, :], d["vec"]).then_inc(k.vec_loaded, 16)
    load_ada(k, sp, 0, ADA_FIRST, 0, lambda i: flat(d["w_ada"], i))
    sp.wait_ge(k.ada_done, ADA_FIRST + 2)
    load_section(k, sp, 0, IN1, lambda i: flat(d["w_in"], i), IN_K)
    sp.wait_ge(k.lo_ready, IN1 + 2)
    load_ada(k, sp, ADA_FIRST, ADA_LAST, IN1 % 2, lambda i: flat(d["w_ada"], i + ADA_FIRST))
    sp.wait_ge(k.ada_done, ADA_FIRST + ADA_LAST + 2)
    load_section(k, sp, M_AB1, AB, lambda i: flat(d["w_ab"], i), AB_K)
    load_section(k, sp, M_OUT1, OUT, lambda i: flat(d["w_out"], i), OUT_K)
    load_section(k, sp, M_GU1, GU, lambda i: flat(d["w_gu"], i), GU_K)
    load_section(k, sp, M_DOWN1, DOWN, lambda i: flat(d["w_down"], i), DOWN_K)
    with sp.Fori(0, LAYERS) as l:
        q = l * (L_PANELS // 2)

        def part(start, count, name, size, each=None, first=0):
            n = count if each is None else each
            load_section(k, sp, M_LAYER + start, count, lambda i: flat(d[name], l * n + i + first), size, q)
        part(L_GUA, GU, "w_gu1_2", GU_K)
        part(L_DOWNA, DOWN, "w_down1_2", DOWN_K)
        part(L_SINGLE, SINGLES, "w_in_single_2", AB_K)
        part(L_IN, IN2, "w_in_2", IN_K)
        part(L_AB, AB, "w_ab_2", AB_K)
        part(L_OUT, OUT, "w_out_2", OUT_K)
        part(L_GUB, GU, "w_gu2_2", GU_K)
        part(L_DOWNB, DOWN, "w_down2_2", DOWN_K)
    sp.wait_ge(k.x_ready, KT * (2 + 3 * LAYERS))
    sp.dma_start(d["out"], k.x[:, :, W]).then_inc(k.stored, 16)
    sp.wait_ge(k.stored, 16)



def split_hi(k, act, p, size):
    for par in (0, 1):
        if par == p.par:
            act.wait_ge(k.landed[par], p.landed())
    act.wait_ge(k.panel_done, p.count(1))
    k.nc.scalar.activation(k.w_hi[:, p.par, 0:size * P], k.land[:, p.par, 0:size * P],
                           ACT.Copy).then_inc(k.hi_ready, 1)


def split_lo(k, dve, p, size):
    dve.wait_ge(k.hi_ready, p.count(1))
    k.nc.vector.tensor_tensor(k.w_lo[:, p.par, 0:size * P], k.land[:, p.par, 0:size * P],
                              k.w_hi[:, p.par, 0:size * P].bitcast(F32), ALU.subtract).then_inc(k.lo_ready, 1)


def ahead(fn, k, eng, p, nxt, size):
    if nxt is not None:
        fn(k, eng, p.ahead2(), size if nxt == "same" else nxt)


def panel_begin(k, pe, p):
    pe.wait_ge(k.lo_ready, p.count(3))
    pe.wait_ge(k.acc_free, p.count(1))


def tile_mm(k, out, par, tile, hi, lo, start, stop):
    c = slice(tile * P, (tile + 1) * P)
    mm = k.nc.tensor.matmul
    mm(out, k.w_hi[:, par, c], hi, start=start, stop=False)
    mm(out, k.w_hi[:, par, c], lo, start=False, stop=False)
    return mm(out, k.w_lo[:, par, c], hi, start=False, stop=stop)


def pe_project(k, pe, start, count, tiles, W, loop=0, before=None):
    n = W.stop - W.start

    def one(i, p, _):
        panel_begin(k, pe, p)
        for o in range(tiles):
            for t in range(KT):
                last = tile_mm(k, k.acc[:, 2 * p.par + o, 0:n], p.par, o * KT + t, k.h_hi[:, t, W],
                               k.h_lo[:, t, W], t == 0, t == KT - 1)
        last.then_inc(k.panel_done, 1)
    section(pe, start, count, one, loop)


def pe_down(k, pe, start, W, loop=0):
    n = W.stop - W.start

    def one(i, p, _):
        panel_begin(k, pe, p)
        for t in range(FT):
            last = tile_mm(k, k.acc[:, 2 * p.par, 0:n], p.par, t, k.a_hi[:, t, W], k.a_lo[:, t, W],
                           t == 0, t == FT - 1)
        last.then_inc(k.panel_done, 1)
    section(pe, start, DOWN, one, loop)


def pe_branches(k, pe, start, n, y_hi, y_lo, first, loop=0):
    def one(i, p, _):
        panel_begin(k, pe, p)
        for t in range(KT):
            b = int(t >= first)
            last = tile_mm(k, k.acc[:, 2 * p.par + b, 0:n], p.par, t, y_hi[:, t, 0:n], y_lo[:, t, 0:n],
                           t in (0, first), t in (first - 1, KT - 1))
        last.then_inc(k.panel_done, 1)
    section(pe, start, AB, one, loop)



def pe_stat(k, pe, n, W):
    pe.wait_ge(k.sums_ready, n + 1)
    k.nc.tensor.matmul(k.mb[:, 3, 0:W.stop - W.start], k.mean_ones[:, :], k.ssum[:, W],
                       start=True, stop=True).then_inc(k.stat_done, 1)


def act_root(k, act, n, W):
    act.wait_ge(k.stat_done, n + 1)
    k.nc.scalar.activation(k.root[:, W], k.mb[:, 3, 0:W.stop - W.start], ACT.Sqrt,
                           bias=k.eps[:, 0:1]).then_inc(k.root_ready, 1)


def dve_rstd(k, dve, n, W):
    k.nc.vector.drain().then_inc(k.sums_ready, 1)
    dve.wait_ge(k.root_ready, n + 1)
    k.nc.vector.reciprocal(k.rstd[:, W], k.root[:, W])
    k.nc.vector.memset(k.ssum[:, :], 0.0)
    dve.drain()


def act_pre(k, act, i, W, shift=None, updates=None):
    for t in range(KT):
        if updates is not None:
            act.wait_ge(k.x_ready, updates * KT + (t + 1))
        act.wait_ge(k.sq_used, i * KT + (t + 1))
        k.nc.scalar.activation(k.sq[:, t % 2, W], k.x[:, t, W], ACT.Square).then_inc(k.sq_ready, 1)
    act_root(k, act, i * 2, W)
    for t in range(KT):
        act.wait_ge(k.n_ready, i * KT + (t + 1))
        if shift is None:
            r = k.nc.scalar.activation(k.h_hi[:, t, W], k.f[:, t, W], ACT.Copy)
        else:
            r = k.nc.scalar.activation(k.h_hi[:, t, W], k.f[:, t, W], ACT.Identity, bias=shift(t))
        r.then_inc(k.hh_ready, 1)


def dve_pre(k, dve, i, W, gain, shift=None):
    v = k.nc.vector
    for t in range(KT):
        dve.wait_ge(k.sq_ready, i * KT + (t + 1))
        v.tensor_tensor(k.ssum[:, W], k.ssum[:, W], k.sq[:, t % 2, W], ALU.add).then_inc(k.sq_used, 1)
        if t < KT - 1:
            dve.drain()
    dve_rstd(k, dve, i * 2, W)

    def normed(t):
        v.scalar_tensor_tensor(k.f[:, t, W], k.x[:, t, W], gain(t), k.rstd[:, W], ALU.mult,
                               ALU.mult).then_inc(k.n_ready, 1)
    normed(0)
    for t in range(KT):
        if t + 1 < KT:
            normed(t + 1)
        if t == KT - 1:
            dve.drain()
        dve.wait_ge(k.hh_ready, i * KT + (t + 1))
        hh = k.h_hi[:, t, W].bitcast(F32)
        if shift is None:
            r = v.tensor_tensor(k.h_lo[:, t, W], k.f[:, t, W], hh, ALU.subtract)
        else:
            r = v.scalar_tensor_tensor(k.h_lo[:, t, W], k.f[:, t, W], shift(t), hh, ALU.add, ALU.subtract)
        r.then_inc(k.hl_ready, 1)


def pe_pre(k, pe, i, W):
    pe_stat(k, pe, i * 2, W)
    pe.wait_ge(k.hl_ready, i * KT + KT)
    settle(k, pe)


def act_products(k, act, i, start, tiles, W, size, nxt, loop=0):
    n = W.stop - W.start

    def one(t, p, ahead_size):
        act.wait_ge(k.panel_done, p.count(3))
        for o in range(tiles):
            k.nc.scalar.activation(k.sq_post[:, 2 * p.par + o, W], k.acc[:, 2 * p.par + o, 0:n],
                                   ACT.Square).then_inc(k.sq_post_ready, 1)
        ahead(split_hi, k, act, p, ahead_size, size)
    section(act, start, KT // tiles, one, loop, nxt)


def dve_products(k, dve, i, start, tiles, W, size, nxt, loop=0):
    n = W.stop - W.start
    v = k.nc.vector

    def one(idx, p, ahead_size):
        dve.wait_ge(k.panel_done, p.count(3))
        for o in range(tiles):
            t = idx * tiles + o
            f = k.f[:, bass.ds(t, 1), W].rearrange("p a n -> p (a n)")
            dve.wait_ge(k.sq_post_ready, i * KT + (t + 1))
            v.tensor_copy(f, k.acc[:, 2 * p.par + o, 0:n])
            r = v.tensor_tensor(k.ssum[:, W], k.ssum[:, W], k.sq_post[:, 2 * p.par + o, W], ALU.add)
            if o == tiles - 1:
                r.then_inc(k.acc_free, 1)
            dve.drain()
        ahead(split_lo, k, dve, p, ahead_size, size)
    section(dve, start, KT // tiles, one, loop, nxt)


def dve_post(k, dve, i, W, gain):
    v = k.nc.vector
    dve_rstd(k, dve, i * 2 + 1, W)

    def update(t):
        v.scalar_tensor_tensor(k.sq_post[:, t % 3, W], k.f[:, t, W], gain(t), k.rstd[:, W], ALU.mult, ALU.mult)
    update(0)
    for t in range(KT):
        if t + 1 < KT:
            update(t + 1)
        dve.drain()
        v.tensor_tensor(k.x[:, t, W], k.x[:, t, W], k.sq_post[:, t % 3, W], ALU.add).then_inc(k.x_ready, 1)



def act_gate_up(k, act, i, start, W, nxt, loop=0):
    n = W.stop - W.start

    def one(t, p, ahead_size):
        act.wait_ge(k.panel_done, p.count(3))
        k.nc.scalar.activation(k.sig[:, p.par, W], k.acc[:, 2 * p.par, 0:n], ACT.Sigmoid).then_inc(k.sig_ready, 1)
        ahead(split_hi, k, act, p, ahead_size, GU_K)
        act.wait_ge(k.acc_free, p.count(3))
        k.nc.scalar.activation(k.a_hi[:, bass.ds(t, 1), W].rearrange("p a n -> p (a n)"), k.a_ff[:, p.par, W],
                               ACT.Copy).then_inc(k.ah_ready, 1)
    section(act, start, GU, one, loop, nxt)


def dve_gate_up(k, dve, i, start, W, nxt, loop=0):
    n = W.stop - W.start
    v = k.nc.vector

    def one(t, p, ahead_size):
        dve.wait_ge(k.sig_ready, i * FT + (t + 1))
        v.tensor_tensor(k.t_ff[:, p.par, W], k.sig[:, p.par, W], k.acc[:, 2 * p.par, 0:n], ALU.mult)
        dve.drain()
        v.tensor_tensor(k.a_ff[:, p.par, W], k.t_ff[:, p.par, W], k.acc[:, 2 * p.par + 1, 0:n],
                        ALU.mult).then_inc(k.acc_free, 1)
        ahead(split_lo, k, dve, p, ahead_size, GU_K)
        dve.drain()
        dve.wait_ge(k.ah_ready, i * FT + (t + 1))
        a = bass.ds(t, 1)
        v.tensor_tensor(k.a_lo[:, a, W].rearrange("p a n -> p (a n)"), k.a_ff[:, p.par, W],
                        k.a_hi[:, a, W].rearrange("p a n -> p (a n)").bitcast(F32),
                        ALU.subtract).then_inc(k.al_ready, 1)
    section(dve, start, GU, one, loop, nxt)


def act_ffn(k, act, i, gu, down, post, W, nxt, loop=0):
    act_gate_up(k, act, i, gu, W, (DOWN_K, DOWN_K), loop)
    act_products(k, act, post, down, 1, W, DOWN_K, nxt, loop)
    act_root(k, act, post * 2 + 1, W)


def dve_ffn(k, dve, i, gu, down, post, W, gain, nxt, loop=0):
    dve_gate_up(k, dve, i, gu, W, (DOWN_K, DOWN_K), loop)
    dve_products(k, dve, post, down, 1, W, DOWN_K, nxt, loop)
    dve_post(k, dve, post, W, gain)


def pe_ffn(k, pe, i, gu, down, post, W, loop=0):
    pe_project(k, pe, gu, GU, 2, W, loop)
    pe.wait_ge(k.al_ready, i * FT + FT)
    settle(k, pe)
    pe_down(k, pe, down, W, loop)
    pe_stat(k, pe, post * 2 + 1, W)



def act_ahead_only(k, act, start, count, size, nxt, loop=0):
    section(act, start, count, lambda t, p, s: ahead(split_hi, k, act, p, s, size), loop, nxt)


def dve_copy_out(k, dve, start, count, tiles, dst, n, size, nxt, loop=0, signal=None):
    def one(i, p, ahead_size):
        dve.wait_ge(k.panel_done, p.count(3))
        k.nc.vector.tensor_copy(dst(i), k.acc[:, 2 * p.par:2 * p.par + tiles, 0:n]).then_inc(k.acc_free, 1)
        if signal is not None:
            k.nc.vector.drain().then_inc(signal, 1)
        ahead(split_lo, k, dve, p, ahead_size, size)
    section(dve, start, count, one, loop, nxt)



def dve_merge(k, dve, i, start, n, ga, gb, W, nxt, loop=0):
    v = k.nc.vector

    def one(t, p, ahead_size):
        dve.wait_ge(k.panel_done, p.count(3))
        v.tensor_tensor(k.upd[:, 0, 0:n], ga(t), k.acc[:, 2 * p.par, 0:n], ALU.mult)
        v.tensor_tensor(k.upd[:, 1, 0:n], gb(t), k.acc[:, 2 * p.par + 1, 0:n], ALU.mult).then_inc(k.acc_free, 1)
        dve.drain()
        v.tensor_tensor(k.sq_post[:, p.par, 0:n], k.upd[:, 0, 0:n], k.upd[:, 1, 0:n],
                        ALU.add).then_inc(k.merged, 1)
        ahead(split_lo, k, dve, p, ahead_size, AB_K)
        dve.drain()
        dve.wait_ge(k.yh_ready, i * KT + (t + 1))
        a = bass.ds(t, 1)
        v.tensor_tensor(k.h_lo[:, a, W].rearrange("p a n -> p (a n)"), k.sq_post[:, p.par, 0:n],
                        k.h_hi[:, a, W].rearrange("p a n -> p (a n)").bitcast(F32),
                        ALU.subtract).then_inc(k.yl_ready, 1)
    section(dve, start, AB, one, loop, nxt)


def act_merge(k, act, i, start, n, W, nxt, loop=0):
    def one(t, p, ahead_size):
        ahead(split_hi, k, act, p, ahead_size, AB_K)
        act.wait_ge(k.merged, i * KT + (t + 1))
        k.nc.scalar.activation(k.h_hi[:, bass.ds(t, 1), W].rearrange("p a n -> p (a n)"),
                               k.sq_post[:, p.par, 0:n], ACT.Copy).then_inc(k.yh_ready, 1)
    section(act, start, AB, one, loop, nxt)


def tile(a, i, cols=slice(None), rows=slice(0, P)):
    return a[rows, bass.ds(i, 1), cols].rearrange("p a n -> p (a n)")


def over(a, n, axis=1):
    return a.unsqueeze(axis).broadcast_to([a.shape[0], n, a.shape[1]])


HALVES = (slice(0, HD), slice(HD, P))



UNITS = [(qb, h) for qb in range(2) for h in range(2)]


def pool_att(k, pool):
    k.nc.gpsimd.memset(k.kz[:, :, :, :], 0.0)
    k.nc.gpsimd.memset(k.vz[:, :, :, :, :], 0.0).then_inc(k.gates_ready, 1)


def pe_att(k, pe):
    nc = k.nc
    ident = const(k, "ident")
    with pe.Fori(0, 2) as hp:
        pe.wait_ge(k.pv_evac, hp + 1)
        for g in range(3):
            for b in range(2):
                last = nc.tensor.matmul(k.mb[:, g, b * SEQ:(b + 1) * SEQ], const(k, "rot"),
                                        tile(k.qkv, hp + (b * 6 + 2 * g)), start=True, stop=True)
        last.then_inc(k.rot_done, 1)
        pe.wait_ge(k.q_copied, hp + 1)
        for g in range(2):
            for b in range(2):
                last = nc.tensor.transpose(k.mb[:, 3, (2 * g + b) * P:(2 * g + b + 1) * P],
                                           k.vs[:, g, b * P:(b + 1) * P], ident)
        last.then_inc(k.v_tok, 1)
        pe.wait_ge(k.att_ready, hp + 1)
        for b in range(2):
            last = nc.tensor.transpose(k.mb[:, 0, b * P:(b + 1) * P], k.vs[:, 2, b * P:(b + 1) * P], ident)
        last.then_inc(k.v_tok, 1)
        for u, (qb, h) in enumerate(UNITS):
            n = (qb + 1) * P
            pe.wait_ge(k.masked, hp * 4 + (u + 1))
            for g in range(3):
                last = nc.tensor.matmul(k.mb[:, 1 + g // 2, (g % 2) * SEQ:(g % 2) * SEQ + n],
                                        k.qs[:, g, qb * P:(qb + 1) * P], k.kz[:, g, h, 0:n], start=True, stop=True)
            last.then_inc(k.scored, 1)
            pe.wait_ge(k.v_evac, hp * 2 + 2)
            pe.wait_ge(k.p_norm, hp * 4 + (u + 1))
            nb = 3 * (qb + 1)
            for i in range(nb):
                g, b = divmod(i, qb + 1)
                out = k.mb[:, 0, i * P:(i + 1) * P] if i < 4 else k.mb[:, 3, (i - 4) * P:(i - 3) * P]
                last = nc.tensor.transpose(out, k.p_att[:, g, b * P:(b + 1) * P], ident)
            last.then_inc(k.p_tr, 1)
            pe.wait_ge(k.pt_ready, hp * 4 + (u + 1))
            for i in range(nb):
                g, b = divmod(i, qb + 1)
                last = nc.tensor.matmul(k.acc[:, 0, qb * P:(qb + 1) * P], k.vz[:, g, b, h, :], k.pt_att[:, i, :],
                                        start=(h == 0 and i == 0), stop=(h == 1 and i == nb - 1))
            last.then_inc(k.pv_done, 1)


def act_att(k, act):
    nc = k.nc
    with act.Fori(0, 2) as hp:
        act.wait_ge(k.pv_evac, hp + 1)
        for g in range(3):
            last = nc.scalar.activation(k.vs[:, g, :], tile(k.qkv, hp + (12 + 2 * g)), ACT.Copy)
        last.then_inc(k.q_copied, 1)
        act.wait_ge(k.gates_ready, 1)
        act.wait_ge(k.v_tok, hp * 2 + 1)
        for h in range(2):
            src = k.mb[:, 3, :].rearrange("p (g b c) -> p (g b) c", g=2, b=2)[:, :, HALVES[h]]
            last = nc.scalar.activation(k.vz[:, 0:2, :, h, HALVES[h]].rearrange("p g b c -> p (g b) c"), src, ACT.Copy)
        last.then_inc(k.v_evac, 1)
        act.wait_ge(k.v_tok, hp * 2 + 2)
        for h in range(2):
            src = k.mb[:, 0, 0:2 * P].rearrange("p (b c) -> p b c", b=2)[:, :, HALVES[h]]
            last = nc.scalar.activation(k.vz[:, 2, :, h, HALVES[h]], src, ACT.Copy)
        last.then_inc(k.v_evac, 1)
        for u, (qb, h) in enumerate(UNITS):
            n = (qb + 1) * P
            act.wait_ge(k.max_ready, hp * 4 + (u + 1))
            act.wait_ge(k.p_tr, hp * 4 + (u + 1))
            nc.scalar.activation(k.p_att[:, :, 0:n], k.s_att[:, :, 0:n], ACT.Exp, bias=k.st_att[:, 0:1],
                                 accum_out=k.st_att[:, 1:2]).then_inc(k.p_ready, 1)
            act.wait_ge(k.p_tr, hp * 4 + (u + 2))
            act.wait_ge(k.pv_done, hp * 4 + (u + 1))
            nb = 3 * (qb + 1)
            last = nc.scalar.activation(k.pt_att[:, 0:min(nb, 4), :],
                                        k.mb[:, 0, 0:min(nb, 4) * P].rearrange("p (i c) -> p i c", c=P), ACT.Copy)
            if nb > 4:
                last = nc.scalar.activation(k.pt_att[:, 4:nb, :],
                                            k.mb[:, 3, 0:(nb - 4) * P].rearrange("p (i c) -> p i c", c=P), ACT.Copy)
            last.then_inc(k.pt_ready, 1)


def dve_att(k, dve):
    v = k.nc.vector
    mask = const(k, "mask_att").rearrange("p (g n) -> p g n", g=3)
    dve.wait_ge(k.gates_ready, 1)
    with dve.Fori(0, 2) as hp:
        dve.drain()
        dve.wait_ge(k.rot_done, hp + 1)
        for g in range(3):
            for b in range(2):
                if g or b:
                    dve.drain()
                v.tensor_tensor(k.rt1[:, :], tile(k.qkv, hp + (b * 6 + 2 * g)), const(k, "cos"), ALU.mult)
                v.tensor_tensor(k.rt2[:, :], k.mb[:, g, b * SEQ:(b + 1) * SEQ], const(k, "sin"), ALU.mult)
                dve.drain()
                if b == 0:
                    last = v.tensor_tensor(k.qs[:, g, :], k.rt1[:, :], k.rt2[:, :], ALU.add)
                else:
                    for h, rows in enumerate(HALVES):
                        last = v.tensor_tensor(k.kz[rows, g, h, :], k.rt1[rows, :], k.rt2[rows, :], ALU.add)
        last.then_inc(k.att_ready, 1)
        for u, (qb, h) in enumerate(UNITS):
            n = (qb + 1) * P
            cols = slice((1 - qb) * P, 2 * P)
            dve.wait_ge(k.scored, hp * 4 + (u + 1))
            v.scalar_tensor_tensor(k.s_att[:, 0:2, 0:n], k.mb[:, 1, :].rearrange("p (g n) -> p g n", g=2)[:, :, 0:n],
                                   HD ** -0.5, mask[:, 0:2, cols], ALU.mult, ALU.add)
            v.scalar_tensor_tensor(k.s_att[:, 2, 0:n], k.mb[:, 2, 0:n], HD ** -0.5, mask[:, 2, cols],
                                   ALU.mult, ALU.add).then_inc(k.masked, 1)
            dve.drain()
            v.tensor_reduce(k.st_att[:, 0:1], k.s_att[:, :, 0:n], mybir.AxisListType.XY, ALU.max,
                            negate=True).then_inc(k.max_ready, 1)
            dve.wait_ge(k.p_ready, hp * 4 + (u + 1))
            v.reciprocal(k.st_att[:, 2:3], k.st_att[:, 1:2])
            dve.drain()
            v.tensor_scalar(k.p_att[:, :, 0:n], k.p_att[:, :, 0:n], k.st_att[:, 2:3], None,
                            ALU.mult).then_inc(k.p_norm, 1)
        dve.wait_ge(k.pv_done, hp * 4 + 5)
        v.tensor_copy(tile(k.yb_keep, hp), k.acc[:, 0, 0:SEQ]).then_inc(k.pv_evac, 1)



def pool_shift(k, pool):
    g = k.nc.gpsimd
    with pool.Fori(0, SHIFT_TILES // 2) as i:
        pool.wait_ge(k.pin_ready, i + 1)
        two = bass.ds(i * 2, 2)
        g.tensor_tensor(k.kap[:, 0:2, :], k.p_in[:, two, 0:SEQ], k.p_in[:, two, 1:SEQ + 1], ALU.subtract)
        pool.drain()
        mu = k.vec[:, bass.ds(i * 2 + VEC["mu"][0], 2)].unsqueeze(2).broadcast_to([P, 2, SEQ])
        g.tensor_tensor(k.kap[:, 0:2, :], k.kap[:, 0:2, :], mu, ALU.mult)
        pool.drain()
        g.tensor_tensor(k.p_in[:, two, 1:SEQ + 1], k.p_in[:, two, 1:SEQ + 1], k.kap[:, 0:2, :], ALU.add)
        pool.drain()


def pool_rwkv(k, pool, d):
    g = k.nc.gpsimd
    g.dma_start(k.w2p[:, :], d["w2"]).then_inc(k.lora_loaded, 16)
    g.dma_start(k.a2p[:, :], d["a2"]).then_inc(k.lora_loaded, 16)
    g.dma_start(k.g2[:, :], d["g2"]).then_inc(k.lora_loaded, 16)
    g.memset(k.reset[:, :], 1.0)
    pool.drain()
    g.memset(k.reset[:, 0:SEQ:CHUNK], 0.0).then_inc(k.t_ready, 1)


def pe_pair_sums(k, pe, ready, src, done):
    pe.wait_ge(ready, 1)
    s = src[:, :, :].rearrange("p t n -> p (t n)")
    for b in range(3):
        last = k.nc.tensor.matmul(k.mb[:, b, :], const(k, "pair_ones"), s[:, b * 512:(b + 1) * 512],
                                  start=True, stop=True)
    last.then_inc(done, 1)


def pe_rwkv_prep(k, pe):
    mm = k.nc.tensor.matmul
    x = slice(1, SEQ + 1)
    pe.wait_ge(k.lora_loaded, 48)
    pe.wait_ge(k.wg_ready, 1)
    for c in range(RT):
        b, cols = 2 * (c % 2), slice(c * P, (c + 1) * P)
        if c >= 2:
            pe.wait_ge(k.lora_evac, c - 1)
        mm(k.mb[:, b, 0:SEQ], k.w2p[:, cols], k.p_in[:, T_WA, x], start=True, stop=True)
        mm(k.mb[:, b, SEQ:2 * SEQ], k.a2p[:, cols], k.p_in[:, T_WA, x], start=True, stop=True)
        mm(k.mb[:, b + 1, 0:SEQ], k.g2[:, cols], k.p_in[:, T_G, x], start=True, stop=True).then_inc(k.lora_mm, 1)
    pe.wait_ge(k.lora_evac, RT)
    pe_pair_sums(k, pe, k.kk_sq, k.tmp, k.kk_sum)
    pe.wait_ge(k.kk_root, 1)
    pe_pair_sums(k, pe, k.bon_in, k.c1, k.bon_sum)


def act_rwkv_prep(k, act):
    a = k.nc.scalar.activation
    x = slice(1, SEQ + 1)
    a(k.p_in[0:HD, T_WA, x], k.p_in[0:HD, T_WA, x], ACT.Tanh)
    a(k.p_in[:, T_G, x], k.p_in[:, T_G, x], ACT.Sigmoid).then_inc(k.wg_ready, 1)
    for c in range(RT):
        b = 2 * (c % 2)
        act.wait_ge(k.lora_mm, c + 1)
        a(k.sw[:, c, :], k.mb[:, b, 0:SEQ], ACT.Sigmoid, bias=vec(k, "w0", c))
        a(k.beta[:, c, :], k.mb[:, b, SEQ:2 * SEQ], ACT.Sigmoid, bias=vec(k, "a0", c))
        a(k.gate[:, c, :], k.mb[:, b + 1, 0:SEQ], ACT.Copy).then_inc(k.lora_evac, 1)
    act.wait_ge(k.kk_sum, 1)
    a(k.tmp[:, :, :].rearrange("p t n -> p (t n)").rearrange("p (b n) -> p b n", b=3), k.mb[:, 0:3, :],
      ACT.Sqrt).then_inc(k.kk_root, 1)
    act.wait_ge(k.c_ready, 1)
    a(k.sw[:, :, :], k.sw[:, :, :], ACT.Exp, scale=-DECAY)
    a(k.bon[:, :, :], k.c1[:, :, :], ACT.Exp, scale=DECAY)
    a(k.tmp[:, :, :], k.c1[:, :, :], ACT.Exp, scale=-DECAY).then_inc(k.exp_ready, 1)


def dve_rwkv_prep(k, dve):
    v = k.nc.vector
    x = slice(1, SEQ + 1)
    tt = v.tensor_tensor
    pk, pr, pv = (k.p_in[:, t:t + RT, x] for t in (T_K, T_R, T_V))
    kk, tmp, kap, a, c1, sw = (b[:, :, :] for b in (k.kk, k.tmp, k.kap, k.beta, k.c1, k.sw))
    for t in range(RT):
        v.tensor_scalar(k.kk[:, t, :], k.p_in[:, T_K + t, x], vec(k, "k_k", t), None, ALU.mult)
    dve.drain()
    tt(tmp, kk, kk, ALU.mult).then_inc(k.kk_sq, 1)
    dve.wait_ge(k.lora_evac, RT)
    dve.wait_ge(k.t_ready, 1)
    for t in range(RT):
        v.tensor_tensor_scan(k.c1[:, t, :], k.reset[:, :], k.sw[:, t, :], 0.0, ALU.mult, ALU.add)
    for t in range(RT):
        v.tensor_scalar(k.kap[:, t, :], k.beta[:, t, :], -1.0, vec(k, "k_a", t), ALU.add, ALU.mult)
    dve.drain()
    tt(sw, c1, sw, ALU.subtract)
    for t in range(RT):
        v.scalar_tensor_tensor(k.kap[:, t, :], k.kap[:, t, :], 1.0, k.p_in[:, T_K + t, x], ALU.add, ALU.mult)
    tt(a, a, kk, ALU.mult)
    dve.wait_ge(k.kk_root, 1)
    v.tensor_scalar_max(tmp, tmp, 1e-12)
    dve.drain()
    v.reciprocal(tmp, tmp)
    dve.drain()
    tt(kk, kk, tmp, ALU.mult)
    tt(a, a, tmp, ALU.mult)
    dve.drain().then_inc(k.c_ready, 1)
    dve.wait_ge(k.exp_ready, 1)
    v.tensor_copy(k.pc[:, :, :], k.tmp[:, :, CHUNK - 1:SEQ:CHUNK])
    tt(c1, pr, kap, ALU.mult)
    tt(pk, kk, sw, ALU.mult)
    tt(a, a, k.bon[:, :, :], ALU.mult)
    dve.drain()
    for t in range(RT):
        last = v.tensor_scalar(k.c1[:, t, :], k.c1[:, t, :], vec(k, "r_k", t), None, ALU.mult)
    last.then_inc(k.bon_in, 1)
    tt(kap, kap, k.bon[:, :, :], ALU.mult)
    tt(pr, pr, tmp, ALU.mult)
    dve.drain()
    dve.wait_ge(k.bon_sum, 1)
    for b in range(3):
        tt(k.bon[:, 2 * b:2 * b + 2, :], k.p_in[:, T_V + 2 * b:T_V + 2 * b + 2, x],
           k.mb[:, b, :].rearrange("p (t n) -> p t n", t=2), ALU.mult)
    dve.drain()


def pool_rwkv_zero(k, pool):
    for name in ("al_bd", "be_bd", "ka_bd", "v_bd", "x_bd", "xt_bd", "rt_bd", "akt_bd", "w_bd", "u_bd", "m_bd"):
        k.nc.gpsimd.memset(k.m[name][:, :, :], 0.0)
    k.nc.gpsimd.memset(k.m["s_bd"][:, :, :], 0.0).then_inc(k.arr_ready, 1)
    pool.drain()


def chunks(a):
    return a.rearrange("p (c t) -> p c t", c=NCH)


def pool_rwkv_pairs(k, pool):
    with pool.Fori(0, RT) as j:
        pool.wait_ge(k.y_evac, j + 1)
        for h, rows in enumerate(HALVES):
            k.nc.gpsimd.tensor_copy(k.m["al_bd"][rows, :, HALVES[h]],
                                    chunks(tile(k.p_in, j + T_K, slice(1, SEQ + 1), rows)))
            last = k.nc.gpsimd.tensor_copy(k.m["be_bd"][rows, :, HALVES[h]], chunks(tile(k.beta, j, rows=rows)))
        last.then_inc(k.bd_pool, 1)


ROUNDS = 6


def pe_rwkv_pairs(k, pe):
    nc, m = k.nc, k.m
    mm = nc.tensor.matmul
    ident = const(k, "ident")
    half = CHUNK
    with pe.Fori(0, RT) as j:
        def c_(c, n=P):
            return slice(c * n, (c + 1) * n)
        pe.wait_ge(k.bd_pool, j + 1)
        pe.wait_ge(k.bd_act, j + 1)
        for c in range(NCH):
            both = k.p_in[:, bass.ds(j, 2, 6), 1 + c * half:1 + (c + 1) * half]
            mm(k.mb[:, 0, c_(c)], m["be_bd"][:, c, :], both, start=True, stop=True)
            mm(k.mb[:, 1, c_(c)], m["ka_bd"][:, c, :], both, start=True, stop=True)
            last = mm(k.mb[:, 2, c_(c, half)], m["al_bd"][:, c, :], tile(k.beta, j, c_(c, half)),
                      start=True, stop=True)
        last.then_inc(k.gram, 1)
        for i, name in enumerate(("al_bd", "be_bd", "ka_bd", "v_bd")):
            if i == 1:
                pe.wait_ge(k.gram_evac, j + 1)
            for c in range(NCH):
                last = nc.tensor.transpose(k.mb[:, (3, 0, 1, 2)[i], c_(c)], m[name][:, c, :], ident)
            last.then_inc(k.tok_mm, 1)
        pe.wait_ge(k.tok_evac, j + 1)
        pe.wait_ge(k.tok_act, j + 1)
        for c in range(NCH):
            last = mm(k.mb[:, 3, c_(c, half)], m["akt_bd"][:, c, :], m["vt_st"][:, c, :], start=True, stop=True)
        last.then_inc(k.u0_mm, 1)
        for r in range(ROUNDS):
            if r == 0:
                pe.wait_ge(k.xbd_ready, j + 1)
            else:
                pe.wait_ge(k.round_act, j * 5 + r)
                pe.wait_ge(k.round_evac, j * ROUNDS + r)
            for c in range(NCH):
                if r < ROUNDS - 1:
                    mm(k.mb[:, 0, c_(c, half)], m["xt_bd"][:, c, :], m["x_st"][:, c, :], start=True, stop=True)
                lo = half if r == ROUNDS - 1 else 0
                hi = half if r == 0 else P
                last = mm(k.mb[:, 1, c * P + lo:c * P + hi], m["x_bd"][:, c, :], m["xr"][:, c, lo:hi],
                          start=True, stop=True)
            last.then_inc(k.round_mm, 1)
        pe.wait_ge(k.round_evac, j * ROUNDS + ROUNDS)
        pe.wait_ge(k.u0_evac, j + 1)
        for c in range(NCH):
            mm(k.mb[:, 2, c_(c, half)], m["rt_bd"][:, c, :], m["au"][:, c, 0:half], start=True, stop=True)
            last = mm(k.mb[:, 3, c_(c, half)], m["rt_bd"][:, c, :], m["au"][:, c, half:P], start=True, stop=True)
        last.then_inc(k.wu_mm, 1)
        pe.wait_ge(k.wu_evac, j + 1)
        pe.wait_ge(k.rt_copied, j + 1)
        for c in range(NCH):
            mm(k.mb[:, 1, c_(c, half)], m["w_bd"][:, c, :], m["qbt"][:, c, :], start=True, stop=True)
            if c < NCH - 1:
                mm(k.mb[:, 0, c_(c, half)], m["w_bd"][:, c, :], m["bet_st"][:, c, :], start=True, stop=True)
                mm(k.mb[:, 2, c_(c, half)], m["kat_bd"][:, c, :], m["vt_st"][:, c, :], start=True, stop=False)
                last = mm(k.mb[:, 2, c_(c, half)], m["bet_bd"][:, c, :], m["u_st"][:, c, :], start=False, stop=True)
            else:
                last = None
        nc.tensor.drain().then_inc(k.mfn_mm, 1)
        pe.wait_ge(k.mfn_evac, j + 1)
        pe.wait_ge(k.chain_evac, j * 3 + 1)
        mm(k.mb[:, 3, 0:half], m["m_bd"][:, 1, :], m["n_st"][:, 0, :], start=True, stop=True).then_inc(k.chain_mm, 1)
        pe.wait_ge(k.chain_evac, j * 3 + 2)
        mm(k.mb[:, 3, 0:half], m["m_bd"][:, 2, :], m["s_st"][:, :], start=True, stop=True).then_inc(k.chain_mm, 1)
        pe.wait_ge(k.chain_evac, j * 3 + 3)
        for c in range(NCH):
            out = k.mb[:, 0, c_(c, half)]
            mm(out, m["u_bd"][:, c, :], m["qbt"][:, c, :], start=True, stop=False)
            last = mm(out, m["vt_bd"][:, c, :], m["qkt"][:, c, :], start=False, stop=c == 0)
            if c > 0:
                last = mm(out, m["s_bd"][:, c - 1, :], m["f_st"][:, c, :], start=False, stop=True)
        last.then_inc(k.y_mm, 1)


def act_rwkv_pairs(k, act):
    m = k.m
    a = k.nc.scalar.activation
    half = CHUNK
    act.wait_ge(k.arr_ready, 1)
    with act.Fori(0, RT) as j:
        act.wait_ge(k.y_evac, j + 1)
        for h, rows in enumerate(HALVES):
            a(m["ka_bd"][rows, :, HALVES[h]], chunks(tile(k.kap, j, rows=rows)), ACT.Copy)
            last = a(m["v_bd"][rows, :, HALVES[h]], chunks(tile(k.p_in, j + T_V, slice(1, SEQ + 1), rows)), ACT.Copy)
        last.then_inc(k.bd_act, 1)

        def blocks(bank, n):
            return k.mb[:, bank, 0:NCH * n].rearrange("p (c n) -> p c n", c=NCH)

        def bd(name, src, off=0, scale=1.0):
            for h, rows in enumerate(HALVES):
                r = a(m[name][rows, :, HALVES[h]], src[rows, :, off:off + half], ACT.Copy, scale=scale)
            return r

        def st(dst, src, scale=1.0):
            for h, rows in enumerate(HALVES):
                r = a(dst[rows], src[rows, :, HALVES[h]], ACT.Copy, scale=scale)
            return r
        act.wait_ge(k.tok_mm, j * 4 + 1)
        st(m["au"][:, :, 0:half], blocks(3, P), scale=-1.0)
        act.wait_ge(k.gram_evac, j + 1)
        bd("x_bd", m["x_st"])
        bd("xt_bd", m["xr"]).then_inc(k.xbd_ready, 1)
        act.wait_ge(k.tok_mm, j * 4 + 2)
        a(m["bet_bd"][:, :, :], blocks(0, P), ACT.Copy)
        st(m["bet_st"][:, :, :], blocks(0, P)).then_inc(k.tok_act, 1)
        for r in range(ROUNDS - 1):
            act.wait_ge(k.round_mm, j * ROUNDS + (r + 1))
            if r < ROUNDS - 2:
                a(m["x_st"][:, :, :], blocks(0, half), ACT.Copy)
            bd("x_bd", blocks(0, half)).then_inc(k.round_act, 1)
        act.wait_ge(k.wu_mm, j + 1)
        bd("w_bd", blocks(2, half)).then_inc(k.wu_evac, 1)
        act.wait_ge(k.mfn_mm, j + 1)
        for c in range(NCH - 1):
            last = a(m["n_st"][:, c, :], k.mb[:, 2, c * half:(c + 1) * half], ACT.Copy,
                     scale=k.pc[:, bass.ds(j, 1), c:c + 1].rearrange("p a n -> p (a n)"))
        last.then_inc(k.mfn_evac, 1)


def dve_rwkv_pairs(k, dve):
    m, v = k.m, k.nc.vector
    half = CHUNK
    ui, us, ls, i2 = (const(k, n) for n in ("up_incl", "up_strict", "lo_strict", "i2"))
    stt, tt = v.scalar_tensor_tensor, v.tensor_tensor
    dve.wait_ge(k.arr_ready, 1)
    with dve.Fori(0, RT) as j:
        def blocks(bank, n):
            return k.mb[:, bank, 0:NCH * n].rearrange("p (c n) -> p c n", c=NCH)

        def st(dst, src):
            for h, rows in enumerate(HALVES):
                r = v.tensor_copy(dst[rows], src[rows, :, HALVES[h]])
            return r
        dve.wait_ge(k.gram, j + 1)
        tt(m["qbt"][:, :, :], blocks(0, P)[:, :, 0:half], over(ui, NCH), ALU.mult)
        stt(m["xr"][:, :, 0:half], blocks(0, P)[:, :, half:P], -1.0, over(us, NCH), ALU.mult, ALU.mult)
        tt(m["qkt"][:, :, :], blocks(1, P)[:, :, 0:half], over(ui, NCH), ALU.mult)
        for h, rows in enumerate(HALVES):
            tt(m["akt_bd"][rows, :, HALVES[h]], blocks(1, P)[rows, :, half:P], over(us[rows], NCH), ALU.mult)
        stt(m["x_st"][:, :, :], blocks(2, half), -1.0, over(ls, NCH), ALU.mult, ALU.mult).then_inc(k.gram_evac, 1)
        dve.drain()
        tt(m["xr"][:, :, half:P], m["xr"][:, :, 0:half], over(i2, NCH), ALU.add)
        dve.wait_ge(k.tok_mm, j * 4 + 4)
        v.tensor_copy(m["kat_bd"][:, :, :], blocks(1, P))
        v.tensor_copy(m["vt_bd"][:, :, :], blocks(2, P))
        st(m["vt_st"][:, :, :], blocks(2, P)).then_inc(k.tok_evac, 1)
        dve.wait_ge(k.u0_mm, j + 1)
        v.tensor_scalar(m["au"][:, :, half:P], blocks(3, half), -1.0, None, ALU.mult).then_inc(k.u0_evac, 1)
        for r in range(ROUNDS):
            dve.wait_ge(k.round_mm, j * ROUNDS + (r + 1))
            src = blocks(1, P)
            if r < ROUNDS - 1:
                if r < ROUNDS - 2:
                    v.tensor_copy(m["xr"][:, :, 0:half], src[:, :, 0:half])
                    for h, rows in enumerate(HALVES):
                        last = v.tensor_copy(m["xt_bd"][rows, :, HALVES[h]], src[rows, :, 0:half])
                if r > 0:
                    last = tt(m["xr"][:, :, half:P], m["xr"][:, :, half:P], src[:, :, half:P], ALU.add)
            else:
                for h, rows in enumerate(HALVES):
                    last = tt(m["rt_bd"][rows, :, HALVES[h]], m["xr"][rows, :, half:P], src[rows, :, half:P], ALU.add)
            last.then_inc(k.round_evac, 1)
            dve.drain()
        dve.wait_ge(k.wu_mm, j + 1)
        v.tensor_copy(m["u_st"][:, :, :], blocks(3, half))
        for h, rows in enumerate(HALVES):
            last = v.tensor_copy(m["u_bd"][rows, :, HALVES[h]], blocks(3, half)[rows])
        last.then_inc(k.rt_copied, 1)
        dve.wait_ge(k.mfn_mm, j + 1)
        for h, rows in enumerate(HALVES):
            tt(m["m_bd"][rows, 0:NCH - 1, HALVES[h]], blocks(0, half)[rows, 0:NCH - 1], over(i2[rows], NCH - 1), ALU.add)
        tt(m["f_st"][:, :, :], blocks(1, half), chunks(tile(k.p_in, j + T_R, slice(1, SEQ + 1))),
           ALU.add).then_inc(k.chain_evac, 1)
        dve.wait_ge(k.mfn_evac, j + 1)

        def state(c, src):
            for h, rows in enumerate(HALVES):
                r = v.tensor_copy(m["s_bd"][rows, c, HALVES[h]], src[rows])
            return r
        state(0, m["n_st"][:, 0, :])
        for c in (1, 2):
            dve.wait_ge(k.chain_mm, j * 2 + c)
            stt(m["s_st"][:, :], k.mb[:, 3, 0:half], k.pc[:, bass.ds(j, 1), c:c + 1].rearrange("p a n -> p (a n)"),
                m["n_st"][:, c, :], ALU.mult, ALU.add)
            dve.drain()
            state(c, m["s_st"][:, :]).then_inc(k.chain_evac, 1)
        dve.wait_ge(k.y_mm, j + 1)
        v.tensor_copy(tile(k.c1, j), k.mb[:, 0, 0:SEQ]).then_inc(k.y_evac, 1)


def pe_rwkv_out(k, pe):
    pe_pair_sums(k, pe, k.gn_in, k.c1, k.gn_sum)
    pe_pair_sums(k, pe, k.gn_sq, k.tmp, k.gn_sum)


def act_rwkv_out(k, act):
    a = k.nc.scalar.activation
    act.wait_ge(k.gn_sum, 2)
    a(k.tmp[:, :, :].rearrange("p t n -> p (t n)").rearrange("p (b n) -> p b n", b=3), k.mb[:, 0:3, :], ACT.Sqrt,
      bias=k.eps[:, 1:2], scale=1.0 / HD).then_inc(k.gn_root, 1)
    act.wait_ge(k.gn_root, 2)
    a(k.y1_hi[:, 0:RT, :], k.c1[:, :, :], ACT.Copy)
    a(k.y1_hi[:, RT:KT, :], k.yb_keep[:, :, :], ACT.Copy).then_inc(k.gn_root, 1)


def dve_rwkv_out(k, dve):
    v = k.nc.vector
    tt = v.tensor_tensor
    c1 = k.c1[:, :, :]
    v.drain().then_inc(k.gn_in, 1)
    dve.wait_ge(k.gn_sum, 1)
    flat3 = c1.rearrange("p t n -> p (t n)").rearrange("p (b n) -> p b n", b=3)
    v.scalar_tensor_tensor(flat3, k.mb[:, 0:3, :], -1.0 / HD, flat3, ALU.mult, ALU.add)
    dve.drain()
    tt(k.tmp[:, :, :], c1, c1, ALU.mult).then_inc(k.gn_sq, 1)
    dve.wait_ge(k.gn_root, 1)
    v.reciprocal(k.tmp[:, :, :], k.tmp[:, :, :])
    dve.drain()
    tt(c1, c1, k.tmp[:, :, :], ALU.mult)
    dve.drain()
    for t in range(RT):
        v.tensor_scalar(k.c1[:, t, :], k.c1[:, t, :], vec(k, "lnx_w", t), vec(k, "lnx_b", t), ALU.mult, ALU.add)
    dve.drain()
    tt(c1, c1, k.bon[:, :, :], ALU.add)
    dve.drain()
    tt(c1, c1, k.gate[:, :, :], ALU.mult)
    dve.drain().then_inc(k.gn_root, 1)
    dve.wait_ge(k.gn_root, 3)
    tt(k.y1_lo[:, 0:RT, :], c1, k.y1_hi[:, 0:RT, :].bitcast(F32), ALU.subtract)
    tt(k.y1_lo[:, RT:KT, :], k.yb_keep[:, :, :], k.y1_hi[:, RT:KT, :].bitcast(F32), ALU.subtract)
    dve.drain()



FF_ROWS = slice(32, 40)


def pe_gates2(k, pe, l):
    pe.wait_ge(k.dec_in, l * 16 + 16)
    for t in range(2):
        last = k.nc.tensor.matmul(k.mb[:, t, 0:TOK], k.wal[:, t * P:(t + 1) * P], k.small[:, :], start=True, stop=True)
    last.then_inc(k.dec_mm, 1)


def act_gates2(k, act, l):
    a = k.nc.scalar.activation
    b_f = vec(k, "b_f", layer=l, rows=FF_ROWS)
    a(k.lf[0:8, :], k.small[FF_ROWS, :], ACT.Abs, bias=b_f)
    act.wait_ge(k.dec_mm, l + 1)
    for t in range(2):
        a(k.e1[:, t, :], k.mb[:, t, 0:TOK], ACT.Abs, bias=vec(k, "b_alpha", t, l))
    act.drain().then_inc(k.dec_abs, 1)
    a(k.lf[0:8, :], k.lf[0:8, :], ACT.Exp, scale=-1.0)
    a(k.e1[:, :, :], k.e1[:, :, :], ACT.Exp, scale=-1.0)
    act.drain()
    a(k.lf[0:8, :], k.lf[0:8, :], ACT.Ln, bias=1.0)
    a(k.e1[:, :, :], k.e1[:, :, :], ACT.Ln, bias=1.0).then_inc(k.dec_exp, 1)
    act.wait_ge(k.gz_ready, l + 1)
    s = 1.0 / 16.0
    a(k.e1[:, :, :], k.e2[:, :, :], ACT.Exp, scale=s)
    a(k.gst[:, :, :, :], k.gst[:, :, :, :], ACT.Exp, scale=s)
    act.drain()
    a(k.e2[:, :, :], k.e2[:, :, :], ACT.Exp, scale=-s).then_inc(k.gexp_ready, 1)
    a(k.p2[:, T_GA:T_GA + 16, :], k.p2[:, T_GA:T_GA + 16, :], ACT.Sigmoid)


def dve_gates2(k, dve, l):
    v = k.nc.vector
    v.tensor_scalar(k.cum[0:8, :], k.small[FF_ROWS, :], vec(k, "b_f", layer=l, rows=FF_ROWS), 0.0, ALU.add, ALU.min)
    dve.wait_ge(k.dec_abs, l + 1)
    for t in range(2):
        v.tensor_scalar(k.gcum[:, t, :], k.mb[:, t, 0:TOK], vec(k, "b_alpha", t, l), 0.0, ALU.add, ALU.min)
    dve.drain()
    dve.wait_ge(k.dec_exp, l + 1)
    v.tensor_tensor(k.lf[0:8, :], k.cum[0:8, :], k.lf[0:8, :], ALU.subtract)
    v.tensor_tensor(k.e1[:, :, :], k.gcum[:, :, :], k.e1[:, :, :], ALU.subtract)
    v.memset(k.e2[:, :, :], 1.0)
    dve.drain()
    v.tensor_tensor_scan(k.cum[0:8, :], k.e2[0:8, 0, :], k.lf[0:8, :], 0.0, ALU.mult, ALU.add)
    dve.drain()
    v.memset(k.e2[:, :, 0:TOK:GLA_C], 0.0)
    dve.drain()
    for t in range(2):
        v.tensor_tensor_scan(k.gcum[:, t, :], k.e2[:, t, :], k.e1[:, t, :], 0.0, ALU.mult, ALU.add)
    eye = const(k, "eye8", slice(0, 8))
    v.memset(k.minus8[:, :], -float(HD) ** 0.5)
    dve.drain()
    v.tensor_tensor(k.cumz[:, :, :], over(k.cum[0:8, :], 8), eye.unsqueeze(2).broadcast_to([8, 8, TOK]), ALU.mult)
    for t in range(2):
        g = k.gcum[:, t, :].rearrange("p (n c) -> p n c", n=GLA_N)
        mid = g[:, :, GLA_C // 2:GLA_C // 2 + 1]
        v.tensor_tensor(k.e2[:, t, :].rearrange("p (n c) -> p n c", n=GLA_N), g,
                        mid.broadcast_to([P, GLA_N, GLA_C]), ALU.subtract)
        v.tensor_copy(k.gst[:, t, 0, :], mid.rearrange("p n c -> p (n c)"))
        v.tensor_copy(k.gst[:, t, 1, :], g[:, :, GLA_C - 1:GLA_C].rearrange("p n c -> p (n c)"))
        v.tensor_tensor(k.gst[:, t, 2, :], g[:, :, GLA_C - 1:GLA_C].rearrange("p n c -> p (n c)"),
                        mid.rearrange("p n c -> p (n c)"), ALU.subtract)
    dve.drain()
    v.tensor_scalar(k.e2[:, :, :], k.e2[:, :, :], 80.0 * 16, -80.0 * 16, ALU.min, ALU.max).then_inc(k.gz_ready, 1)
    dve.wait_ge(k.gexp_ready, l + 1)
    q, kk = k.p2[:, T_GQ:T_GQ + 2, :], k.p2[:, T_GK:T_GK + 2, :]
    v.scalar_tensor_tensor(q, q, HD ** -0.5, k.e1[:, :, :], ALU.mult, ALU.mult)
    v.tensor_tensor(kk, kk, k.e2[:, :, :], ALU.mult)



FOX_UNITS = [(b, h) for b in range(3) for h in range(2)]


def pool_fox(k, pool):
    k.nc.gpsimd.memset(k.fkz[:, :, :], 0.0)
    k.nc.gpsimd.memset(k.fvz[:, :, :, :], 0.0)
    k.nc.gpsimd.memset(k.fvs[:, :], 0.0)
    pool.drain()


def pe_fox(k, pe, l):
    nc = k.nc
    ident = const(k, "ident")
    with pe.Fori(0, FOX_PAIRS) as i:
        it = l * FOX_PAIRS + i
        pe.wait_ge(k.fox_copy, it + 1)
        settle(k, pe)
        for b, (lo, hi) in enumerate(BLOCKS):
            last = nc.tensor.transpose(k.mb[0:hi - lo, 3, b * P:(b + 1) * P], k.fvs[:, lo:hi], ident)
        last.then_inc(k.fox_tok, 1)
        for u, (b, h) in enumerate(FOX_UNITS):
            lo, hi = BLOCKS[b]
            n = hi - lo
            pe.wait_ge(k.fox_masked, it * 6 + (u + 1))
            out = k.mb[:, 1, 0:hi]
            nc.tensor.matmul(out, k.fqs[:, lo:lo + P], k.fkz[:, h, 0:hi], start=True, stop=False)
            nc.tensor.matmul(out, k.minus8[:, :], k.cumz[:, bass.ds(i * 2 + h, 1), 0:hi].rearrange("p a n -> p (a n)"),
                             start=False, stop=True).then_inc(k.fox_sc, 1)
            pe.wait_ge(k.fox_tok_evac, it + 1)
            pe.wait_ge(k.fox_norm, it * 6 + (u + 1))
            settle(k, pe)
            for c in range(b + 1):
                clo, chi = BLOCKS[c]
                last = nc.tensor.transpose(k.mb[0:chi - clo, 2, c * P:c * P + n], k.fp[0:n, clo:chi],
                                           ident[0:n, 0:n])
            last.then_inc(k.fox_tr, 1)
            pe.wait_ge(k.fox_pt, it * 6 + (u + 1))
            settle(k, pe)
            for c in range(b + 1):
                clo, chi = BLOCKS[c]
                last = nc.tensor.matmul(k.acc[:, 0, lo:hi], k.fvz[0:chi - clo, c, h, :], k.fpt[0:chi - clo, c, 0:n],
                                        start=(h == 0 and c == 0), stop=(h == 1 and c == b))
            last.then_inc(k.fox_pv, 1)


def act_fox(k, act, l):
    a = k.nc.scalar.activation
    with act.Fori(0, FOX_PAIRS) as i:
        it = l * FOX_PAIRS + i
        act.wait_ge(k.fox_y, it + 1)
        a(k.fqs[:, :], tile(k.p2, i + T_FQ), ACT.Copy)
        for h, rows in enumerate(HALVES):
            a(k.fkz[rows, h, :], tile(k.p2, i + T_FK, rows=rows), ACT.Copy)
        a(k.fvs[:, :], tile(k.p2, i + T_FV), ACT.Copy).then_inc(k.fox_copy, 1)
        act.wait_ge(k.fox_tok, it + 1)
        for c, (lo, hi) in enumerate(BLOCKS):
            for h in range(2):
                last = a(k.fvz[0:hi - lo, c, h, HALVES[h]],
                         k.mb[0:hi - lo, 3, c * P + h * HD:c * P + (h + 1) * HD], ACT.Copy)
        last.then_inc(k.fox_tok_evac, 1)
        for u, (b, h) in enumerate(FOX_UNITS):
            lo, hi = BLOCKS[b]
            n = hi - lo
            act.wait_ge(k.max_ready, 8 + it * 6 + (u + 1))
            act.wait_ge(k.fox_tr, it * 6 + (u + 1))
            a(k.fp[0:n, 0:hi], k.fs[0:n, 0:hi], ACT.Exp, bias=k.fstat[0:n, 0:1],
              accum_out=k.fstat[0:n, 1:2]).then_inc(k.fox_p, 1)
            act.wait_ge(k.fox_tr, it * 6 + (u + 2))
            act.wait_ge(k.fox_pv, it * 6 + (u + 1))
            for c in range(b + 1):
                clo, chi = BLOCKS[c]
                last = a(k.fpt[0:chi - clo, c, 0:n], k.mb[0:chi - clo, 2, c * P:c * P + n], ACT.Copy)
            last.then_inc(k.fox_pt, 1)
        act.wait_ge(k.t_ready, 1 + it + 1)
        a(tile(k.y_hi, i), k.fy[:, :], ACT.Copy).then_inc(k.y_ready, 1)


def dve_fox(k, dve, l):
    v = k.nc.vector
    mask = const(k, "mask_fox")
    with dve.Fori(0, FOX_PAIRS) as i:
        it = l * FOX_PAIRS + i
        for u, (b, h) in enumerate(FOX_UNITS):
            lo, hi = BLOCKS[b]
            n = hi - lo
            at = (TOK - P) - lo
            dve.wait_ge(k.fox_sc, it * 6 + (u + 1))
            v.scalar_tensor_tensor(k.fs[0:n, 0:hi], k.mb[0:n, 1, 0:hi], HD ** -0.5, mask[0:n, at:at + hi],
                                   ALU.mult, ALU.add).then_inc(k.fox_masked, 1)
            dve.drain()
            v.tensor_reduce(k.fstat[0:n, 0:1], k.fs[0:n, 0:hi], AX, ALU.max, negate=True).then_inc(k.max_ready, 1)
            dve.wait_ge(k.fox_p, it * 6 + (u + 1))
            v.reciprocal(k.fstat[0:n, 2:3], k.fstat[0:n, 1:2])
            dve.drain()
            v.tensor_scalar(k.fp[0:n, 0:hi], k.fp[0:n, 0:hi], k.fstat[0:n, 2:3], None,
                            ALU.mult).then_inc(k.fox_norm, 1)
        dve.wait_ge(k.fox_pv, it * 6 + 7)
        v.tensor_copy(k.fy[:, :], k.acc[:, 0, 0:TOK]).then_inc(k.t_ready, 1)
        dve.drain()
        dve.wait_ge(k.y_ready, it + 1)
        v.tensor_tensor(tile(k.y_lo, i), k.fy[:, :], tile(k.y_hi, i).bitcast(F32), ALU.subtract).then_inc(k.fox_y, 1)



def pool_gla(k, pool):
    k.nc.gpsimd.memset(k.gkz[:, :, :], 0.0)
    k.nc.gpsimd.memset(k.gsm[:, :, :, :], 0.0).then_inc(k.gla_zero, 1)


def pe_gla(k, pe, l):
    nc = k.nc
    mm = nc.tensor.matmul
    ident = const(k, "ident")
    with pe.Fori(0, 2) as i:
        it = l * 2 + i
        pe.wait_ge(k.gla_copy, it + 1)
        for n in range(GLA_N):
            c = slice(n * GLA_C, (n + 1) * GLA_C)
            nc.tensor.transpose(k.mb[0:GLA_C, 2, n * P:(n + 1) * P], k.gks[:, c], ident)
            for h in range(2):
                last = nc.tensor.transpose(k.mb[0:GLA_C, h, n * P:(n + 1) * P], k.gvs[:, h, c], ident)
        last.then_inc(k.gla_tok, 1)
        for h in range(2):
            for n in range(GLA_N):
                c = slice(n * GLA_C, (n + 1) * GLA_C)
                last = mm(k.acc[0:GLA_C, h, c], k.gkz[:, h, c], tile(k.p2, i + T_GQ, c), start=True, stop=True)
        last.then_inc(k.gla_att, 1)
        pe.wait_ge(k.gla_tok_evac, it + 1)
        for h in range(2):
            for n in range(GLA_N - 1):
                last = mm(k.mb[:, 2 + h, n * P:(n + 1) * P], k.gkt[:, n, :], k.gvt[:, n, h, :], start=True, stop=True)
        last.then_inc(k.gla_state, 1)
        pe.wait_ge(k.gla_att_evac, it + 1)
        pe.wait_ge(k.gla_state_evac, it + 1)
        for h in range(2):
            for n in range(GLA_N):
                c = slice(n * GLA_C, (n + 1) * GLA_C)
                last = mm(k.mb[:, h, c], k.gvt[:, n, h, :], k.gat[:, n, h, :], start=True, stop=n == 0)
                if n > 0:
                    last = mm(k.mb[:, h, c], k.gsm[:, n - 1, h, :], tile(k.p2, i + T_GQ, c), start=False, stop=True)
        last.then_inc(k.gla_o, 1)
        pe.wait_ge(k.gla_sq, it + 1)
        for h in range(2):
            last = mm(k.acc[:, h, 0:TOK], k.mean_ones[:, :], k.gsq[:, h, :], start=True, stop=True)
        last.then_inc(k.gla_mean, 1)


def act_gla(k, act, l):
    a = k.nc.scalar.activation
    act.wait_ge(k.gla_zero, l + 1)
    settle(k, act)
    with act.Fori(0, 2) as i:
        it = l * 2 + i
        act.wait_ge(k.gla_y, it + 1)
        for h, rows in enumerate(HALVES):
            a(k.gkz[rows, h, :], tile(k.p2, i + T_GK, rows=rows), ACT.Copy)
        a(k.gks[:, :], tile(k.p2, i + T_GK), ACT.Copy)
        a(k.gvs[:, :, :], k.p2[:, bass.ds(i * 2 + T_GV, 2), :], ACT.Copy).then_inc(k.gla_copy, 1)
        act.wait_ge(k.gla_tok, it + 1)
        for h in range(2):
            a(k.gvt[:, :, h, :], k.mb[0:GLA_C, h, :].rearrange("p (n c) -> p n c", n=GLA_N), ACT.Copy)
        a(k.gkt[:, :, :], k.mb[0:GLA_C, 2, :].rearrange("p (n c) -> p n c", n=GLA_N),
          ACT.Copy).then_inc(k.gla_tok_evac, 1)
        a(k.gr_[:, :, :], k.p2[:, bass.ds(i * 2 + T_GR, 2), :], ACT.Sigmoid)
        act.wait_ge(k.gla_o, it + 1)
        for h in range(2):
            a(k.go[:, h, :], k.mb[:, h, 0:TOK], ACT.Copy)
            last = a(k.gsq[:, h, :], k.mb[:, h, 0:TOK], ACT.Square)
        last.then_inc(k.gla_sq, 1)
        act.wait_ge(k.gla_mean, it + 1)
        for h in range(2):
            last = a(k.gsq[:, h, :], k.acc[:, h, 0:TOK], ACT.Sqrt, bias=k.eps[:, 0:1], scale=float(D) / P)
        last.then_inc(k.gla_root, 1)
        for h in range(2):
            act.wait_ge(k.wh_y, it * 2 + (h + 1))
            a(tile(k.y_hi, i * 2 + (4 + h)), k.go[:, h, :], ACT.Copy).then_inc(k.gyh_ready, 1)


def dve_gla(k, dve, l):
    v = k.nc.vector
    gm = const(k, "gla_mask", slice(0, GLA_C))
    dve.wait_ge(k.gla_zero, l + 1)
    settle(k, dve)
    with dve.Fori(0, 2) as i:
        it = l * 2 + i
        dve.wait_ge(k.gla_att, it + 1)
        for h in range(2):
            last = v.tensor_tensor(k.gat[:, :, h, :], k.acc[0:GLA_C, h, 0:TOK].rearrange("p (n c) -> p n c", n=GLA_N),
                                   over(gm, GLA_N), ALU.mult)
        last.then_inc(k.gla_att_evac, 1)
        dve.wait_ge(k.gla_state, it + 1)

        def factor(which, n, rows):
            g = k.gst[rows, bass.ds(i, 1), which, n:n + 1]
            return g.rearrange("p a n -> p (a n)")
        for h, rows in enumerate(HALVES):
            s = k.gs[rows, :]
            for n in range(GLA_N - 1):
                add = k.mb[rows, 2 + h, n * P:(n + 1) * P]
                if n > 0:
                    v.tensor_scalar(s, s, factor(1, n, rows), None, ALU.mult)
                    dve.drain()
                    v.scalar_tensor_tensor(s, add, factor(2, n, rows), s, ALU.mult, ALU.add)
                else:
                    v.tensor_scalar(s, add, factor(2, n, rows), None, ALU.mult)
                dve.drain()
                last = v.tensor_scalar(k.gsm[rows, n, h, :], s, factor(0, n + 1, rows), None, ALU.mult)
        last.then_inc(k.gla_state_evac, 1)
        dve.wait_ge(k.gla_root, it + 1)
        v.reciprocal(k.gsq[:, :, :], k.gsq[:, :, :])
        v.tensor_tensor(k.gr_[:, :, :], k.gr_[:, :, :], k.p2[:, bass.ds(i * 2 + T_GR, 2), :], ALU.mult)
        dve.drain()
        for h in range(2):
            g = k.vec[:, bass.ds(l * VEC_LAYER + i * 2 + (VEC["g_gla"][0] + h), 1)]
            v.scalar_tensor_tensor(k.go[:, h, :], k.go[:, h, :], g, k.gsq[:, h, :], ALU.mult, ALU.mult)
        dve.drain()
        for h in range(2):
            v.tensor_tensor(k.go[:, h, :], k.go[:, h, :], k.gr_[:, h, :], ALU.mult).then_inc(k.wh_y, 1)
        for h in range(2):
            t = i * 2 + (4 + h)
            dve.drain()
            dve.wait_ge(k.gyh_ready, it * 2 + (h + 1))
            last = v.tensor_tensor(tile(k.y_lo, t), k.go[:, h, :], tile(k.y_hi, t).bitcast(F32), ALU.subtract)
        last.then_inc(k.gla_y, 1)



W1 = slice(META, TOK)
W2 = slice(0, TOK)


def pe_ada(k, pe, first, count, land_first):
    def one(i, b, half):
        par = (land_first + b) % 2
        pe.wait_ge(k.landed[par], (half + 1) * 16)
        for o in range(2):
            for t in range(KT):
                last = k.nc.tensor.matmul(k.mb[:, 2, bass.ds(i * 2 + (2 * first + o), 1)],
                                          k.land[:, par, (o * KT + t) * P:(o * KT + t + 1) * P],
                                          k.csil[:, t:t + 1], start=t == 0, stop=t == KT - 1)
        last.then_inc(k.ada_done, 1)
    with pe.Fori(0, count // 2) as i:
        for b in range(2):
            one(i * 2 + b, b, (land_first + b) // 2 + i)


def program_tensor(k, pe):
    pe.sem_inc(k.ada_done, 2)
    pe.sem_inc(k.panel_done, 2)
    pe.sem_inc(k.p_tr, 1)
    pe.sem_inc(k.pv_done, 1)
    pe.sem_inc(k.fox_tr, 1)
    pe.sem_inc(k.fox_pv, 1)
    pe.wait_ge(k.const_ready, 1)
    pe.wait_ge(k.vec_loaded, 32)
    pe.wait_ge(k.csil_ready, 1)
    pe_ada(k, pe, 0, ADA_FIRST, 0)
    pe_pre(k, pe, 0, W1)
    pe_project(k, pe, 0, IN1, 2, W1)
    pe_ada(k, pe, ADA_FIRST, ADA_LAST, ADA_FIRST + IN1)
    stage_end(k, pe, 1)
    pe_att(k, pe)
    stage_end(k, pe, 2)
    pe_rwkv_prep(k, pe)
    stage_end(k, pe, 3)
    pe_rwkv_pairs(k, pe)
    pe_rwkv_out(k, pe)
    stage_end(k, pe, 4)
    pe_branches(k, pe, M_AB1, SEQ, k.y1_hi, k.y1_lo, RT)
    pe.wait_ge(k.yl_ready, KT)
    pe_project(k, pe, M_OUT1, OUT, 2, W1)
    pe_stat(k, pe, 1, W1)
    pe_pre(k, pe, 1, W1)
    pe_ffn(k, pe, 0, M_GU1, M_DOWN1, 1, W1)
    with pe.Fori(0, LAYERS) as l:
        loop = l * (L_PANELS // 2)
        pe_pre(k, pe, l * 3 + 2, W2)
        pe_ffn(k, pe, l * 2 + 1, M_LAYER + L_GUA, M_LAYER + L_DOWNA, l * 3 + 2, W2, loop)
        pe_pre(k, pe, l * 3 + 3, W2)
        pe_project(k, pe, M_LAYER + L_SINGLE, SINGLES, 1, W2, loop)
        pe_project(k, pe, M_LAYER + L_IN, IN2, 2, W2, loop)
        stage_end(k, pe, l * 4 + 5)
        pe_gates2(k, pe, l)
        stage_end(k, pe, l * 4 + 6)
        pe_fox(k, pe, l)
        stage_end(k, pe, l * 4 + 7)
        pe_gla(k, pe, l)
        stage_end(k, pe, l * 4 + 8)
        pe_branches(k, pe, M_LAYER + L_AB, TOK, k.y_hi, k.y_lo, 4, loop)
        pe.wait_ge(k.yl_ready, l * KT + 2 * KT)
        settle(k, pe)
        pe_project(k, pe, M_LAYER + L_OUT, OUT, 2, W2, loop)
        pe_stat(k, pe, l * 6 + 7, W2)
        pe_pre(k, pe, l * 3 + 4, W2)
        pe_ffn(k, pe, l * 2 + 2, M_LAYER + L_GUB, M_LAYER + L_DOWNB, l * 3 + 4, W2, loop)


def prologue(fn, k, eng, start, size, loop=0):
    for b in range(2):
        fn(k, eng, Panel.of(start + b, loop), size)


def program_scalar(k, act, d):
    nc = k.nc
    act.dma_start(k.const[:, :], d["const"]).then_inc(k.vec_loaded, 16)
    act.dma_start(k.x[:, :, W1], d["x"]).then_inc(k.x_loaded, 16)
    act.dma_start(k.x[:, :, 0:META], d["meta"]).then_inc(k.x_loaded, 16)
    act.wait_ge(k.vec_loaded, 32)
    nc.scalar.activation(k.csil[:, :], vec(k, "c", n=KT), ACT.Sigmoid).then_inc(k.csig, 1)
    act.wait_ge(k.const_ready, 1)
    act.wait_ge(k.x_loaded, 32)
    act_pre(k, act, 0, W1, lambda t: k.mod[:, t:t + 1])
    prologue(split_hi, k, act, 0, IN_K)
    act_ahead_only(k, act, 0, IN1, IN_K, (None, None))
    stage_end(k, act, 1)
    act_att(k, act)
    stage_end(k, act, 2)
    act_rwkv_prep(k, act)
    nc.scalar.activation(k.gates[:, :, :], k.gates[:, :, :], ACT.Sigmoid)
    stage_end(k, act, 3)
    prologue(split_hi, k, act, M_AB1, AB_K)
    act_rwkv_pairs(k, act)
    act_rwkv_out(k, act)
    stage_end(k, act, 4)
    act_merge(k, act, 0, M_AB1, SEQ, W1, (OUT_K, OUT_K))
    act_products(k, act, 0, M_OUT1, 2, W1, OUT_K, (GU_K, GU_K))
    act_root(k, act, 1, W1)
    act_pre(k, act, 1, W1, lambda t: k.mod[:, 24 + t:25 + t], updates=0)
    act_ffn(k, act, 0, M_GU1, M_DOWN1, 1, W1, (None, None))
    with act.Fori(0, LAYERS) as l:
        loop = l * (L_PANELS // 2)
        prologue(split_hi, k, act, M_LAYER, GU_K, loop)
        act_pre(k, act, l * 3 + 2, W2, updates=l * 3 + 1)
        act_ffn(k, act, l * 2 + 1, M_LAYER + L_GUA, M_LAYER + L_DOWNA, l * 3 + 2, W2, (AB_K, AB_K), loop)
        act_pre(k, act, l * 3 + 3, W2, updates=l * 3 + 2)
        act_ahead_only(k, act, M_LAYER + L_SINGLE, SINGLES, AB_K, (IN_K, IN_K), loop)
        act_ahead_only(k, act, M_LAYER + L_IN, IN2, IN_K, (AB_K, AB_K), loop)
        stage_end(k, act, l * 4 + 5)
        act_gates2(k, act, l)
        stage_end(k, act, l * 4 + 6)
        act_fox(k, act, l)
        stage_end(k, act, l * 4 + 7)
        act_gla(k, act, l)
        stage_end(k, act, l * 4 + 8)
        act_merge(k, act, l + 1, M_LAYER + L_AB, TOK, W2, (OUT_K, OUT_K), loop)
        act_products(k, act, l * 3 + 3, M_LAYER + L_OUT, 2, W2, OUT_K, (GU_K, GU_K), loop)
        act_root(k, act, l * 6 + 7, W2)
        act_pre(k, act, l * 3 + 4, W2, updates=l * 3 + 3)
        act_ffn(k, act, l * 2 + 2, M_LAYER + L_GUB, M_LAYER + L_DOWNB, l * 3 + 4, W2, (None, None), loop)


def program_vector(k, dve):
    v = k.nc.vector
    dve.sem_inc(k.lo_ready, 2)
    dve.sem_inc(k.acc_free, 2)
    dve.sem_inc(k.sq_used, 2)
    dve.sem_inc(k.pv_evac, 1)
    dve.sem_inc(k.masked, 1)
    dve.sem_inc(k.y_evac, 1)
    dve.sem_inc(k.fox_y, 1)
    dve.sem_inc(k.fox_masked, 1)
    dve.sem_inc(k.gla_y, 1)
    v.memset(k.ssum[:, :], 0.0)
    dve.wait_ge(k.csig, 1)
    v.tensor_tensor(k.csil[:, :], k.csil[:, :], vec(k, "c", n=KT), ALU.mult).then_inc(k.csil_ready, 1)
    for l in range(LAYERS):
        for name in ("post1", "post2"):
            p = vec(k, name, l * VEC_LAYER, n=KT)
            v.tensor_scalar(p, p, 0.5, None, ALU.mult)
    dve.wait_ge(k.ada_done, ADA_FIRST + 2)
    v.tensor_tensor(k.mod[:, 0:16], k.mb[:, 2, 0:16], vec(k, "b_ada", n=16), ALU.add)
    dve.drain()
    v.scalar_tensor_tensor(k.fold[:, 0, :], k.mod[:, 8:16], 1.0, vec(k, "g_pre_mix", n=KT), ALU.add, ALU.mult)
    dve.drain()
    dve_pre(k, dve, 0, W1, lambda t: k.fold[:, 0, t:t + 1], lambda t: k.mod[:, t:t + 1])
    prologue(split_lo, k, dve, 0, IN_K)

    def dst(i):
        return k.p_in[:, bass.ds(i * 2, 2), 1:SEQ + 1]
    dve.wait_ge(k.const_ready, 2)
    dve_copy_out(k, dve, 0, 10, 2, dst, SEQ, IN_K, (IN_K, IN_K), signal=k.pin_ready)
    dve_copy_out(k, dve, 10, 9, 2, lambda i: k.qkv[:, bass.ds(i * 2, 2), :], SEQ, IN_K, (IN_K, IN_K))
    dve_copy_out(k, dve, 19, 8, 2, lambda i: k.gates[:, bass.ds(i * 2, 2), :], SEQ, IN_K, (None, None))
    dve.wait_ge(k.ada_done, ADA_FIRST + ADA_LAST + 2)
    v.tensor_tensor(k.mod[:, 16:48], k.mb[:, 2, 16:48], vec(k, "b_ada", 16, n=32), ALU.add)
    dve.drain()
    v.tensor_tensor(k.fold[:, 1, :], k.mod[:, 16:24], vec(k, "g_post_mix", n=KT), ALU.mult)
    v.scalar_tensor_tensor(k.fold[:, 2, :], k.mod[:, 32:40], 1.0, vec(k, "g_pre_ffn", n=KT), ALU.add, ALU.mult)
    v.tensor_tensor(k.fold[:, 3, :], k.mod[:, 40:48], vec(k, "g_post_ffn", n=KT), ALU.mult)
    stage_end(k, dve, 1)
    dve_att(k, dve)
    stage_end(k, dve, 2)
    dve_rwkv_prep(k, dve)
    stage_end(k, dve, 3)
    prologue(split_lo, k, dve, M_AB1, AB_K)
    dve_rwkv_pairs(k, dve)
    dve_rwkv_out(k, dve)
    stage_end(k, dve, 4)
    dve_merge(k, dve, 0, M_AB1, SEQ, lambda t: tile(k.gates, t), lambda t: tile(k.gates, t + 8), W1, (OUT_K, OUT_K))
    dve_products(k, dve, 0, M_OUT1, 2, W1, OUT_K, (GU_K, GU_K))
    dve_post(k, dve, 0, W1, lambda t: k.fold[:, 1, t:t + 1])
    dve_pre(k, dve, 1, W1, lambda t: k.fold[:, 2, t:t + 1], lambda t: k.mod[:, 24 + t:25 + t])
    dve_ffn(k, dve, 0, M_GU1, M_DOWN1, 1, W1, lambda t: k.fold[:, 3, t:t + 1], (None, None))
    with dve.Fori(0, LAYERS) as l:
        loop = l * (L_PANELS // 2)

        def gain(name):
            return lambda t: vec(k, name, t, l)
        prologue(split_lo, k, dve, M_LAYER, GU_K, loop)
        dve_pre(k, dve, l * 3 + 2, W2, gain("pre1"))
        dve_ffn(k, dve, l * 2 + 1, M_LAYER + L_GUA, M_LAYER + L_DOWNA, l * 3 + 2, W2, gain("post1"),
                (AB_K, AB_K), loop)
        dve_pre(k, dve, l * 3 + 3, W2, gain("pre_mix"))

        def single(i):
            return k.small[:, :].unsqueeze(1) if i == 0 else k.p2[:, i - 1:i, :]
        dve_copy_out(k, dve, M_LAYER + L_SINGLE, SINGLES, 1, single, TOK, AB_K, (IN_K, IN_K), loop)
        dve_copy_out(k, dve, M_LAYER + L_IN, IN2, 2, lambda i: k.p2[:, bass.ds(i * 2 + 2, 2), :], TOK, IN_K,
                     (AB_K, AB_K), loop)
        stage_end(k, dve, l * 4 + 5)
        dve_gates2(k, dve, l)
        stage_end(k, dve, l * 4 + 6)
        dve_fox(k, dve, l)
        stage_end(k, dve, l * 4 + 7)
        dve_gla(k, dve, l)
        stage_end(k, dve, l * 4 + 8)
        dve_merge(k, dve, l + 1, M_LAYER + L_AB, TOK, lambda t: tile(k.p2, t + T_GA), lambda t: tile(k.p2, t + T_GB),
                  W2, (OUT_K, OUT_K), loop)
        dve_products(k, dve, l * 3 + 3, M_LAYER + L_OUT, 2, W2, OUT_K, (GU_K, GU_K), loop)
        dve_post(k, dve, l * 3 + 3, W2, gain("post_mix"))
        dve_pre(k, dve, l * 3 + 4, W2, gain("pre2"))
        dve_ffn(k, dve, l * 2 + 2, M_LAYER + L_GUB, M_LAYER + L_DOWNB, l * 3 + 4, W2, gain("post2"),
                (None, None), loop)


def program_gpsimd(k, pool, d):
    g = k.nc.gpsimd
    g.memset(k.mean_ones[:, :], 1.0 / D)
    g.memset(k.eps[:, 0:1], EPS)
    g.memset(k.eps[:, 1:2], GN_EPS).then_inc(k.const_ready, 1)
    g.memset(k.p_in[:, :, 0:1], 0.0).then_inc(k.const_ready, 1)
    pool_shift(k, pool)
    stage_end(k, pool, 1)
    pool_att(k, pool)
    stage_end(k, pool, 2)
    pool_rwkv(k, pool, d)
    stage_end(k, pool, 3)
    pool_rwkv_zero(k, pool)
    pool_rwkv_pairs(k, pool)
    stage_end(k, pool, 4)
    with pool.Fori(0, LAYERS) as l:
        stage_end(k, pool, l * 4 + 5)
        pool.dma_start(k.wal[:, :], flat(d["wal"], l)).then_inc(k.dec_in, 16)
        pool_fox(k, pool)
        stage_end(k, pool, l * 4 + 6)
        stage_end(k, pool, l * 4 + 7)
        pool_gla(k, pool)
        stage_end(k, pool, l * 4 + 8)


def build(nc, d):
    with ExitStack() as ctx:
        k = Kernel()
        k.nc = nc
        allocate(k, nc, ctx)
        semaphores(k, lambda name: ctx.enter_context(nc.semaphore(name)))
        block = ctx.enter_context(nc.Block())

        @block.sync
        def _(sp):
            program_sync(k, sp, d)

        @block.tensor
        def _(pe):
            program_tensor(k, pe)

        @block.scalar
        def _(act):
            program_scalar(k, act, d)

        @block.vector
        def _(dve):
            program_vector(k, dve)

        @block.gpsimd
        def _(pool):
            program_gpsimd(k, pool, d)



def panels(w, per):
    kt, nt = w.shape[0] // P, w.shape[1] // P
    return w.reshape(kt, P, nt // per, per, P).transpose(2, 1, 3, 0, 4).reshape(nt // per, P, per * kt * P)


def gate_up(w):
    return w.reshape(KT, P, 2, FT, P).transpose(3, 1, 2, 0, 4).reshape(FT, P, GU_K * P)


def columns(v):
    return v.reshape(-1, P).T


def lay_out(x):
    f = {name: np.asarray(a) for name, a in x.items()}
    d = {}
    d["x"] = np.ascontiguousarray(f["x"][0].T.reshape(KT, P, SEQ).transpose(1, 0, 2))
    d["meta"] = np.ascontiguousarray(f["meta_tokens_2"].T.reshape(KT, P, META).transpose(1, 0, 2))
    v = np.zeros((P, VEC_COLS), np.float32)

    def put(name, a, layer=0):
        at, n = VEC[name]
        at += layer * VEC_LAYER
        v[:, at:at + n] = columns(a.reshape(-1))
    for name, src in (("c", "c"), ("b_ada", "b_ada"), ("g_pre_mix",) * 2, ("g_post_mix",) * 2, ("mu", "mu_shift"),
                      ("w0",) * 2, ("a0",) * 2, ("k_k",) * 2, ("k_a",) * 2, ("r_k",) * 2, ("lnx_w",) * 2,
                      ("lnx_b",) * 2, ("g_pre_ffn",) * 2, ("g_post_ffn",) * 2):
        put(name, f[src])
    for l in range(LAYERS):
        for name, src in (("pre1", "g_pre_ffn1_2"), ("post1", "g_post_ffn1_2"), ("pre_mix", "g_pre_mix_2"),
                          ("post_mix", "g_post_mix_2"), ("pre2", "g_pre_ffn2_2"), ("post2", "g_post_ffn2_2"),
                          ("b_alpha", "b_alpha_2"), ("g_gla", "g_gla_out_2")):
            put(name, f[src][l], l)
        v[FF_ROWS, VEC["b_f"][0] + l * VEC_LAYER] = f["b_f_2"][l]
    d["vec"] = v
    d["const"] = constants()
    d["w_ada"] = panels(f["w_ada"][0], 2)
    w = f["w_in"][0]
    d["w_in"] = panels(w, 2)
    d["w_ab"] = panels(np.concatenate([f["w_a"][0], f["w_b"][0]], 0), 1)
    d["w_out"] = panels(f["w_out"][0], 2)
    d["w_gu"] = gate_up(f["w_ffn_in"][0])
    d["w_down"] = panels(f["w_ffn_out"][0], 1)
    low = np.zeros((2, P, RW), np.float32)
    low[0, 0:HD] = f["w2"][0]
    low[1, HD:P] = f["a2"][0]
    d["w2"], d["a2"], d["g2"] = low[0], low[1], f["g2"][0]
    wal = np.zeros((LAYERS, P, 256), np.float32)
    wal[:, 0:16] = f["w_alpha_up_2"]
    d["wal"] = wal

    def layers(fn):
        return np.concatenate([fn(l) for l in range(LAYERS)], 0)
    sizes = (512, 512, 512, 8, 256, 256, 512, 16, 512, 1024, 1024)
    ends = np.cumsum(sizes)

    def split_in(l):
        w = f["w_in_2"][l]
        fq, fk, fv, ff, gq, gk, gv, ga, gr, ma, mb = (w[:, e - s:e] for s, e in zip(sizes, ends))
        small = np.zeros((D, P), np.float32)
        small[:, 0:16] = ga
        small[:, FF_ROWS] = ff
        return small, np.concatenate([fq, fk, fv, gq, gk, gv, gr, ma, mb], 1)
    d["w_in_single_2"] = layers(lambda l: panels(np.concatenate([split_in(l)[0], split_in(l)[1][:, 0:2 * P]], 1), 1))
    d["w_in_2"] = layers(lambda l: panels(split_in(l)[1][:, 2 * P:], 2))
    d["w_ab_2"] = layers(lambda l: panels(np.concatenate([f["w_fox_o_2"][l], f["w_gla_o_2"][l]], 0), 1))
    d["w_out_2"] = layers(lambda l: panels(f["w_out_2"][l], 2))
    for n in ("1", "2"):
        d["w_gu" + n + "_2"] = layers(lambda l: gate_up(f["w_ffn" + n + "_gu_2"][l]))
        d["w_down" + n + "_2"] = layers(lambda l: panels(f["w_ffn" + n + "_down_2"][l], 1))
    return {name: np.ascontiguousarray(a) for name, a in d.items()}


def kernel(**inputs):
    import concourse.bacc as bacc
    from concourse.bass_utils import run_bass_kernel_spmd as run

    nc = bacc.Bacc("TRN2", target_bir_lowering=False, num_devices=1)
    arrays = {f"in_{name}": a for name, a in lay_out(inputs).items()}
    d = {name[3:]: nc.dram_tensor(name, a.shape, F32, kind="ExternalInput").ap() for name, a in arrays.items()}
    d["out"] = nc.dram_tensor("out_x", (P, KT, SEQ), F32, kind="ExternalOutput").ap()
    build(nc, d)
    got = run(nc, [arrays], core_ids=[0]).results[0]["out_x"]
    return np.ascontiguousarray(got.transpose(2, 1, 0).reshape(1, SEQ, D))
```

```python
from contextlib import ExitStack

import numpy as np
import concourse.bass as bass
from concourse import mybir

F32 = mybir.dt.float32
F32R = mybir.dt.float32r
ALU = mybir.AluOpType
ACT = mybir.ActivationFunctionType
AX = mybir.AxisListType.X

P = 128
D = 1024
KT = D // P
SEQ = 256
META = 16
TOK = META + SEQ
HD = 64
EPS = 1e-6
NEG = -1e30

RW = 768
RT = RW // P
SHIFT_TILES = 20
GN_EPS = 64e-5
DECAY = float(np.exp(-0.5))
CHUNK = 64
NCH = SEQ // CHUNK
FF = 2816
FT = FF // P
GROUPS = ((128, 1), (512, 4), (2048, 16))

LAYERS = 2
FOX_PAIRS = 4
GLA_C = 68
GLA_N = TOK // GLA_C
BLOCKS = ((0, 16), (16, 144), (144, 272))

GU_K, DOWN_K, IN_K, AB_K, OUT_K = 16, FT, 16, 8, 16
ADA_FIRST, ADA_LAST = 8, 16
ADA_K = 16
IN1, AB, OUT, GU, DOWN = 27, 8, 4, 22, 8
SINGLES, IN2 = 3, 19
M_AB1 = IN1
M_OUT1 = M_AB1 + AB
M_GU1 = M_OUT1 + OUT
M_DOWN1 = M_GU1 + GU
M_LAYER = M_DOWN1 + DOWN
L_GUA, L_DOWNA = 0, GU
L_SINGLE = GU + DOWN
L_IN = L_SINGLE + SINGLES
L_AB = L_IN + IN2
L_OUT = L_AB + AB
L_GUB = L_OUT + OUT
L_DOWNB = L_GUB + GU
L_PANELS = L_DOWNB + DOWN
assert L_PANELS % 2 == 0

T_R, T_K, T_V, T_WA, T_G = 0, 6, 12, 18, 19
T_FQ, T_FK, T_FV, T_GQ, T_GK, T_GV, T_GR, T_GA, T_GB = 0, 4, 8, 12, 14, 16, 20, 24, 32


def vector_table():
    at, cols = {}, 0
    for name, n in (("c", 8), ("b_ada", 48), ("g_pre_mix", 8), ("g_post_mix", 8), ("mu", 20), ("w0", 6), ("a0", 6),
                    ("k_k", 6), ("k_a", 6), ("r_k", 6), ("lnx_w", 6), ("lnx_b", 6), ("g_pre_ffn", 8),
                    ("g_post_ffn", 8)):
        at[name] = (cols, n)
        cols += n
    first = cols
    for name, n in (("pre1", 8), ("post1", 8), ("pre_mix", 8), ("post_mix", 8), ("pre2", 8), ("post2", 8),
                    ("b_alpha", 2), ("b_f", 1), ("g_gla", 4)):
        at[name] = (cols, n)
        cols += n
    per_layer = cols - first
    return at, cols + per_layer * (LAYERS - 1), per_layer


VEC, VEC_COLS, VEC_LAYER = vector_table()
CONST = {}
_at = 0
for _name, _n in (("ident", 128), ("rot", 128), ("mask_att", 768), ("mask_fox", 272), ("up_strict", 64),
                  ("lo_strict", 64), ("up_incl", 64), ("i2", 64), ("pair_ones", 128),
                  ("cos", 256), ("sin", 256), ("gla_mask", 68), ("eye8", 8)):
    CONST[_name] = (_at, _n)
    _at += _n
CONST_COLS = _at


def constants():
    c = np.zeros((P, CONST_COLS), np.float32)

    def put(name, a):
        at, n = CONST[name]
        c[:a.shape[0], at:at + n] = a.reshape(a.shape[0], n)

    i = np.arange(P)
    put("ident", np.eye(P))
    rot = np.zeros((P, P))
    for m in range(P):
        h, o = divmod(m, HD)
        if o < HD // 2:
            rot[h * HD + o + HD // 2, m] = -1.0
        else:
            rot[h * HD + o - HD // 2, m] = 1.0
    put("rot", rot)
    q, k = i[:, None], i[None, :]
    masks = np.zeros((P, 3, 2, P))
    for g, (window, dil) in enumerate(GROUPS):
        before, diag = q + P - k, q - k
        masks[:, g, 0] = np.where((before % dil == 0) & (before <= window), 0.0, NEG)
        masks[:, g, 1] = np.where((diag % dil == 0) & (diag >= 0) & (diag <= window), 0.0, NEG)
    put("mask_att", masks)
    put("mask_fox", np.concatenate([np.zeros((P, 144)), np.where(q >= k, 0.0, NEG)], 1))
    same = (q // CHUNK) == (k // CHUNK)
    s, t = (i % CHUNK)[:, None], np.arange(CHUNK)[None, :]
    put("up_strict", np.where(s < t, 1.0, 0.0))
    put("lo_strict", np.where(s > t, 1.0, 0.0))
    put("up_incl", np.where(s <= t, 1.0, 0.0))
    put("i2", np.where(s == t, 1.0, 0.0))
    put("pair_ones", np.where(same, 1.0, 0.0))
    half = HD // 2
    inv = (10000.0 ** (-np.arange(half, dtype=np.float32) / half)).astype(np.float32)
    ang = np.arange(SEQ, dtype=np.float32)[None, :] * inv[i % half][:, None]
    put("cos", np.cos(ang))
    put("sin", np.sin(ang))
    g = np.arange(GLA_C)
    put("gla_mask", np.where(g[:, None] <= g[None, :], 1.0, 0.0))
    put("eye8", np.eye(8))
    return c


class Panel:

    def __init__(self, half, par):
        self.half, self.par = half, par

    @classmethod
    def of(cls, m, loop=0):
        return cls(m // 2 + loop, m % 2)

    def ahead2(self):
        return Panel(self.half + 1, self.par)

    def count(self, extra):
        return self.half * 2 + (self.par + extra)

    def landed(self):
        return (self.half + 1) * 16


def section(eng, start, count, fn, loop=0, after=(None, None)):
    pairs = (count - 2) // 2
    if pairs > 0:
        with eng.Fori(0, pairs) as i:
            for b in range(2):
                fn(i * 2 + b, Panel.of(start + b, loop + i), "same")
    for t in range(2 * max(pairs, 0), count):
        left = count - 1 - t
        fn(t, Panel.of(start + t, loop), "same" if left >= 2 else after[1 - left])


class Kernel:
    pass


def allocate(k, nc, ctx):
    where = [16512]

    def at(name, shape, dt=F32, offset=None):
        size = 4 * int(np.prod(shape[1:]))
        here = where[0] if offset is None else offset
        t = nc.alloc_sbuf_tensor_at(name, shape, dt, offset=here)
        here += -(-size // 32) * 32
        if offset is None:
            where[0] = here
        return t, here

    def fixed(name, shape, dt=F32):
        return at(name, shape, dt)[0]

    def chain(start, *items):
        out = []
        for name, shape, *dt in items:
            t, start = at(name, shape, dt[0] if dt else F32, offset=start)
            out.append(t)
        return out, start

    k.land = fixed("land", [P, 2, FT * P])
    k.w_hi = fixed("w_hi", [P, 2, FT * P], F32R)
    k.w_lo = fixed("w_lo", [P, 2, FT * P], F32R)
    k.x = fixed("x", [P, KT, TOK])
    k.const = fixed("const", [P, CONST_COLS])
    k.vec = fixed("vec", [P, VEC_COLS])
    k.ssum = fixed("ssum", [P, TOK])
    k.root = fixed("root", [P, TOK])
    k.rstd = fixed("rstd", [P, TOK])
    norm_at = where[0]
    k.sq = fixed("sq", [P, 2, TOK])
    k.sq_post = fixed("sq_post", [P, 4, TOK])
    k.upd = fixed("upd", [P, 2, TOK])
    norm_end = where[0]
    k.mean_ones = fixed("mean_ones", [P, P])
    k.mod = fixed("mod", [P, 48])
    k.fold = fixed("fold", [P, 4, KT])
    k.csil = fixed("csil", [P, KT])
    k.eps = fixed("eps", [P, 2])
    h_at = where[0]
    k.h_hi = fixed("h_hi", [P, KT, TOK], F32R)
    k.h_lo = fixed("h_lo", [P, KT, TOK], F32R)
    k.f = fixed("f", [P, KT, TOK])
    h_end = where[0]
    arena = where[0]
    top = 229344

    (k.a_hi, k.a_lo, k.sig, k.t_ff, k.a_ff), end = chain(
        arena, ("a_hi", [P, FT, TOK], F32R), ("a_lo", [P, FT, TOK], F32R), ("sig", [P, 2, TOK]),
        ("t_ff", [P, 2, TOK]), ("a_ff", [P, 2, TOK]))
    assert end <= top, end

    (k.p_in, k.gates, k.c1), qkv_at = chain(
        arena, ("p_in", [P, SHIFT_TILES, SEQ + 1]), ("gates", [P, 16, SEQ]), ("c1", [P, RT, SEQ]))
    (k.qkv,), late = chain(qkv_at, ("qkv", [P, 18, SEQ]))
    (k.ada_first,), end = chain(arena, ("ada_first", [P, ADA_FIRST, ADA_K * P]))
    assert end <= top, (end, top)
    (k.ada_land,), end = chain(late, ("ada_land", [P, 2, ADA_K * P]))
    assert end <= top, (end, top)
    (k.qs, k.kz), end = chain(h_at, ("qs", [P, 3, SEQ]), ("kz", [P, 3, 2, SEQ]),)
    (k.vs, k.vz, k.s_att), end = chain(
        end, ("vs", [P, 3, SEQ]), ("vz", [P, 3, 2, 2, P]), ("s_att", [P, 2, 3, SEQ]))
    (k.rt1, k.rt2), _ = chain(norm_at, ("rt1", [P, 2, SEQ]), ("rt2", [P, 2, SEQ]))
    assert end <= h_end, (end, h_end)
    (k.p_att, k.pt_att, k.st_att), att_end = chain(
        late, ("p_att", [P, 2, 3, SEQ]), ("pt_att", [P, 2, 6, P]), ("st_att", [P, 2, 4]))
    assert att_end <= late + 4 * 2 * RT * SEQ + 96
    (k.bon, k.gate, k.tmp), end = chain(
        qkv_at, ("bon", [P, RT, SEQ]), ("gate", [P, RT, SEQ]), ("tmp", [P, RT, SEQ]))
    assert end <= late
    (k.beta, k.kap), rest = chain(late, ("beta", [P, RT, SEQ]), ("kap", [P, RT, SEQ]))
    (k.sw, k.kk, k.reset, k.w2p, k.a2p), end2 = chain(
        h_at, ("sw", [P, RT, SEQ]), ("kk", [P, RT, SEQ]), ("reset", [P, SEQ]), ("w2p", [P, RW]), ("a2p", [P, RW]))
    (k.g2,), end2 = chain(end2, ("g2", [P, RW]))
    assert end2 <= h_end
    (k.pc, k.yb_keep), rest = chain(rest, ("pc", [P, RT, NCH]), ("yb_keep", [P, 2, SEQ]))
    bd = [P, NCH, P]
    st = [P, NCH, CHUNK]
    names = (("al_bd", bd), ("be_bd", bd), ("ka_bd", bd), ("v_bd", bd), ("xr", bd), ("x_st", st),
             ("x_bd", bd), ("xt_bd", bd), ("rt_bd", bd), ("akt_bd", bd))
    place = h_at
    made = {}
    for name, shape in names:
        (made[name],), place = chain(place, (name, shape))
    assert place <= h_end, (place, h_end)
    place = rest
    for name, shape in (("qbt", st), ("qkt", st), ("au", bd), ("bet_bd", bd), ("bet_st", st), ("kat_bd", bd),
                        ("vt_bd", bd)):
        (made[name],), place = chain(place, (name, shape))
    assert place <= top, (place, top)
    place = qkv_at + 2 * 4 * RT * SEQ
    for name, shape in (("w_bd", bd), ("u_bd", bd), ("f_st", st), ("n_st", st)):
        (made[name],), place = chain(place, (name, shape))
    assert place <= late, (place, late)
    place = norm_at
    for name, shape in (("vt_st", st), ("u_st", st), ("m_bd", bd), ("s_st", [P, CHUNK]), ("s_bd", [P, 3, P])):
        (made[name],), place = chain(place, (name, shape))
    assert place <= norm_end, (place, norm_end)
    place = 16512 + 4 * 2 * FT * P
    second = {}
    for name, t in made.items():
        (second[name],), place = chain(place, (name + "_2nd", list(t.shape)))
    assert place <= 16512 + 4 * 6 * FT * P, place
    k.m = (made, second)
    (k.y1_hi, k.y1_lo), end = chain(arena, ("y1_hi", [P, KT, SEQ], F32R), ("y1_lo", [P, KT, SEQ], F32R))
    assert end <= arena + 4 * SHIFT_TILES * (SEQ + 1)

    (k.p2, k.y_hi, k.y_lo), mix_at = chain(
        arena, ("p2", [P, 40, TOK]), ("y_hi", [P, KT, TOK], F32R), ("y_lo", [P, KT, TOK], F32R))
    (k.small, k.wal, k.gcum), end = chain(mix_at, ("small", [P, TOK]), ("wal", [P, 256]), ("gcum", [P, 2, TOK]))
    (k.gst, k.cum, k.lf), end = chain(end, ("gst", [P, 2, 3, GLA_N]), ("cum", [P, TOK]), ("lf", [P, TOK]))
    k.mix_rest = end
    (k.e1, k.e2), end = chain(end, ("e1", [P, 2, TOK]), ("e2", [P, 2, TOK]))
    (k.minus8,), end = chain(end, ("minus8", [8, P]))
    assert end <= top, (end, top)
    (k.fqs, k.fkz, k.fvs, k.fvz, k.fs, k.fp, k.fpt, k.cumz), end = chain(
        h_at, ("fqs", [P, TOK]), ("fkz", [P, 2, TOK]), ("fvs", [P, TOK]), ("fvz", [P, 3, 2, P]),
        ("fs", [P, 2, TOK]), ("fp", [P, 2, TOK]), ("fpt", [P, 2, 3, P]), ("cumz", [8, 8, TOK]))
    assert end <= h_end, (end, h_end)
    (k.fstat, k.fy), end = chain(
        k.mix_rest, ("fstat", [P, 2, 4]), ("fy", [P, TOK]))
    assert end <= top
    (k.gkz, k.gks, k.gvs, k.gvt, k.gat, k.gkt, k.gs, k.gsm, k.go), end = chain(
        h_at, ("gkz", [P, 2, TOK]), ("gks", [P, TOK]), ("gvs", [P, 2, TOK]), ("gvt", [GLA_C, GLA_N, 2, P]),
        ("gat", [GLA_C, GLA_N, 2, GLA_C]), ("gkt", [GLA_C, GLA_N, P]), ("gs", [P, P]), ("gsm", [P, 3, 2, P]),
        ("go", [P, 2, TOK]))
    assert end <= h_end, (end, h_end)
    (k.gsq, k.gr_, k.gy), end = chain(k.mix_rest, ("gsq", [P, 2, TOK]), ("gr_", [P, 2, TOK]), ("gy", [P, TOK]))
    assert end <= top, (end, top)

    k.acc = ctx.enter_context(nc.psum_tensor("acc", [P, 4, 512], F32))
    k.mb = ctx.enter_context(nc.psum_tensor("mb", [P, 4, 512], F32))
    k.stat = k.mb[:, 3, 0:TOK]


def semaphores(k, sem):
    k.landed = (sem("landed0"), sem("landed1"))
    k.ada_first_landed = [sem(f"ada_first_landed{i}") for i in range(ADA_FIRST)]
    k.ada_landed = (sem("ada_landed0"), sem("ada_landed1"))
    k.ada_products = sem("ada_products")
    k.ada_done = sem("ada_done")
    k.hi_ready = sem("hi_ready")
    k.lo_ready = sem("lo_ready")
    k.panel_done = sem("panel_done")
    k.acc_free = sem("acc_free")
    k.x_loaded = sem("x_loaded")
    k.vec_loaded = sem("vec_loaded")
    k.lora_loaded = sem("lora_loaded")
    k.const_ready = sem("const_ready")
    k.csig = sem("csig")
    k.stored = sem("stored")
    k.sq_ready = sem("sq_ready")
    k.sq_used = sem("sq_used")
    k.sq_post_ready = sem("sq_post_ready")
    k.sums_ready = sem("sums_ready")
    k.stat_done = sem("stat_done")
    k.root_ready = sem("root_ready")
    k.n_ready = sem("n_ready")
    k.hh_ready = sem("hh_ready")
    k.hl_ready = sem("hl_ready")
    k.x_ready = sem("x_ready")
    k.sig_ready = sem("sig_ready")
    k.ah_ready = sem("ah_ready")
    k.al_ready = sem("al_ready")
    k.stage = sem("stage")
    k.pin_ready = sem("pin_ready")
    k.gla_zero = sem("gla_zero")
    k.gates_ready = sem("gates_ready")
    k.merged = sem("merged")
    k.yh_ready = sem("yh_ready")
    k.yl_ready = sem("yl_ready")
    k.t_ready = sem("t_ready")
    k.rot_done = sem("rot_done")
    k.q_copied = sem("q_copied")
    k.att_ready = sem("att_ready")
    k.v_tok = sem("v_tok")
    k.v_evac = sem("v_evac")
    k.scored = sem("scored")
    k.masked = sem("masked")
    k.p_ready = sem("p_ready")
    k.p_norm = sem("p_norm")
    k.p_tr = sem("p_tr")
    k.pt_ready = sem("pt_ready")
    k.pv_done = sem("pv_done")
    k.pv_evac = sem("pv_evac")
    k.wg_ready = sem("wg_ready")
    k.lora_mm = sem("lora_mm")
    k.lora_evac = sem("lora_evac")
    k.kk_sq = sem("kk_sq")
    k.kk_sum = sem("kk_sum")
    k.kk_root = sem("kk_root")
    k.c_ready = sem("c_ready")
    k.exp_ready = sem("exp_ready")
    k.arr_ready = sem("arr_ready")
    k.bon_in = sem("bon_in")
    k.bon_sum = sem("bon_sum")
    k.bd_pool = sem("bd_pool")
    k.bd_act = sem("bd_act")
    k.xbd_ready = sem("xbd_ready")
    k.round_act = sem("round_act")
    k.tok_act = sem("tok_act")
    k.max_ready = sem("max_ready")
    k.gram = sem("gram")
    k.gram_evac = sem("gram_evac")
    k.tok_mm = sem("tok_mm")
    k.tok_evac = sem("tok_evac")
    k.round_mm = sem("round_mm")
    k.round_evac = sem("round_evac")
    k.rt_copied = sem("rt_copied")
    k.u0_mm = sem("u0_mm")
    k.u0_evac = sem("u0_evac")
    k.wu_mm = sem("wu_mm")
    k.wu_evac = sem("wu_evac")
    k.mfn_mm = sem("mfn_mm")
    k.mfn_evac = sem("mfn_evac")
    k.chain_mm = sem("chain_mm")
    k.chain_evac = sem("chain_evac")
    k.y_mm = sem("y_mm")
    k.y_evac = sem("y_evac")
    k.gn_in = sem("gn_in")
    k.gn_sum = sem("gn_sum")
    k.gn_root = sem("gn_root")
    k.gn_sq = sem("gn_sq")
    k.dec_in = sem("dec_in")
    k.dec_exp = sem("dec_exp")
    k.dec_abs = sem("dec_abs")
    k.dec_mm = sem("dec_mm")
    k.gz_ready = sem("gz_ready")
    k.gexp_ready = sem("gexp_ready")
    k.gla_copy = sem("gla_copy")
    k.gla_tok = sem("gla_tok")
    k.gla_tok_evac = sem("gla_tok_evac")
    k.gla_att = sem("gla_att")
    k.gla_att_evac = sem("gla_att_evac")
    k.gla_state = sem("gla_state")
    k.gla_state_evac = sem("gla_state_evac")
    k.gla_o = sem("gla_o")
    k.gla_sq = sem("gla_sq")
    k.gla_mean = sem("gla_mean")
    k.gla_root = sem("gla_root")
    k.gla_y = sem("gla_y")
    k.wh_y = sem("wh_y")
    k.gyh_ready = sem("gyh_ready")
    k.y_ready = sem("y_ready")
    k.csil_ready = sem("csil_ready")
    k.settled = sem("settled")
    k.fox_copy = sem("fox_copy")
    k.fox_tok = sem("fox_tok")
    k.fox_tok_evac = sem("fox_tok_evac")
    k.fox_sc = sem("fox_sc")
    k.fox_masked = sem("fox_masked")
    k.fox_p = sem("fox_p")
    k.fox_norm = sem("fox_norm")
    k.fox_tr = sem("fox_tr")
    k.fox_pt = sem("fox_pt")
    k.fox_pv = sem("fox_pv")
    k.fox_y = sem("fox_y")


def stage_end(k, eng, n):
    eng.drain().then_inc(k.stage, 1)
    eng.wait_ge(k.stage, n * 4)
    settle(k, eng)


def settle(k, eng):
    eng.sem_inc(k.settled, 1)


def const(k, name, rows=slice(0, P)):
    at, n = CONST[name]
    return k.const[rows, at:at + n]


def vec(k, name, t=0, layer=None, n=1, rows=slice(0, P)):
    at = VEC[name][0]
    if layer is None:
        return k.vec[rows, bass.ds(at + t, n)]
    return k.vec[rows, bass.ds(layer * VEC_LAYER + (at + t), n)]



def load(k, sp, par, half, dram, size):
    sp.dma_start(k.land[:, par, 0:size * P], dram).then_inc(k.landed[par], 16)


def load_section(k, sp, start, count, dram, size, loop=0):
    def one(i, p, _):
        sp.wait_ge(k.lo_ready, p.count(1))
        load(k, sp, p.par, p.half, dram(i), size)
    section(sp, start, count, one, loop)


def load_with_ada(k, sp, d):
    def ada(i, slot):
        sp.dma_start(k.ada_land[:, slot, :], flat(d["w_ada"], i + ADA_FIRST)).then_inc(k.ada_landed[slot], 16)

    def one(i, p, _):
        sp.wait_ge(k.lo_ready, p.count(1))
        load(k, sp, p.par, p.half, flat(d["w_in"], i + 2), IN_K)
        sp.wait_ge(k.ada_products, i + (ADA_FIRST + 1))
        ada(i + 2, p.par)
    for b in range(2):
        load(k, sp, b, None, flat(d["w_in"], b), IN_K)
    sp.wait_ge(k.ada_products, ADA_FIRST)
    for b in range(2):
        ada(b, b)
    section(sp, 2, ADA_LAST - 2, one)


def flat(ap, i):
    return ap[bass.ds(i, 1), :, :].rearrange("a p n -> p (a n)")


def program_sync(k, sp, d):
    W = slice(META, TOK)
    sp.dma_start(k.vec[:, :], d["vec"]).then_inc(k.vec_loaded, 16)
    for i in range(ADA_FIRST):
        sp.dma_start(k.ada_first[:, i, :], flat(d["w_ada"], i)).then_inc(k.ada_first_landed[i], 16)
    load_with_ada(k, sp, d)
    load_section(k, sp, ADA_LAST, IN1 - ADA_LAST, lambda i: flat(d["w_in"], i + ADA_LAST), IN_K)
    load_section(k, sp, M_AB1, AB, lambda i: flat(d["w_ab"], i), AB_K)
    load_section(k, sp, M_OUT1, OUT, lambda i: flat(d["w_out"], i), OUT_K)
    load_section(k, sp, M_GU1, GU, lambda i: flat(d["w_gu"], i), GU_K)
    load_section(k, sp, M_DOWN1, DOWN, lambda i: flat(d["w_down"], i), DOWN_K)
    with sp.Fori(0, LAYERS) as l:
        q = l * (L_PANELS // 2)

        def part(start, count, name, size, each=None, first=0):
            n = count if each is None else each
            load_section(k, sp, M_LAYER + start, count, lambda i: flat(d[name], l * n + i + first), size, q)
        part(L_GUA, GU, "w_gu1_2", GU_K)
        part(L_DOWNA, DOWN, "w_down1_2", DOWN_K)
        part(L_SINGLE, SINGLES, "w_in_single_2", AB_K)
        part(L_IN, IN2, "w_in_2", IN_K)
        part(L_AB, AB, "w_ab_2", AB_K)
        part(L_OUT, OUT, "w_out_2", OUT_K)
        part(L_GUB, GU, "w_gu2_2", GU_K)
        part(L_DOWNB, DOWN, "w_down2_2", DOWN_K)
    sp.wait_ge(k.x_ready, KT * (2 + 3 * LAYERS))
    sp.dma_start(d["out"], k.x[:, :, W]).then_inc(k.stored, 16)
    sp.wait_ge(k.stored, 16)



def split_hi(k, act, p, size):
    for par in (0, 1):
        if par == p.par:
            act.wait_ge(k.landed[par], p.landed())
    act.wait_ge(k.panel_done, p.count(1))
    k.nc.scalar.activation(k.w_hi[:, p.par, 0:size * P], k.land[:, p.par, 0:size * P],
                           ACT.Copy).then_inc(k.hi_ready, 1)


def split_lo(k, dve, p, size):
    dve.wait_ge(k.hi_ready, p.count(1))
    k.nc.vector.tensor_tensor(k.w_lo[:, p.par, 0:size * P], k.land[:, p.par, 0:size * P],
                              k.w_hi[:, p.par, 0:size * P].bitcast(F32), ALU.subtract).then_inc(k.lo_ready, 1)


def ahead(fn, k, eng, p, nxt, size):
    if nxt is not None:
        fn(k, eng, p.ahead2(), size if nxt == "same" else nxt)


def panel_begin(k, pe, p):
    pe.wait_ge(k.lo_ready, p.count(3))
    pe.wait_ge(k.acc_free, p.count(1))


def tile_mm(k, out, par, tile, hi, lo, start, stop):
    c = slice(tile * P, (tile + 1) * P)
    mm = k.nc.tensor.matmul
    mm(out, k.w_hi[:, par, c], hi, start=start, stop=False)
    mm(out, k.w_hi[:, par, c], lo, start=False, stop=False)
    return mm(out, k.w_lo[:, par, c], hi, start=False, stop=stop)


def pe_project(k, pe, start, count, tiles, W, loop=0, ada=False):
    n = W.stop - W.start

    def one(i, p, _):
        panel_begin(k, pe, p)
        for o in range(tiles):
            for t in range(KT):
                last = tile_mm(k, k.acc[:, 2 * p.par + o, 0:n], p.par, o * KT + t, k.h_hi[:, t, W],
                               k.h_lo[:, t, W], t == 0, t == KT - 1)
        last.then_inc(k.panel_done, 1)
        if ada:
            pe_ada(k, pe, i + ADA_FIRST, p.par)
    section(pe, start, count, one, loop)



def dve_ada(k, dve, n, slot, src):
    w = src.rearrange("p (o t c) -> p t o c", o=2, t=KT)
    dve.wait_ge(k.ada_done, n + 1)
    sums, more = k.sq_post[:, 2 * slot:2 * slot + 2, 0:2 * P], k.upd[:, :, 0:2 * P]
    for t in range(KT):
        out = (sums if t % 4 < 2 else more)[:, t % 2, :].rearrange("p (o c) -> p o c", o=2)
        c = k.csil[:, t:t + 1]
        if t < 4:
            k.nc.vector.tensor_scalar(out, w[:, t], c, None, ALU.mult)
        else:
            k.nc.vector.scalar_tensor_tensor(out, w[:, t], c, out, ALU.mult, ALU.add)
        if t % 4 == 3:
            dve.drain()
    k.nc.vector.tensor_tensor(sums, sums, more, ALU.add).then_inc(k.ada_products, 1)


def pe_ada(k, pe, n, slot):
    pe.wait_ge(k.ada_products, n + 1)
    for o in range(2):
        for s in range(2):
            last = k.nc.tensor.matmul(k.mb[:, 2, bass.ds(n * 2 + o, 1)],
                                      k.sq_post[:, 2 * slot + s, o * P:(o + 1) * P],
                                      k.mean_ones[:, 0:1], start=s == 0, stop=s == 1)
    last.then_inc(k.ada_done, 1)


def dve_mod(k, dve, first, n):
    k.nc.vector.scalar_tensor_tensor(k.mod[:, first:first + n], k.mb[:, 2, first:first + n], float(D),
                                     vec(k, "b_ada", first, n=n), ALU.mult, ALU.add)
    dve.drain()


def dve_split_with_ada(k, dve, start, count, nxt):
    def one(i, p, ahead_size):
        dve.drain()
        dve.wait_ge(k.ada_landed[p.par], p.landed())
        dve_ada(k, dve, i + ADA_FIRST, p.par, k.ada_land[:, p.par, :])
        ahead(split_lo, k, dve, p, ahead_size, IN_K)
    section(dve, start, count, one, 0, nxt)


def pe_down(k, pe, start, W, loop=0):
    n = W.stop - W.start

    def one(i, p, _):
        panel_begin(k, pe, p)
        for t in range(FT):
            last = tile_mm(k, k.acc[:, 2 * p.par, 0:n], p.par, t, k.a_hi[:, t, W], k.a_lo[:, t, W],
                           t == 0, t == FT - 1)
        last.then_inc(k.panel_done, 1)
    section(pe, start, DOWN, one, loop)


def pe_branches(k, pe, start, n, y_hi, y_lo, first, loop=0):
    def one(i, p, _):
        panel_begin(k, pe, p)
        for t in range(KT):
            b = int(t >= first)
            last = tile_mm(k, k.acc[:, 2 * p.par + b, 0:n], p.par, t, y_hi[:, t, 0:n], y_lo[:, t, 0:n],
                           t in (0, first), t in (first - 1, KT - 1))
        last.then_inc(k.panel_done, 1)
    section(pe, start, AB, one, loop)



def pe_stat(k, pe, n, W):
    pe.wait_ge(k.sums_ready, n + 1)
    k.nc.tensor.matmul(k.mb[:, 3, 0:W.stop - W.start], k.mean_ones[:, :], k.ssum[:, W],
                       start=True, stop=True).then_inc(k.stat_done, 1)


def act_root(k, act, n, W):
    act.wait_ge(k.stat_done, n + 1)
    k.nc.scalar.activation(k.root[:, W], k.mb[:, 3, 0:W.stop - W.start], ACT.Sqrt,
                           bias=k.eps[:, 0:1]).then_inc(k.root_ready, 1)


def dve_rstd(k, dve, n, W):
    k.nc.vector.drain().then_inc(k.sums_ready, 1)
    dve.wait_ge(k.root_ready, n + 1)
    k.nc.vector.reciprocal(k.rstd[:, W], k.root[:, W])
    k.nc.vector.memset(k.ssum[:, :], 0.0)
    dve.drain()


def act_pre_sums(k, act, i, W, updates=None):
    for t in range(KT):
        if updates is not None:
            act.wait_ge(k.x_ready, updates * KT + (t + 1))
        act.wait_ge(k.sq_used, i * KT + (t + 1))
        k.nc.scalar.activation(k.sq[:, t % 2, W], k.x[:, t, W], ACT.Square).then_inc(k.sq_ready, 1)
    act_root(k, act, i * 2, W)


def act_pre(k, act, i, W, shift=None, updates=None):
    act_pre_sums(k, act, i, W, updates)
    act_pre_split(k, act, i, W, shift)


def act_pre_split(k, act, i, W, shift=None):
    for t in range(KT):
        act.wait_ge(k.n_ready, i * KT + (t + 1))
        if shift is None:
            r = k.nc.scalar.activation(k.h_hi[:, t, W], k.f[:, t, W], ACT.Copy)
        else:
            r = k.nc.scalar.activation(k.h_hi[:, t, W], k.f[:, t, W], ACT.Identity, bias=shift(t))
        r.then_inc(k.hh_ready, 1)


def dve_pre_sums(k, dve, i, W):
    v = k.nc.vector
    for t in range(KT):
        dve.wait_ge(k.sq_ready, i * KT + (t + 1))
        v.tensor_tensor(k.ssum[:, W], k.ssum[:, W], k.sq[:, t % 2, W], ALU.add).then_inc(k.sq_used, 1)
        if t < KT - 1:
            dve.drain()
    dve_rstd(k, dve, i * 2, W)


def dve_pre(k, dve, i, W, gain, shift=None):
    dve_pre_sums(k, dve, i, W)
    dve_pre_apply(k, dve, i, W, gain, shift)


def dve_pre_apply(k, dve, i, W, gain, shift=None):
    v = k.nc.vector

    def normed(t):
        v.scalar_tensor_tensor(k.f[:, t, W], k.x[:, t, W], gain(t), k.rstd[:, W], ALU.mult,
                               ALU.mult).then_inc(k.n_ready, 1)
    normed(0)
    for t in range(KT):
        if t + 1 < KT:
            normed(t + 1)
        if t == KT - 1:
            dve.drain()
        dve.wait_ge(k.hh_ready, i * KT + (t + 1))
        hh = k.h_hi[:, t, W].bitcast(F32)
        if shift is None:
            r = v.tensor_tensor(k.h_lo[:, t, W], k.f[:, t, W], hh, ALU.subtract)
        else:
            r = v.scalar_tensor_tensor(k.h_lo[:, t, W], k.f[:, t, W], shift(t), hh, ALU.add, ALU.subtract)
        r.then_inc(k.hl_ready, 1)


def pe_pre(k, pe, i, W):
    pe_stat(k, pe, i * 2, W)
    pe_h_ready(k, pe, i)


def pe_h_ready(k, pe, i):
    pe.wait_ge(k.hl_ready, i * KT + KT)
    settle(k, pe)


def act_products(k, act, i, start, tiles, W, size, nxt, loop=0):
    n = W.stop - W.start

    def one(t, p, ahead_size):
        act.wait_ge(k.panel_done, p.count(3))
        for o in range(tiles):
            k.nc.scalar.activation(k.sq_post[:, 2 * p.par + o, W], k.acc[:, 2 * p.par + o, 0:n],
                                   ACT.Square).then_inc(k.sq_post_ready, 1)
        ahead(split_hi, k, act, p, ahead_size, size)
    section(act, start, KT // tiles, one, loop, nxt)


def dve_products(k, dve, i, start, tiles, W, size, nxt, loop=0):
    n = W.stop - W.start
    v = k.nc.vector

    def one(idx, p, ahead_size):
        dve.wait_ge(k.panel_done, p.count(3))
        for o in range(tiles):
            t = idx * tiles + o
            f = k.f[:, bass.ds(t, 1), W].rearrange("p a n -> p (a n)")
            dve.wait_ge(k.sq_post_ready, i * KT + (t + 1))
            v.tensor_copy(f, k.acc[:, 2 * p.par + o, 0:n])
            r = v.tensor_tensor(k.ssum[:, W], k.ssum[:, W], k.sq_post[:, 2 * p.par + o, W], ALU.add)
            if o == tiles - 1:
                r.then_inc(k.acc_free, 1)
            dve.drain()
        ahead(split_lo, k, dve, p, ahead_size, size)
    section(dve, start, KT // tiles, one, loop, nxt)


def dve_post(k, dve, i, W, gain):
    v = k.nc.vector
    dve_rstd(k, dve, i * 2 + 1, W)

    def update(t):
        v.scalar_tensor_tensor(k.sq_post[:, t % 3, W], k.f[:, t, W], gain(t), k.rstd[:, W], ALU.mult, ALU.mult)
    update(0)
    for t in range(KT):
        if t + 1 < KT:
            update(t + 1)
        dve.drain()
        v.tensor_tensor(k.x[:, t, W], k.x[:, t, W], k.sq_post[:, t % 3, W], ALU.add).then_inc(k.x_ready, 1)



def act_gate_up(k, act, i, start, W, nxt, loop=0):
    n = W.stop - W.start

    def one(t, p, ahead_size):
        act.wait_ge(k.panel_done, p.count(3))
        k.nc.scalar.activation(k.sig[:, p.par, W], k.acc[:, 2 * p.par, 0:n], ACT.Sigmoid).then_inc(k.sig_ready, 1)
        ahead(split_hi, k, act, p, ahead_size, GU_K)
        act.wait_ge(k.acc_free, p.count(3))
        k.nc.scalar.activation(k.a_hi[:, bass.ds(t, 1), W].rearrange("p a n -> p (a n)"), k.a_ff[:, p.par, W],
                               ACT.Copy).then_inc(k.ah_ready, 1)
    section(act, start, GU, one, loop, nxt)


def dve_gate_up(k, dve, i, start, W, nxt, loop=0):
    n = W.stop - W.start
    v = k.nc.vector

    def one(t, p, ahead_size):
        dve.wait_ge(k.sig_ready, i * FT + (t + 1))
        v.tensor_tensor(k.t_ff[:, p.par, W], k.sig[:, p.par, W], k.acc[:, 2 * p.par, 0:n], ALU.mult)
        dve.drain()
        v.tensor_tensor(k.a_ff[:, p.par, W], k.t_ff[:, p.par, W], k.acc[:, 2 * p.par + 1, 0:n],
                        ALU.mult).then_inc(k.acc_free, 1)
        ahead(split_lo, k, dve, p, ahead_size, GU_K)
        dve.drain()
        dve.wait_ge(k.ah_ready, i * FT + (t + 1))
        a = bass.ds(t, 1)
        v.tensor_tensor(k.a_lo[:, a, W].rearrange("p a n -> p (a n)"), k.a_ff[:, p.par, W],
                        k.a_hi[:, a, W].rearrange("p a n -> p (a n)").bitcast(F32),
                        ALU.subtract).then_inc(k.al_ready, 1)
    section(dve, start, GU, one, loop, nxt)


def act_ffn(k, act, i, gu, down, post, W, nxt, loop=0):
    act_gate_up(k, act, i, gu, W, (DOWN_K, DOWN_K), loop)
    act_products(k, act, post, down, 1, W, DOWN_K, nxt, loop)
    act_root(k, act, post * 2 + 1, W)


def dve_ffn(k, dve, i, gu, down, post, W, gain, nxt, loop=0):
    dve_gate_up(k, dve, i, gu, W, (DOWN_K, DOWN_K), loop)
    dve_products(k, dve, post, down, 1, W, DOWN_K, nxt, loop)
    dve_post(k, dve, post, W, gain)


def pe_ffn(k, pe, i, gu, down, post, W, loop=0):
    pe_project(k, pe, gu, GU, 2, W, loop)
    pe.wait_ge(k.al_ready, i * FT + FT)
    settle(k, pe)
    pe_down(k, pe, down, W, loop)
    pe_stat(k, pe, post * 2 + 1, W)



def act_ahead_only(k, act, start, count, size, nxt, loop=0):
    section(act, start, count, lambda t, p, s: ahead(split_hi, k, act, p, s, size), loop, nxt)


def act_copy_out(k, act, start, count, tiles, dst, n, size, nxt, loop=0, signal=None):
    def one(i, p, ahead_size):
        ahead(split_hi, k, act, p, ahead_size, size)
        act.wait_ge(k.panel_done, p.count(3))
        k.nc.scalar.activation(dst(i), k.acc[:, 2 * p.par:2 * p.par + tiles, 0:n], ACT.Copy).then_inc(k.acc_free, 1)
        if signal is not None:
            k.nc.scalar.drain().then_inc(signal, 1)
    section(act, start, count, one, loop, nxt)


def dve_copy_out(k, dve, start, count, tiles, dst, n, size, nxt, loop=0, signal=None):
    def one(i, p, ahead_size):
        dve.wait_ge(k.panel_done, p.count(3))
        k.nc.vector.tensor_copy(dst(i), k.acc[:, 2 * p.par:2 * p.par + tiles, 0:n]).then_inc(k.acc_free, 1)
        if signal is not None:
            k.nc.vector.drain().then_inc(signal, 1)
        ahead(split_lo, k, dve, p, ahead_size, size)
    section(dve, start, count, one, loop, nxt)



def dve_merge(k, dve, i, start, n, ga, gb, W, nxt, loop=0):
    v = k.nc.vector

    def one(t, p, ahead_size):
        dve.wait_ge(k.panel_done, p.count(3))
        v.tensor_tensor(k.upd[:, 0, 0:n], ga(t), k.acc[:, 2 * p.par, 0:n], ALU.mult)
        v.tensor_tensor(k.upd[:, 1, 0:n], gb(t), k.acc[:, 2 * p.par + 1, 0:n], ALU.mult).then_inc(k.acc_free, 1)
        dve.drain()
        v.tensor_tensor(k.sq_post[:, p.par, 0:n], k.upd[:, 0, 0:n], k.upd[:, 1, 0:n],
                        ALU.add).then_inc(k.merged, 1)
        ahead(split_lo, k, dve, p, ahead_size, AB_K)
        dve.drain()
        dve.wait_ge(k.yh_ready, i * KT + (t + 1))
        a = bass.ds(t, 1)
        v.tensor_tensor(k.h_lo[:, a, W].rearrange("p a n -> p (a n)"), k.sq_post[:, p.par, 0:n],
                        k.h_hi[:, a, W].rearrange("p a n -> p (a n)").bitcast(F32),
                        ALU.subtract).then_inc(k.yl_ready, 1)
    section(dve, start, AB, one, loop, nxt)


def act_merge(k, act, i, start, n, W, nxt, loop=0):
    def one(t, p, ahead_size):
        ahead(split_hi, k, act, p, ahead_size, AB_K)
        act.wait_ge(k.merged, i * KT + (t + 1))
        k.nc.scalar.activation(k.h_hi[:, bass.ds(t, 1), W].rearrange("p a n -> p (a n)"),
                               k.sq_post[:, p.par, 0:n], ACT.Copy).then_inc(k.yh_ready, 1)
    section(act, start, AB, one, loop, nxt)


def tile(a, i, cols=slice(None), rows=slice(0, P)):
    return a[rows, bass.ds(i, 1), cols].rearrange("p a n -> p (a n)")


def over(a, n, axis=1):
    return a.unsqueeze(axis).broadcast_to([a.shape[0], n, a.shape[1]])


HALVES = (slice(0, HD), slice(HD, P))




def att_transposed(k, h, i, n):
    if i < 4:
        bank, at = (k.mb[:, 0, :], k.acc[:, 3, :])[h], i * P
    else:
        bank, at = k.mb[:, 3, :], (2 * h + i - 4) * P
    return bank[:, at:at + n * P]


def pool_att(k, pool):
    k.nc.gpsimd.memset(k.kz[:, :, :, :], 0.0)
    k.nc.gpsimd.memset(k.vz[:, :, :, :, :], 0.0).then_inc(k.gates_ready, 1)


def pe_att(k, pe):
    nc = k.nc
    ident = const(k, "ident")
    with pe.Fori(0, 2) as hp:
        pe.wait_ge(k.pv_evac, hp + 1)
        for g in range(3):
            for b in range(2):
                last = nc.tensor.matmul(k.mb[:, g, b * SEQ:(b + 1) * SEQ], const(k, "rot"),
                                        tile(k.qkv, hp + (b * 6 + 2 * g)), start=True, stop=True)
        last.then_inc(k.rot_done, 1)
        pe.wait_ge(k.q_copied, hp + 1)
        for g in range(2):
            for b in range(2):
                last = nc.tensor.transpose(k.mb[:, 3, (2 * g + b) * P:(2 * g + b + 1) * P],
                                           k.vs[:, g, b * P:(b + 1) * P], ident)
        last.then_inc(k.v_tok, 1)
        pe.wait_ge(k.att_ready, hp + 1)
        for b in range(2):
            last = nc.tensor.transpose(k.mb[:, 0, b * P:(b + 1) * P], k.vs[:, 2, b * P:(b + 1) * P], ident)
        last.then_inc(k.v_tok, 1)

        def scores(qb):
            n = (qb + 1) * P
            for h in range(2):
                pe.wait_ge(k.masked, hp * 4 + (2 * qb + h + 1))
                for g in range(3):
                    last = nc.tensor.matmul((k.mb, k.acc)[h][:, 1 + g // 2, (g % 2) * SEQ:(g % 2) * SEQ + n],
                                            k.qs[:, g, qb * P:(qb + 1) * P], k.kz[:, g, h, 0:n],
                                            start=True, stop=True)
                last.then_inc(k.scored, 1)
        scores(0)
        pe.wait_ge(k.v_evac, hp * 2 + 2)
        for qb in range(2):
            nb = 3 * (qb + 1)
            for h in range(2):
                pe.wait_ge(k.p_norm, hp * 4 + (2 * qb + h + 1))
                for i in range(nb):
                    g, b = divmod(i, qb + 1)
                    last = nc.tensor.transpose(att_transposed(k, h, i, 1), k.p_att[:, h, g, b * P:(b + 1) * P], ident)
                last.then_inc(k.p_tr, 1)
            if qb == 0:
                scores(1)
            for h in range(2):
                pe.wait_ge(k.pt_ready, hp * 4 + (2 * qb + h + 1))
                for i in range(nb):
                    g, b = divmod(i, qb + 1)
                    last = nc.tensor.matmul(k.acc[:, 0, qb * P:(qb + 1) * P], k.vz[:, g, b, h, :],
                                            k.pt_att[:, h, i, :], start=(h == 0 and i == 0),
                                            stop=(h == 1 and i == nb - 1))
                last.then_inc(k.pv_done, 1)


def act_att(k, act):
    nc = k.nc
    with act.Fori(0, 2) as hp:
        act.wait_ge(k.pv_evac, hp + 1)
        for g in range(3):
            last = nc.scalar.activation(k.vs[:, g, :], tile(k.qkv, hp + (12 + 2 * g)), ACT.Copy)
        last.then_inc(k.q_copied, 1)
        act.wait_ge(k.gates_ready, 1)
        act.wait_ge(k.v_tok, hp * 2 + 1)
        for h in range(2):
            src = k.mb[:, 3, :].rearrange("p (g b c) -> p (g b) c", g=2, b=2)[:, :, HALVES[h]]
            last = nc.scalar.activation(k.vz[:, 0:2, :, h, HALVES[h]].rearrange("p g b c -> p (g b) c"), src, ACT.Copy)
        last.then_inc(k.v_evac, 1)
        act.wait_ge(k.v_tok, hp * 2 + 2)
        for h in range(2):
            src = k.mb[:, 0, 0:2 * P].rearrange("p (b c) -> p b c", b=2)[:, :, HALVES[h]]
            last = nc.scalar.activation(k.vz[:, 2, :, h, HALVES[h]], src, ACT.Copy)
        last.then_inc(k.v_evac, 1)
        for qb in range(2):
            n = (qb + 1) * P
            nb = 3 * (qb + 1)
            for h in range(2):
                act.wait_ge(k.max_ready, hp * 4 + (2 * qb + h + 1))
                act.wait_ge(k.p_tr, hp * 4 + (2 * qb + h + 1))
                nc.scalar.activation(k.p_att[:, h, :, 0:n], k.s_att[:, h, :, 0:n], ACT.Exp,
                                     bias=k.st_att[:, h, 0:1], accum_out=k.st_att[:, h, 1:2]).then_inc(k.p_ready, 1)
            act.wait_ge(k.p_tr, hp * 4 + (2 * qb + 4))
            for h in range(2):
                act.wait_ge(k.pv_done, hp * 4 + (2 * qb + h + 1))
                last = nc.scalar.activation(k.pt_att[:, h, 0:min(nb, 4), :],
                                            att_transposed(k, h, 0, min(nb, 4)).rearrange("p (i c) -> p i c", c=P),
                                            ACT.Copy)
                if nb > 4:
                    last = nc.scalar.activation(k.pt_att[:, h, 4:nb, :],
                                                att_transposed(k, h, 4, nb - 4).rearrange("p (i c) -> p i c", c=P),
                                                ACT.Copy)
                last.then_inc(k.pt_ready, 1)


def dve_att(k, dve):
    v = k.nc.vector
    mask = const(k, "mask_att").rearrange("p (g n) -> p g n", g=3)
    dve.wait_ge(k.gates_ready, 1)
    with dve.Fori(0, 2) as hp:
        dve.drain()
        dve.wait_ge(k.rot_done, hp + 1)
        for g in range(3):
            for b in range(2):
                rt1, rt2 = k.rt1[:, b, :], k.rt2[:, b, :]
                v.tensor_tensor(rt1, tile(k.qkv, hp + (b * 6 + 2 * g)), const(k, "cos"), ALU.mult)
                v.tensor_tensor(rt2, k.mb[:, g, b * SEQ:(b + 1) * SEQ], const(k, "sin"), ALU.mult)
                dve.drain()
                if b == 0:
                    last = v.tensor_tensor(k.qs[:, g, :], rt1, rt2, ALU.add)
                else:
                    for h, rows in enumerate(HALVES):
                        last = v.tensor_tensor(k.kz[rows, g, h, :], rt1[rows], rt2[rows], ALU.add)
        last.then_inc(k.att_ready, 1)
        for qb in range(2):
            n = (qb + 1) * P
            cols = slice((1 - qb) * P, 2 * P)
            for h in range(2):
                bank = (k.mb, k.acc)[h]
                dve.wait_ge(k.scored, hp * 4 + (2 * qb + h + 1))
                v.scalar_tensor_tensor(k.s_att[:, h, 0:2, 0:n],
                                       bank[:, 1, :].rearrange("p (g n) -> p g n", g=2)[:, :, 0:n], HD ** -0.5,
                                       mask[:, 0:2, cols], ALU.mult, ALU.add)
                v.scalar_tensor_tensor(k.s_att[:, h, 2, 0:n], bank[:, 2, 0:n], HD ** -0.5, mask[:, 2, cols],
                                       ALU.mult, ALU.add).then_inc(k.masked, 1)
                dve.drain()
                v.tensor_reduce(k.st_att[:, h, 0:1], k.s_att[:, h, :, 0:n], mybir.AxisListType.XY, ALU.max,
                                negate=True).then_inc(k.max_ready, 1)
            for h in range(2):
                dve.wait_ge(k.p_ready, hp * 4 + (2 * qb + h + 1))
                v.reciprocal(k.st_att[:, h, 2:3], k.st_att[:, h, 1:2])
                dve.drain()
                v.tensor_scalar(k.p_att[:, h, :, 0:n], k.p_att[:, h, :, 0:n], k.st_att[:, h, 2:3], None,
                                ALU.mult).then_inc(k.p_norm, 1)
        dve.wait_ge(k.pv_done, hp * 4 + 6)
        v.tensor_copy(tile(k.yb_keep, hp), k.acc[:, 0, 0:SEQ]).then_inc(k.pv_evac, 1)



def pool_shift(k, pool):
    g = k.nc.gpsimd
    with pool.Fori(0, SHIFT_TILES // 2) as i:
        pool.wait_ge(k.pin_ready, i + 1)
        two = bass.ds(i * 2, 2)
        g.tensor_tensor(k.c1[:, 0:2, :], k.p_in[:, two, 0:SEQ], k.p_in[:, two, 1:SEQ + 1], ALU.subtract)
        pool.drain()
        mu = k.vec[:, bass.ds(i * 2 + VEC["mu"][0], 2)].unsqueeze(2).broadcast_to([P, 2, SEQ])
        g.tensor_tensor(k.c1[:, 0:2, :], k.c1[:, 0:2, :], mu, ALU.mult)
        pool.drain()
        g.tensor_tensor(k.p_in[:, two, 1:SEQ + 1], k.p_in[:, two, 1:SEQ + 1], k.c1[:, 0:2, :], ALU.add)
        pool.drain()


def pool_rwkv(k, pool, d):
    g = k.nc.gpsimd
    g.dma_start(k.w2p[:, :], d["w2"]).then_inc(k.lora_loaded, 16)
    g.dma_start(k.a2p[:, :], d["a2"]).then_inc(k.lora_loaded, 16)
    g.dma_start(k.g2[:, :], d["g2"]).then_inc(k.lora_loaded, 16)
    g.memset(k.reset[:, :], 1.0)
    pool.drain()
    g.memset(k.reset[:, 0:SEQ:CHUNK], 0.0).then_inc(k.t_ready, 1)


def pe_pair_sums(k, pe, ready, src, done):
    pe.wait_ge(ready, 1)
    s = src[:, :, :].rearrange("p t n -> p (t n)")
    for b in range(3):
        last = k.nc.tensor.matmul(k.mb[:, b, :], const(k, "pair_ones"), s[:, b * 512:(b + 1) * 512],
                                  start=True, stop=True)
    last.then_inc(done, 1)


def pe_rwkv_prep(k, pe):
    mm = k.nc.tensor.matmul
    x = slice(1, SEQ + 1)
    pe.wait_ge(k.lora_loaded, 48)
    pe.wait_ge(k.wg_ready, 1)
    for c in range(RT):
        b, cols = 2 * (c % 2), slice(c * P, (c + 1) * P)
        if c >= 2:
            pe.wait_ge(k.lora_evac, c - 1)
        mm(k.mb[:, b, 0:SEQ], k.w2p[:, cols], k.p_in[:, T_WA, x], start=True, stop=True)
        mm(k.mb[:, b, SEQ:2 * SEQ], k.a2p[:, cols], k.p_in[:, T_WA, x], start=True, stop=True)
        mm(k.mb[:, b + 1, 0:SEQ], k.g2[:, cols], k.p_in[:, T_G, x], start=True, stop=True).then_inc(k.lora_mm, 1)
    pe.wait_ge(k.lora_evac, RT)
    pe_pair_sums(k, pe, k.kk_sq, k.tmp, k.kk_sum)
    pe.wait_ge(k.kk_root, 1)
    pe_pair_sums(k, pe, k.bon_in, k.c1, k.bon_sum)


def act_rwkv_prep(k, act):
    a = k.nc.scalar.activation
    x = slice(1, SEQ + 1)
    a(k.p_in[0:HD, T_WA, x], k.p_in[0:HD, T_WA, x], ACT.Tanh)
    a(k.p_in[:, T_G, x], k.p_in[:, T_G, x], ACT.Sigmoid).then_inc(k.wg_ready, 1)
    for c in range(RT):
        b = 2 * (c % 2)
        act.wait_ge(k.lora_mm, c + 1)
        a(k.sw[:, c, :], k.mb[:, b, 0:SEQ], ACT.Sigmoid, bias=vec(k, "w0", c))
        a(k.beta[:, c, :], k.mb[:, b, SEQ:2 * SEQ], ACT.Sigmoid, bias=vec(k, "a0", c))
        a(k.gate[:, c, :], k.mb[:, b + 1, 0:SEQ], ACT.Copy).then_inc(k.lora_evac, 1)
    act.wait_ge(k.kk_sum, 1)
    a(k.tmp[:, :, :].rearrange("p t n -> p (t n)").rearrange("p (b n) -> p b n", b=3), k.mb[:, 0:3, :],
      ACT.Sqrt).then_inc(k.kk_root, 1)
    act.wait_ge(k.c_ready, 1)
    a(k.sw[:, :, :], k.sw[:, :, :], ACT.Exp, scale=-DECAY)
    a(k.bon[:, :, :], k.c1[:, :, :], ACT.Exp, scale=DECAY)
    a(k.tmp[:, :, :], k.c1[:, :, :], ACT.Exp, scale=-DECAY).then_inc(k.exp_ready, 1)


def dve_rwkv_prep(k, dve):
    v = k.nc.vector
    x = slice(1, SEQ + 1)
    tt = v.tensor_tensor
    pk, pr, pv = (k.p_in[:, t:t + RT, x] for t in (T_K, T_R, T_V))
    kk, tmp, kap, a, c1, sw = (b[:, :, :] for b in (k.kk, k.tmp, k.kap, k.beta, k.c1, k.sw))
    for t in range(RT):
        v.tensor_scalar(k.kk[:, t, :], k.p_in[:, T_K + t, x], vec(k, "k_k", t), None, ALU.mult)
    dve.drain()
    tt(tmp, kk, kk, ALU.mult).then_inc(k.kk_sq, 1)
    dve.wait_ge(k.lora_evac, RT)
    dve.wait_ge(k.t_ready, 1)
    for t in range(RT):
        v.tensor_tensor_scan(k.c1[:, t, :], k.reset[:, :], k.sw[:, t, :], 0.0, ALU.mult, ALU.add)
    for t in range(RT):
        v.tensor_scalar(k.kap[:, t, :], k.beta[:, t, :], -1.0, vec(k, "k_a", t), ALU.add, ALU.mult)
    dve.drain()
    tt(sw, c1, sw, ALU.subtract)
    for t in range(RT):
        v.scalar_tensor_tensor(k.kap[:, t, :], k.kap[:, t, :], 1.0, k.p_in[:, T_K + t, x], ALU.add, ALU.mult)
    tt(a, a, kk, ALU.mult)
    dve.wait_ge(k.kk_root, 1)
    v.tensor_scalar_max(tmp, tmp, 1e-12)
    dve.drain()
    v.reciprocal(tmp, tmp)
    dve.drain()
    tt(kk, kk, tmp, ALU.mult)
    tt(a, a, tmp, ALU.mult)
    dve.drain().then_inc(k.c_ready, 1)
    dve.wait_ge(k.exp_ready, 1)
    v.tensor_copy(k.pc[:, :, :], k.tmp[:, :, CHUNK - 1:SEQ:CHUNK])
    tt(c1, pr, kap, ALU.mult)
    tt(pk, kk, sw, ALU.mult)
    tt(a, a, k.bon[:, :, :], ALU.mult)
    dve.drain()
    for t in range(RT):
        last = v.tensor_scalar(k.c1[:, t, :], k.c1[:, t, :], vec(k, "r_k", t), None, ALU.mult)
    last.then_inc(k.bon_in, 1)
    tt(kap, kap, k.bon[:, :, :], ALU.mult)
    tt(pr, pr, tmp, ALU.mult)
    dve.drain()
    dve.wait_ge(k.bon_sum, 1)
    for b in range(3):
        tt(k.bon[:, 2 * b:2 * b + 2, :], k.p_in[:, T_V + 2 * b:T_V + 2 * b + 2, x],
           k.mb[:, b, :].rearrange("p (t n) -> p t n", t=2), ALU.mult)
    dve.drain()



STREAMS = (0, 1)


def nth(j, per, idx, s):
    return j * (2 * per) + (2 * idx + s + 1)


def pool_rwkv_zero(k, pool):
    for s in STREAMS:
        for name in ("al_bd", "be_bd", "ka_bd", "v_bd", "x_bd", "xt_bd", "rt_bd", "akt_bd", "w_bd", "u_bd", "m_bd"):
            k.nc.gpsimd.memset(k.m[s][name][:, :, :], 0.0)
        k.nc.gpsimd.memset(k.m[s]["s_bd"][:, :, :], 0.0).then_inc(k.arr_ready, 1)
    pool.drain()


def chunks(a):
    return a.rearrange("p (c t) -> p c t", c=NCH)


def pool_rwkv_pairs(k, pool):
    with pool.Fori(0, RT // 2) as j:
        for s in STREAMS:
            pair = j * 2 + s
            pool.wait_ge(k.y_evac, nth(j, 1, 0, s))
            for h, rows in enumerate(HALVES):
                k.nc.gpsimd.tensor_copy(k.m[s]["al_bd"][rows, :, HALVES[h]],
                                        chunks(tile(k.p_in, pair + T_K, slice(1, SEQ + 1), rows)))
                last = k.nc.gpsimd.tensor_copy(k.m[s]["be_bd"][rows, :, HALVES[h]],
                                               chunks(tile(k.beta, pair, rows=rows)))
            last.then_inc(k.bd_pool, 1)


ROUNDS = 6


def pe_rwkv_pairs(k, pe):
    nc = k.nc
    mm = nc.tensor.matmul
    ident = const(k, "ident")
    half = CHUNK
    banks = (k.mb, k.acc)

    def c_(c, n=P):
        return slice(c * n, (c + 1) * n)
    with pe.Fori(0, RT // 2) as j:
        for s in STREAMS:
            m, bank, pair = k.m[s], banks[s], j * 2 + s
            pe.wait_ge(k.bd_pool, nth(j, 1, 0, s))
            pe.wait_ge(k.bd_act, nth(j, 1, 0, s))
            for c in range(NCH):
                both = k.p_in[:, bass.ds(pair, 2, 6), 1 + c * half:1 + (c + 1) * half]
                mm(bank[:, 0, c_(c)], m["be_bd"][:, c, :], both, start=True, stop=True)
                mm(bank[:, 1, c_(c)], m["ka_bd"][:, c, :], both, start=True, stop=True)
                last = mm(bank[:, 2, c_(c, half)], m["al_bd"][:, c, :], tile(k.beta, pair, c_(c, half)),
                          start=True, stop=True)
            last.then_inc(k.gram, 1)
        for i, name in enumerate(("al_bd", "be_bd", "ka_bd", "v_bd")):
            for s in STREAMS:
                if i == 1:
                    pe.wait_ge(k.gram_evac, nth(j, 1, 0, s))
                for c in range(NCH):
                    last = nc.tensor.transpose(banks[s][:, (3, 0, 1, 2)[i], c_(c)], k.m[s][name][:, c, :], ident)
                last.then_inc(k.tok_mm, 1)
        for s in STREAMS:
            m, bank = k.m[s], banks[s]
            pe.wait_ge(k.tok_evac, nth(j, 1, 0, s))
            pe.wait_ge(k.tok_act, nth(j, 1, 0, s))
            for c in range(NCH):
                last = mm(bank[:, 3, c_(c, half)], m["akt_bd"][:, c, :], m["vt_st"][:, c, :], start=True, stop=True)
            last.then_inc(k.u0_mm, 1)
        for r in range(ROUNDS):
            for s in STREAMS:
                m, bank = k.m[s], banks[s]
                if r == 0:
                    pe.wait_ge(k.xbd_ready, nth(j, 1, 0, s))
                else:
                    pe.wait_ge(k.round_act, nth(j, ROUNDS - 1, r - 1, s))
                    pe.wait_ge(k.round_evac, nth(j, ROUNDS, r - 1, s))
                for c in range(NCH):
                    if r < ROUNDS - 1:
                        mm(bank[:, 0, c_(c, half)], m["xt_bd"][:, c, :], m["x_st"][:, c, :], start=True, stop=True)
                    lo = half if r == ROUNDS - 1 else 0
                    hi = half if r == 0 else P
                    last = mm(bank[:, 1, c * P + lo:c * P + hi], m["x_bd"][:, c, :], m["xr"][:, c, lo:hi],
                              start=True, stop=True)
                last.then_inc(k.round_mm, 1)
        for s in STREAMS:
            m, bank = k.m[s], banks[s]
            pe.wait_ge(k.round_evac, nth(j, ROUNDS, ROUNDS - 1, s))
            pe.wait_ge(k.u0_evac, nth(j, 1, 0, s))
            for c in range(NCH):
                mm(bank[:, 2, c_(c, half)], m["rt_bd"][:, c, :], m["au"][:, c, 0:half], start=True, stop=True)
                last = mm(bank[:, 3, c_(c, half)], m["rt_bd"][:, c, :], m["au"][:, c, half:P], start=True, stop=True)
            last.then_inc(k.wu_mm, 1)
        for s in STREAMS:
            m, bank = k.m[s], banks[s]
            pe.wait_ge(k.wu_evac, nth(j, 1, 0, s))
            pe.wait_ge(k.rt_copied, nth(j, 1, 0, s))
            for c in range(NCH):
                if c < NCH - 1:
                    mm(bank[:, 0, c_(c, half)], m["w_bd"][:, c, :], m["bet_st"][:, c, :], start=True, stop=True)
                    mm(bank[:, 2, c_(c, half)], m["kat_bd"][:, c, :], m["vt_st"][:, c, :], start=True, stop=False)
                    mm(bank[:, 2, c_(c, half)], m["bet_bd"][:, c, :], m["u_st"][:, c, :], start=False, stop=True)
                last = mm(bank[:, 1, c_(c, half)], m["w_bd"][:, c, :], m["qbt"][:, c, :], start=True, stop=True)
            last.then_inc(k.mfn_mm, 1)
        for c in range(2):
            for s in STREAMS:
                m, bank = k.m[s], banks[s]
                if c == 0:
                    pe.wait_ge(k.mfn_evac, nth(j, 1, 0, s))
                pe.wait_ge(k.chain_evac, nth(j, 3, c, s))
                before = m["n_st"][:, 0, :] if c == 0 else m["s_st"][:, :]
                mm(bank[:, 3, 0:half], m["m_bd"][:, c + 1, :], before, start=True, stop=True).then_inc(k.chain_mm, 1)
        for s in STREAMS:
            m, bank = k.m[s], banks[s]
            pe.wait_ge(k.chain_evac, nth(j, 3, 2, s))
            for c in range(NCH):
                out = bank[:, 0, c_(c, half)]
                mm(out, m["u_bd"][:, c, :], m["qbt"][:, c, :], start=True, stop=False)
                last = mm(out, m["vt_bd"][:, c, :], m["qkt"][:, c, :], start=False, stop=c == 0)
                if c > 0:
                    last = mm(out, m["s_bd"][:, c - 1, :], m["f_st"][:, c, :], start=False, stop=True)
            last.then_inc(k.y_mm, 1)


def act_rwkv_pairs(k, act):
    a = k.nc.scalar.activation
    half = CHUNK
    banks = (k.mb, k.acc)

    def blocks(s, bank, n):
        return banks[s][:, bank, 0:NCH * n].rearrange("p (c n) -> p c n", c=NCH)

    def bd(s, name, src):
        for h, rows in enumerate(HALVES):
            r = a(k.m[s][name][rows, :, HALVES[h]], src[rows, :, 0:half], ACT.Copy)
        return r

    def st(dst, src, scale=1.0):
        for h, rows in enumerate(HALVES):
            r = a(dst[rows], src[rows, :, HALVES[h]], ACT.Copy, scale=scale)
        return r
    act.wait_ge(k.arr_ready, 2)
    with act.Fori(0, RT // 2) as j:
        for s in STREAMS:
            m, pair = k.m[s], j * 2 + s
            act.wait_ge(k.y_evac, nth(j, 1, 0, s))
            for h, rows in enumerate(HALVES):
                a(m["ka_bd"][rows, :, HALVES[h]], chunks(tile(k.kap, pair, rows=rows)), ACT.Copy)
                last = a(m["v_bd"][rows, :, HALVES[h]], chunks(tile(k.p_in, pair + T_V, slice(1, SEQ + 1), rows)),
                         ACT.Copy)
            last.then_inc(k.bd_act, 1)
        for s in STREAMS:
            m = k.m[s]
            act.wait_ge(k.tok_mm, nth(j, 4, 0, s))
            st(m["au"][:, :, 0:half], blocks(s, 3, P), scale=-1.0)
            act.wait_ge(k.gram_evac, nth(j, 1, 0, s))
            bd(s, "x_bd", m["x_st"])
            bd(s, "xt_bd", m["xr"]).then_inc(k.xbd_ready, 1)
        for s in STREAMS:
            m = k.m[s]
            act.wait_ge(k.tok_mm, nth(j, 4, 1, s))
            a(m["bet_bd"][:, :, :], blocks(s, 0, P), ACT.Copy)
            st(m["bet_st"][:, :, :], blocks(s, 0, P)).then_inc(k.tok_act, 1)
        for r in range(ROUNDS - 1):
            for s in STREAMS:
                act.wait_ge(k.round_mm, nth(j, ROUNDS, r, s))
                if r < ROUNDS - 2:
                    a(k.m[s]["x_st"][:, :, :], blocks(s, 0, half), ACT.Copy)
                bd(s, "x_bd", blocks(s, 0, half)).then_inc(k.round_act, 1)
        for s in STREAMS:
            act.wait_ge(k.wu_mm, nth(j, 1, 0, s))
            bd(s, "w_bd", blocks(s, 2, half)).then_inc(k.wu_evac, 1)
        for s in STREAMS:
            pair = j * 2 + s
            act.wait_ge(k.mfn_mm, nth(j, 1, 0, s))
            for c in range(NCH - 1):
                last = a(k.m[s]["n_st"][:, c, :], banks[s][:, 2, c * half:(c + 1) * half], ACT.Copy,
                         scale=k.pc[:, bass.ds(pair, 1), c:c + 1].rearrange("p a n -> p (a n)"))
            last.then_inc(k.mfn_evac, 1)


def dve_rwkv_pairs(k, dve):
    v = k.nc.vector
    half = CHUNK
    banks = (k.mb, k.acc)
    ui, us, ls, i2 = (const(k, n) for n in ("up_incl", "up_strict", "lo_strict", "i2"))
    stt, tt = v.scalar_tensor_tensor, v.tensor_tensor

    def blocks(s, bank, n):
        return banks[s][:, bank, 0:NCH * n].rearrange("p (c n) -> p c n", c=NCH)

    def st(dst, src):
        for h, rows in enumerate(HALVES):
            r = v.tensor_copy(dst[rows], src[rows, :, HALVES[h]])
        return r
    dve.wait_ge(k.arr_ready, 2)
    with dve.Fori(0, RT // 2) as j:
        for s in STREAMS:
            m = k.m[s]
            dve.wait_ge(k.gram, nth(j, 1, 0, s))
            stt(m["xr"][:, :, 0:half], blocks(s, 0, P)[:, :, half:P], -1.0, over(us, NCH), ALU.mult, ALU.mult)
            stt(m["x_st"][:, :, :], blocks(s, 2, half), -1.0, over(ls, NCH), ALU.mult, ALU.mult)
            tt(m["qbt"][:, :, :], blocks(s, 0, P)[:, :, 0:half], over(ui, NCH), ALU.mult)
            tt(m["qkt"][:, :, :], blocks(s, 1, P)[:, :, 0:half], over(ui, NCH), ALU.mult)
            for h, rows in enumerate(HALVES):
                last = tt(m["akt_bd"][rows, :, HALVES[h]], blocks(s, 1, P)[rows, :, half:P], over(us[rows], NCH),
                          ALU.mult)
            last.then_inc(k.gram_evac, 1)
        dve.drain()
        for s in STREAMS:
            m = k.m[s]
            tt(m["xr"][:, :, half:P], m["xr"][:, :, 0:half], over(i2, NCH), ALU.add)
        for s in STREAMS:
            m = k.m[s]
            dve.wait_ge(k.tok_mm, nth(j, 4, 3, s))
            st(m["vt_st"][:, :, :], blocks(s, 2, P))
            v.tensor_copy(m["kat_bd"][:, :, :], blocks(s, 1, P))
            v.tensor_copy(m["vt_bd"][:, :, :], blocks(s, 2, P)).then_inc(k.tok_evac, 1)
        for s in STREAMS:
            dve.wait_ge(k.u0_mm, nth(j, 1, 0, s))
            v.tensor_scalar(k.m[s]["au"][:, :, half:P], blocks(s, 3, half), -1.0, None,
                            ALU.mult).then_inc(k.u0_evac, 1)
        for r in range(ROUNDS):
            for s in STREAMS:
                m = k.m[s]
                dve.wait_ge(k.round_mm, nth(j, ROUNDS, r, s))
                src = blocks(s, 1, P)
                if r < ROUNDS - 1:
                    if r < ROUNDS - 2:
                        v.tensor_copy(m["xr"][:, :, 0:half], src[:, :, 0:half])
                        for h, rows in enumerate(HALVES):
                            last = v.tensor_copy(m["xt_bd"][rows, :, HALVES[h]], src[rows, :, 0:half])
                    if r > 0:
                        last = tt(m["xr"][:, :, half:P], m["xr"][:, :, half:P], src[:, :, half:P], ALU.add)
                else:
                    for h, rows in enumerate(HALVES):
                        last = tt(m["rt_bd"][rows, :, HALVES[h]], m["xr"][rows, :, half:P], src[rows, :, half:P],
                                  ALU.add)
                last.then_inc(k.round_evac, 1)
            dve.drain()
        for s in STREAMS:
            m = k.m[s]
            dve.wait_ge(k.wu_mm, nth(j, 1, 0, s))
            v.tensor_copy(m["u_st"][:, :, :], blocks(s, 3, half))
            for h, rows in enumerate(HALVES):
                last = v.tensor_copy(m["u_bd"][rows, :, HALVES[h]], blocks(s, 3, half)[rows])
            last.then_inc(k.rt_copied, 1)
        for s in STREAMS:
            m, pair = k.m[s], j * 2 + s
            dve.wait_ge(k.mfn_mm, nth(j, 1, 0, s))
            for h, rows in enumerate(HALVES):
                tt(m["m_bd"][rows, 0:NCH - 1, HALVES[h]], blocks(s, 0, half)[rows, 0:NCH - 1],
                   over(i2[rows], NCH - 1), ALU.add)
            tt(m["f_st"][:, :, :], blocks(s, 1, half), chunks(tile(k.p_in, pair + T_R, slice(1, SEQ + 1))),
               ALU.add).then_inc(k.chain_evac, 1)

        def state(s, c, src):
            for h, rows in enumerate(HALVES):
                r = v.tensor_copy(k.m[s]["s_bd"][rows, c, HALVES[h]], src[rows])
            return r
        for s in STREAMS:
            dve.wait_ge(k.mfn_evac, nth(j, 1, 0, s))
            state(s, 0, k.m[s]["n_st"][:, 0, :])
        for c in (1, 2):
            for s in STREAMS:
                m, pair = k.m[s], j * 2 + s
                dve.wait_ge(k.chain_mm, nth(j, 2, c - 1, s))
                stt(m["s_st"][:, :], banks[s][:, 3, 0:half],
                    k.pc[:, bass.ds(pair, 1), c:c + 1].rearrange("p a n -> p (a n)"), m["n_st"][:, c, :],
                    ALU.mult, ALU.add)
            dve.drain()
            for s in STREAMS:
                state(s, c, k.m[s]["s_st"][:, :]).then_inc(k.chain_evac, 1)
        for s in STREAMS:
            dve.wait_ge(k.y_mm, nth(j, 1, 0, s))
            v.tensor_copy(tile(k.c1, j * 2 + s), banks[s][:, 0, 0:SEQ]).then_inc(k.y_evac, 1)


def pe_rwkv_out(k, pe):
    pe_pair_sums(k, pe, k.gn_in, k.c1, k.gn_sum)
    pe_pair_sums(k, pe, k.gn_sq, k.tmp, k.gn_sum)


def act_rwkv_out(k, act):
    a = k.nc.scalar.activation
    act.wait_ge(k.gn_sum, 2)
    a(k.tmp[:, :, :].rearrange("p t n -> p (t n)").rearrange("p (b n) -> p b n", b=3), k.mb[:, 0:3, :], ACT.Sqrt,
      bias=k.eps[:, 1:2], scale=1.0 / HD).then_inc(k.gn_root, 1)
    act.wait_ge(k.gn_root, 2)
    a(k.y1_hi[:, 0:RT, :], k.c1[:, :, :], ACT.Copy)
    a(k.y1_hi[:, RT:KT, :], k.yb_keep[:, :, :], ACT.Copy).then_inc(k.gn_root, 1)


def dve_rwkv_out(k, dve):
    v = k.nc.vector
    tt = v.tensor_tensor
    c1 = k.c1[:, :, :]
    v.drain().then_inc(k.gn_in, 1)
    dve.wait_ge(k.gn_sum, 1)
    flat3 = c1.rearrange("p t n -> p (t n)").rearrange("p (b n) -> p b n", b=3)
    v.scalar_tensor_tensor(flat3, k.mb[:, 0:3, :], -1.0 / HD, flat3, ALU.mult, ALU.add)
    dve.drain()
    tt(k.tmp[:, :, :], c1, c1, ALU.mult).then_inc(k.gn_sq, 1)
    dve.wait_ge(k.gn_root, 1)
    v.reciprocal(k.tmp[:, :, :], k.tmp[:, :, :])
    dve.drain()
    tt(c1, c1, k.tmp[:, :, :], ALU.mult)
    dve.drain()
    for t in range(RT):
        v.tensor_scalar(k.c1[:, t, :], k.c1[:, t, :], vec(k, "lnx_w", t), vec(k, "lnx_b", t), ALU.mult, ALU.add)
    dve.drain()
    tt(c1, c1, k.bon[:, :, :], ALU.add)
    dve.drain()
    tt(c1, c1, k.gate[:, :, :], ALU.mult)
    dve.drain().then_inc(k.gn_root, 1)
    dve.wait_ge(k.gn_root, 3)
    tt(k.y1_lo[:, 0:RT, :], c1, k.y1_hi[:, 0:RT, :].bitcast(F32), ALU.subtract)
    tt(k.y1_lo[:, RT:KT, :], k.yb_keep[:, :, :], k.y1_hi[:, RT:KT, :].bitcast(F32), ALU.subtract)
    dve.drain()



FF_ROWS = slice(32, 40)


def pe_gates2(k, pe, l):
    pe.wait_ge(k.dec_in, l * 16 + 16)
    for t in range(2):
        last = k.nc.tensor.matmul(k.mb[:, t, 0:TOK], k.wal[:, t * P:(t + 1) * P], k.small[:, :], start=True, stop=True)
    last.then_inc(k.dec_mm, 1)


def act_gates2(k, act, l):
    a = k.nc.scalar.activation
    b_f = vec(k, "b_f", layer=l, rows=FF_ROWS)
    a(k.lf[0:8, :], k.small[FF_ROWS, :], ACT.Abs, bias=b_f)
    act.wait_ge(k.dec_mm, l + 1)
    for t in range(2):
        a(k.e1[:, t, :], k.mb[:, t, 0:TOK], ACT.Abs, bias=vec(k, "b_alpha", t, l))
    act.drain().then_inc(k.dec_abs, 1)
    a(k.lf[0:8, :], k.lf[0:8, :], ACT.Exp, scale=-1.0)
    a(k.e1[:, :, :], k.e1[:, :, :], ACT.Exp, scale=-1.0)
    act.drain()
    a(k.lf[0:8, :], k.lf[0:8, :], ACT.Ln, bias=1.0)
    a(k.e1[:, :, :], k.e1[:, :, :], ACT.Ln, bias=1.0).then_inc(k.dec_exp, 1)
    act.wait_ge(k.gz_ready, l + 1)
    s = 1.0 / 16.0
    a(k.e1[:, :, :], k.e2[:, :, :], ACT.Exp, scale=s)
    a(k.gst[:, :, :, :], k.gst[:, :, :, :], ACT.Exp, scale=s)
    act.drain()
    a(k.e2[:, :, :], k.e2[:, :, :], ACT.Exp, scale=-s).then_inc(k.gexp_ready, 1)
    a(k.p2[:, T_GA:T_GA + 16, :], k.p2[:, T_GA:T_GA + 16, :], ACT.Sigmoid)


def dve_gates2(k, dve, l):
    v = k.nc.vector
    v.tensor_scalar(k.cum[0:8, :], k.small[FF_ROWS, :], vec(k, "b_f", layer=l, rows=FF_ROWS), 0.0, ALU.add, ALU.min)
    dve.wait_ge(k.dec_abs, l + 1)
    for t in range(2):
        v.tensor_scalar(k.gcum[:, t, :], k.mb[:, t, 0:TOK], vec(k, "b_alpha", t, l), 0.0, ALU.add, ALU.min)
    dve.drain()
    dve.wait_ge(k.dec_exp, l + 1)
    v.tensor_tensor(k.lf[0:8, :], k.cum[0:8, :], k.lf[0:8, :], ALU.subtract)
    v.tensor_tensor(k.e1[:, :, :], k.gcum[:, :, :], k.e1[:, :, :], ALU.subtract)
    v.memset(k.e2[:, :, :], 1.0)
    dve.drain()
    v.tensor_tensor_scan(k.cum[0:8, :], k.e2[0:8, 0, :], k.lf[0:8, :], 0.0, ALU.mult, ALU.add)
    dve.drain()
    v.memset(k.e2[:, :, 0:TOK:GLA_C], 0.0)
    dve.drain()
    for t in range(2):
        v.tensor_tensor_scan(k.gcum[:, t, :], k.e2[:, t, :], k.e1[:, t, :], 0.0, ALU.mult, ALU.add)
    eye = const(k, "eye8", slice(0, 8))
    v.memset(k.minus8[:, :], -float(HD) ** 0.5)
    dve.drain()
    v.tensor_tensor(k.cumz[:, :, :], over(k.cum[0:8, :], 8), eye.unsqueeze(2).broadcast_to([8, 8, TOK]), ALU.mult)
    for t in range(2):
        g = k.gcum[:, t, :].rearrange("p (n c) -> p n c", n=GLA_N)
        mid = g[:, :, GLA_C // 2:GLA_C // 2 + 1]
        v.tensor_tensor(k.e2[:, t, :].rearrange("p (n c) -> p n c", n=GLA_N), g,
                        mid.broadcast_to([P, GLA_N, GLA_C]), ALU.subtract)
        v.tensor_copy(k.gst[:, t, 0, :], mid.rearrange("p n c -> p (n c)"))
        v.tensor_copy(k.gst[:, t, 1, :], g[:, :, GLA_C - 1:GLA_C].rearrange("p n c -> p (n c)"))
        v.tensor_tensor(k.gst[:, t, 2, :], g[:, :, GLA_C - 1:GLA_C].rearrange("p n c -> p (n c)"),
                        mid.rearrange("p n c -> p (n c)"), ALU.subtract)
    dve.drain()
    v.tensor_scalar(k.e2[:, :, :], k.e2[:, :, :], 80.0 * 16, -80.0 * 16, ALU.min, ALU.max).then_inc(k.gz_ready, 1)
    dve.wait_ge(k.gexp_ready, l + 1)
    q, kk = k.p2[:, T_GQ:T_GQ + 2, :], k.p2[:, T_GK:T_GK + 2, :]
    v.scalar_tensor_tensor(q, q, HD ** -0.5, k.e1[:, :, :], ALU.mult, ALU.mult)
    v.tensor_tensor(kk, kk, k.e2[:, :, :], ALU.mult)





def pool_fox(k, pool):
    k.nc.gpsimd.memset(k.fkz[:, :, :], 0.0)
    k.nc.gpsimd.memset(k.fvz[:, :, :, :], 0.0)
    k.nc.gpsimd.memset(k.fvs[:, :], 0.0)
    pool.drain()


def pe_fox(k, pe, l):
    nc = k.nc
    ident = const(k, "ident")
    with pe.Fori(0, FOX_PAIRS) as i:
        it = l * FOX_PAIRS + i
        pe.wait_ge(k.fox_copy, it + 1)
        settle(k, pe)
        for b, (lo, hi) in enumerate(BLOCKS):
            last = nc.tensor.transpose(k.mb[0:hi - lo, 3, b * P:(b + 1) * P], k.fvs[:, lo:hi], ident)
        last.then_inc(k.fox_tok, 1)

        def scores(b):
            lo, hi = BLOCKS[b]
            for h in range(2):
                pe.wait_ge(k.fox_masked, it * 6 + (2 * b + h + 1))
                out = k.mb[:, h, 0:hi]
                nc.tensor.matmul(out, k.fqs[:, lo:lo + P], k.fkz[:, h, 0:hi], start=True, stop=False)
                nc.tensor.matmul(out, k.minus8[:, :],
                                 k.cumz[:, bass.ds(i * 2 + h, 1), 0:hi].rearrange("p a n -> p (a n)"),
                                 start=False, stop=True).then_inc(k.fox_sc, 1)
        scores(0)
        for b, (lo, hi) in enumerate(BLOCKS):
            n = hi - lo
            for h in range(2):
                pe.wait_ge(k.fox_norm, it * 6 + (2 * b + h + 1))
                settle(k, pe)
                tr = (k.mb[:, 2, :], k.acc[:, 2, :])[h]
                for c in range(b + 1):
                    clo, chi = BLOCKS[c]
                    last = nc.tensor.transpose(tr[0:chi - clo, c * P:c * P + n], k.fp[0:n, h, clo:chi],
                                               ident[0:n, 0:n])
                last.then_inc(k.fox_tr, 1)
            if b + 1 < len(BLOCKS):
                scores(b + 1)
            pe.wait_ge(k.fox_tok_evac, it + 1)
            for h in range(2):
                pe.wait_ge(k.fox_pt, it * 6 + (2 * b + h + 1))
                settle(k, pe)
                for c in range(b + 1):
                    clo, chi = BLOCKS[c]
                    last = nc.tensor.matmul(k.acc[:, 0, lo:hi], k.fvz[0:chi - clo, c, h, :],
                                            k.fpt[0:chi - clo, h, c, 0:n],
                                            start=(h == 0 and c == 0), stop=(h == 1 and c == b))
                last.then_inc(k.fox_pv, 1)


def act_fox(k, act, l):
    a = k.nc.scalar.activation
    with act.Fori(0, FOX_PAIRS) as i:
        it = l * FOX_PAIRS + i
        act.wait_ge(k.fox_y, it + 1)
        a(k.fqs[:, :], tile(k.p2, i + T_FQ), ACT.Copy)
        for h, rows in enumerate(HALVES):
            a(k.fkz[rows, h, :], tile(k.p2, i + T_FK, rows=rows), ACT.Copy)
        a(k.fvs[:, :], tile(k.p2, i + T_FV), ACT.Copy).then_inc(k.fox_copy, 1)
        act.wait_ge(k.fox_tok, it + 1)
        for c, (lo, hi) in enumerate(BLOCKS):
            for h in range(2):
                last = a(k.fvz[0:hi - lo, c, h, HALVES[h]],
                         k.mb[0:hi - lo, 3, c * P + h * HD:c * P + (h + 1) * HD], ACT.Copy)
        last.then_inc(k.fox_tok_evac, 1)
        for b, (lo, hi) in enumerate(BLOCKS):
            n = hi - lo
            for h in range(2):
                act.wait_ge(k.max_ready, 8 + it * 6 + (2 * b + h + 1))
                act.wait_ge(k.fox_tr, it * 6 + (2 * b + h + 1))
                a(k.fp[0:n, h, 0:hi], k.fs[0:n, h, 0:hi], ACT.Exp, bias=k.fstat[0:n, h, 0:1],
                  accum_out=k.fstat[0:n, h, 1:2]).then_inc(k.fox_p, 1)
            for h in range(2):
                act.wait_ge(k.fox_tr, it * 6 + (2 * b + h + 3))
                act.wait_ge(k.fox_pv, it * 6 + (2 * b + h + 1))
                tr = (k.mb[:, 2, :], k.acc[:, 2, :])[h]
                for c in range(b + 1):
                    clo, chi = BLOCKS[c]
                    last = a(k.fpt[0:chi - clo, h, c, 0:n], tr[0:chi - clo, c * P:c * P + n], ACT.Copy)
                last.then_inc(k.fox_pt, 1)
        act.wait_ge(k.t_ready, 1 + it + 1)
        a(tile(k.y_hi, i), k.fy[:, :], ACT.Copy).then_inc(k.y_ready, 1)


def dve_fox(k, dve, l):
    v = k.nc.vector
    mask = const(k, "mask_fox")
    with dve.Fori(0, FOX_PAIRS) as i:
        it = l * FOX_PAIRS + i
        for b, (lo, hi) in enumerate(BLOCKS):
            n = hi - lo
            at = (TOK - P) - lo
            for h in range(2):
                dve.wait_ge(k.fox_sc, it * 6 + (2 * b + h + 1))
                v.scalar_tensor_tensor(k.fs[0:n, h, 0:hi], k.mb[0:n, h, 0:hi], HD ** -0.5, mask[0:n, at:at + hi],
                                       ALU.mult, ALU.add).then_inc(k.fox_masked, 1)
                dve.drain()
                v.tensor_reduce(k.fstat[0:n, h, 0:1], k.fs[0:n, h, 0:hi], AX, ALU.max,
                                negate=True).then_inc(k.max_ready, 1)
            for h in range(2):
                dve.wait_ge(k.fox_p, it * 6 + (2 * b + h + 1))
                v.reciprocal(k.fstat[0:n, h, 2:3], k.fstat[0:n, h, 1:2])
                dve.drain()
                v.tensor_scalar(k.fp[0:n, h, 0:hi], k.fp[0:n, h, 0:hi], k.fstat[0:n, h, 2:3], None,
                                ALU.mult).then_inc(k.fox_norm, 1)
        dve.wait_ge(k.fox_pv, it * 6 + 8)
        v.tensor_copy(k.fy[:, :], k.acc[:, 0, 0:TOK]).then_inc(k.t_ready, 1)
        dve.drain()
        dve.wait_ge(k.y_ready, it + 1)
        v.tensor_tensor(tile(k.y_lo, i), k.fy[:, :], tile(k.y_hi, i).bitcast(F32), ALU.subtract).then_inc(k.fox_y, 1)



def pool_gla(k, pool):
    k.nc.gpsimd.memset(k.gkz[:, :, :], 0.0)
    k.nc.gpsimd.memset(k.gsm[:, :, :, :], 0.0).then_inc(k.gla_zero, 1)


def pe_gla(k, pe, l):
    nc = k.nc
    mm = nc.tensor.matmul
    ident = const(k, "ident")
    with pe.Fori(0, 2) as i:
        it = l * 2 + i
        pe.wait_ge(k.gla_copy, it + 1)
        for n in range(GLA_N):
            c = slice(n * GLA_C, (n + 1) * GLA_C)
            nc.tensor.transpose(k.mb[0:GLA_C, 2, n * P:(n + 1) * P], k.gks[:, c], ident)
            for h in range(2):
                last = nc.tensor.transpose(k.mb[0:GLA_C, h, n * P:(n + 1) * P], k.gvs[:, h, c], ident)
        last.then_inc(k.gla_tok, 1)
        for h in range(2):
            for n in range(GLA_N):
                c = slice(n * GLA_C, (n + 1) * GLA_C)
                last = mm(k.acc[0:GLA_C, h, c], k.gkz[:, h, c], tile(k.p2, i + T_GQ, c), start=True, stop=True)
        last.then_inc(k.gla_att, 1)
        pe.wait_ge(k.gla_tok_evac, it + 1)
        for h in range(2):
            for n in range(GLA_N - 1):
                last = mm(k.mb[:, 2 + h, n * P:(n + 1) * P], k.gkt[:, n, :], k.gvt[:, n, h, :], start=True, stop=True)
        last.then_inc(k.gla_state, 1)
        pe.wait_ge(k.gla_att_evac, it + 1)
        pe.wait_ge(k.gla_state_evac, it + 1)
        for h in range(2):
            for n in range(GLA_N):
                c = slice(n * GLA_C, (n + 1) * GLA_C)
                last = mm(k.mb[:, h, c], k.gvt[:, n, h, :], k.gat[:, n, h, :], start=True, stop=n == 0)
                if n > 0:
                    last = mm(k.mb[:, h, c], k.gsm[:, n - 1, h, :], tile(k.p2, i + T_GQ, c), start=False, stop=True)
        last.then_inc(k.gla_o, 1)
        pe.wait_ge(k.gla_sq, it + 1)
        for h in range(2):
            last = mm(k.acc[:, h, 0:TOK], k.mean_ones[:, :], k.gsq[:, h, :], start=True, stop=True)
        last.then_inc(k.gla_mean, 1)


def act_gla(k, act, l):
    a = k.nc.scalar.activation
    act.wait_ge(k.gla_zero, l + 1)
    settle(k, act)
    with act.Fori(0, 2) as i:
        it = l * 2 + i
        act.wait_ge(k.gla_y, it + 1)
        for h, rows in enumerate(HALVES):
            a(k.gkz[rows, h, :], tile(k.p2, i + T_GK, rows=rows), ACT.Copy)
        a(k.gks[:, :], tile(k.p2, i + T_GK), ACT.Copy)
        a(k.gvs[:, :, :], k.p2[:, bass.ds(i * 2 + T_GV, 2), :], ACT.Copy).then_inc(k.gla_copy, 1)
        act.wait_ge(k.gla_tok, it + 1)
        for h in range(2):
            a(k.gvt[:, :, h, :], k.mb[0:GLA_C, h, :].rearrange("p (n c) -> p n c", n=GLA_N), ACT.Copy)
        a(k.gkt[:, :, :], k.mb[0:GLA_C, 2, :].rearrange("p (n c) -> p n c", n=GLA_N),
          ACT.Copy).then_inc(k.gla_tok_evac, 1)
        a(k.gr_[:, :, :], k.p2[:, bass.ds(i * 2 + T_GR, 2), :], ACT.Sigmoid)
        act.wait_ge(k.gla_o, it + 1)
        for h in range(2):
            a(k.go[:, h, :], k.mb[:, h, 0:TOK], ACT.Copy)
            last = a(k.gsq[:, h, :], k.mb[:, h, 0:TOK], ACT.Square)
        last.then_inc(k.gla_sq, 1)
        act.wait_ge(k.gla_mean, it + 1)
        for h in range(2):
            last = a(k.gsq[:, h, :], k.acc[:, h, 0:TOK], ACT.Sqrt, bias=k.eps[:, 0:1], scale=float(D) / P)
        last.then_inc(k.gla_root, 1)
        for h in range(2):
            act.wait_ge(k.wh_y, it * 2 + (h + 1))
            a(tile(k.y_hi, i * 2 + (4 + h)), k.go[:, h, :], ACT.Copy).then_inc(k.gyh_ready, 1)


def dve_gla(k, dve, l):
    v = k.nc.vector
    gm = const(k, "gla_mask", slice(0, GLA_C))
    dve.wait_ge(k.gla_zero, l + 1)
    settle(k, dve)
    with dve.Fori(0, 2) as i:
        it = l * 2 + i
        dve.wait_ge(k.gla_att, it + 1)
        for h in range(2):
            last = v.tensor_tensor(k.gat[:, :, h, :], k.acc[0:GLA_C, h, 0:TOK].rearrange("p (n c) -> p n c", n=GLA_N),
                                   over(gm, GLA_N), ALU.mult)
        last.then_inc(k.gla_att_evac, 1)
        dve.wait_ge(k.gla_state, it + 1)

        def factor(which, n, rows):
            g = k.gst[rows, bass.ds(i, 1), which, n:n + 1]
            return g.rearrange("p a n -> p (a n)")
        for h, rows in enumerate(HALVES):
            s = k.gs[rows, :]
            for n in range(GLA_N - 1):
                add = k.mb[rows, 2 + h, n * P:(n + 1) * P]
                if n > 0:
                    v.tensor_scalar(s, s, factor(1, n, rows), None, ALU.mult)
                    dve.drain()
                    v.scalar_tensor_tensor(s, add, factor(2, n, rows), s, ALU.mult, ALU.add)
                else:
                    v.tensor_scalar(s, add, factor(2, n, rows), None, ALU.mult)
                dve.drain()
                last = v.tensor_scalar(k.gsm[rows, n, h, :], s, factor(0, n + 1, rows), None, ALU.mult)
        last.then_inc(k.gla_state_evac, 1)
        dve.wait_ge(k.gla_root, it + 1)
        v.reciprocal(k.gsq[:, :, :], k.gsq[:, :, :])
        v.tensor_tensor(k.gr_[:, :, :], k.gr_[:, :, :], k.p2[:, bass.ds(i * 2 + T_GR, 2), :], ALU.mult)
        dve.drain()
        for h in range(2):
            g = k.vec[:, bass.ds(l * VEC_LAYER + i * 2 + (VEC["g_gla"][0] + h), 1)]
            v.scalar_tensor_tensor(k.go[:, h, :], k.go[:, h, :], g, k.gsq[:, h, :], ALU.mult, ALU.mult)
        dve.drain()
        for h in range(2):
            v.tensor_tensor(k.go[:, h, :], k.go[:, h, :], k.gr_[:, h, :], ALU.mult).then_inc(k.wh_y, 1)
        for h in range(2):
            t = i * 2 + (4 + h)
            dve.drain()
            dve.wait_ge(k.gyh_ready, it * 2 + (h + 1))
            last = v.tensor_tensor(tile(k.y_lo, t), k.go[:, h, :], tile(k.y_hi, t).bitcast(F32), ALU.subtract)
        last.then_inc(k.gla_y, 1)



W1 = slice(META, TOK)
W2 = slice(0, TOK)


def program_tensor(k, pe):
    pe.sem_inc(k.ada_done, 2)
    pe.sem_inc(k.panel_done, 2)
    pe.sem_inc(k.p_tr, 2)
    pe.sem_inc(k.pv_done, 2)
    pe.sem_inc(k.fox_tr, 2)
    pe.sem_inc(k.fox_pv, 2)
    pe.wait_ge(k.const_ready, 1)
    pe.wait_ge(k.vec_loaded, 32)
    pe_stat(k, pe, 0, W1)
    with pe.Fori(0, ADA_FIRST // 2) as i:
        for b in range(2):
            pe_ada(k, pe, i * 2 + b, b)
    pe_h_ready(k, pe, 0)
    pe_project(k, pe, 0, ADA_LAST, 2, W1, ada=True)
    pe_project(k, pe, ADA_LAST, IN1 - ADA_LAST, 2, W1)
    stage_end(k, pe, 1)
    pe_att(k, pe)
    stage_end(k, pe, 2)
    pe_rwkv_prep(k, pe)
    stage_end(k, pe, 3)
    pe_rwkv_pairs(k, pe)
    pe_rwkv_out(k, pe)
    stage_end(k, pe, 4)
    pe_branches(k, pe, M_AB1, SEQ, k.y1_hi, k.y1_lo, RT)
    pe.wait_ge(k.yl_ready, KT)
    pe_project(k, pe, M_OUT1, OUT, 2, W1)
    pe_stat(k, pe, 1, W1)
    pe_pre(k, pe, 1, W1)
    pe_ffn(k, pe, 0, M_GU1, M_DOWN1, 1, W1)
    with pe.Fori(0, LAYERS) as l:
        loop = l * (L_PANELS // 2)
        pe_pre(k, pe, l * 3 + 2, W2)
        pe_ffn(k, pe, l * 2 + 1, M_LAYER + L_GUA, M_LAYER + L_DOWNA, l * 3 + 2, W2, loop)
        pe_pre(k, pe, l * 3 + 3, W2)
        pe_project(k, pe, M_LAYER + L_SINGLE, SINGLES, 1, W2, loop)
        pe_project(k, pe, M_LAYER + L_IN, IN2, 2, W2, loop)
        stage_end(k, pe, l * 4 + 5)
        pe_gates2(k, pe, l)
        stage_end(k, pe, l * 4 + 6)
        pe_fox(k, pe, l)
        stage_end(k, pe, l * 4 + 7)
        pe_gla(k, pe, l)
        stage_end(k, pe, l * 4 + 8)
        pe_branches(k, pe, M_LAYER + L_AB, TOK, k.y_hi, k.y_lo, 4, loop)
        pe.wait_ge(k.yl_ready, l * KT + 2 * KT)
        settle(k, pe)
        pe_project(k, pe, M_LAYER + L_OUT, OUT, 2, W2, loop)
        pe_stat(k, pe, l * 6 + 7, W2)
        pe_pre(k, pe, l * 3 + 4, W2)
        pe_ffn(k, pe, l * 2 + 2, M_LAYER + L_GUB, M_LAYER + L_DOWNB, l * 3 + 4, W2, loop)


def prologue(fn, k, eng, start, size, loop=0):
    for b in range(2):
        fn(k, eng, Panel.of(start + b, loop), size)


def program_scalar(k, act, d):
    nc = k.nc
    act.dma_start(k.const[:, :], d["const"]).then_inc(k.vec_loaded, 16)
    act.dma_start(k.x[:, :, W1], d["x"]).then_inc(k.x_loaded, 16)
    act.dma_start(k.x[:, :, 0:META], d["meta"]).then_inc(k.x_loaded, 16)
    act.wait_ge(k.vec_loaded, 32)
    nc.scalar.activation(k.csil[:, :], vec(k, "c", n=KT), ACT.Sigmoid).then_inc(k.csig, 1)
    act.wait_ge(k.const_ready, 1)
    act.wait_ge(k.x_loaded, 32)
    act_pre_sums(k, act, 0, W1)
    prologue(split_hi, k, act, 0, IN_K)
    act_pre_split(k, act, 0, W1, lambda t: k.mod[:, t:t + 1])
    act.wait_ge(k.const_ready, 2)
    act_copy_out(k, act, 0, 10, 2, lambda i: k.p_in[:, bass.ds(i * 2, 2), 1:SEQ + 1], SEQ, IN_K, (IN_K, IN_K),
                 signal=k.pin_ready)
    act_copy_out(k, act, 10, 9, 2, lambda i: k.qkv[:, bass.ds(i * 2, 2), :], SEQ, IN_K, (IN_K, IN_K))
    act_copy_out(k, act, 19, 8, 2, lambda i: k.gates[:, bass.ds(i * 2, 2), :], SEQ, IN_K, (None, None))
    stage_end(k, act, 1)
    act_att(k, act)
    stage_end(k, act, 2)
    act_rwkv_prep(k, act)
    nc.scalar.activation(k.gates[:, :, :], k.gates[:, :, :], ACT.Sigmoid)
    stage_end(k, act, 3)
    act_rwkv_pairs(k, act)
    act_rwkv_out(k, act)
    stage_end(k, act, 4)
    prologue(split_hi, k, act, M_AB1, AB_K)
    act_merge(k, act, 0, M_AB1, SEQ, W1, (OUT_K, OUT_K))
    act_products(k, act, 0, M_OUT1, 2, W1, OUT_K, (GU_K, GU_K))
    act_root(k, act, 1, W1)
    act_pre(k, act, 1, W1, lambda t: k.mod[:, 24 + t:25 + t], updates=0)
    act_ffn(k, act, 0, M_GU1, M_DOWN1, 1, W1, (None, None))
    with act.Fori(0, LAYERS) as l:
        loop = l * (L_PANELS // 2)
        prologue(split_hi, k, act, M_LAYER, GU_K, loop)
        act_pre(k, act, l * 3 + 2, W2, updates=l * 3 + 1)
        act_ffn(k, act, l * 2 + 1, M_LAYER + L_GUA, M_LAYER + L_DOWNA, l * 3 + 2, W2, (AB_K, AB_K), loop)
        act_pre(k, act, l * 3 + 3, W2, updates=l * 3 + 2)
        act_ahead_only(k, act, M_LAYER + L_SINGLE, SINGLES, AB_K, (IN_K, IN_K), loop)
        act_ahead_only(k, act, M_LAYER + L_IN, IN2, IN_K, (AB_K, AB_K), loop)
        stage_end(k, act, l * 4 + 5)
        act_gates2(k, act, l)
        stage_end(k, act, l * 4 + 6)
        act_fox(k, act, l)
        stage_end(k, act, l * 4 + 7)
        act_gla(k, act, l)
        stage_end(k, act, l * 4 + 8)
        act_merge(k, act, l + 1, M_LAYER + L_AB, TOK, W2, (OUT_K, OUT_K), loop)
        act_products(k, act, l * 3 + 3, M_LAYER + L_OUT, 2, W2, OUT_K, (GU_K, GU_K), loop)
        act_root(k, act, l * 6 + 7, W2)
        act_pre(k, act, l * 3 + 4, W2, updates=l * 3 + 3)
        act_ffn(k, act, l * 2 + 2, M_LAYER + L_GUB, M_LAYER + L_DOWNB, l * 3 + 4, W2, (None, None), loop)


def program_vector(k, dve):
    v = k.nc.vector
    dve.sem_inc(k.lo_ready, 2)
    dve.sem_inc(k.acc_free, 2)
    dve.sem_inc(k.sq_used, 2)
    dve.sem_inc(k.pv_evac, 1)
    dve.sem_inc(k.masked, 2)
    dve.sem_inc(k.y_evac, 2)
    dve.sem_inc(k.fox_y, 1)
    dve.sem_inc(k.fox_masked, 2)
    dve.sem_inc(k.gla_y, 1)
    v.memset(k.ssum[:, :], 0.0)
    dve.wait_ge(k.csig, 1)
    v.tensor_tensor(k.csil[:, :], k.csil[:, :], vec(k, "c", n=KT), ALU.mult).then_inc(k.csil_ready, 1)
    for l in range(LAYERS):
        for name in ("post1", "post2"):
            p = vec(k, name, l * VEC_LAYER, n=KT)
            v.tensor_scalar(p, p, 0.5, None, ALU.mult)
    dve.drain()
    dve_pre_sums(k, dve, 0, W1)
    for i in range(ADA_FIRST):
        dve.drain()
        dve.wait_ge(k.ada_first_landed[i], 16)
        dve_ada(k, dve, i, i % 2, k.ada_first[:, i, :])
    dve.wait_ge(k.ada_done, ADA_FIRST + 2)
    dve_mod(k, dve, 0, 16)
    v.scalar_tensor_tensor(k.fold[:, 0, :], k.mod[:, 8:16], 1.0, vec(k, "g_pre_mix", n=KT), ALU.add, ALU.mult)
    dve.drain()
    dve_pre_apply(k, dve, 0, W1, lambda t: k.fold[:, 0, t:t + 1], lambda t: k.mod[:, t:t + 1])
    prologue(split_lo, k, dve, 0, IN_K)
    dve_split_with_ada(k, dve, 0, ADA_LAST, (IN_K, IN_K))
    section(dve, ADA_LAST, IN1 - ADA_LAST, lambda t, p, s: ahead(split_lo, k, dve, p, s, IN_K))
    dve.wait_ge(k.ada_done, ADA_FIRST + ADA_LAST + 2)
    dve_mod(k, dve, 16, 32)
    v.tensor_tensor(k.fold[:, 1, :], k.mod[:, 16:24], vec(k, "g_post_mix", n=KT), ALU.mult)
    v.scalar_tensor_tensor(k.fold[:, 2, :], k.mod[:, 32:40], 1.0, vec(k, "g_pre_ffn", n=KT), ALU.add, ALU.mult)
    v.tensor_tensor(k.fold[:, 3, :], k.mod[:, 40:48], vec(k, "g_post_ffn", n=KT), ALU.mult)
    stage_end(k, dve, 1)
    dve_att(k, dve)
    stage_end(k, dve, 2)
    dve_rwkv_prep(k, dve)
    stage_end(k, dve, 3)
    dve_rwkv_pairs(k, dve)
    dve_rwkv_out(k, dve)
    stage_end(k, dve, 4)
    prologue(split_lo, k, dve, M_AB1, AB_K)
    dve_merge(k, dve, 0, M_AB1, SEQ, lambda t: tile(k.gates, t), lambda t: tile(k.gates, t + 8), W1, (OUT_K, OUT_K))
    dve_products(k, dve, 0, M_OUT1, 2, W1, OUT_K, (GU_K, GU_K))
    dve_post(k, dve, 0, W1, lambda t: k.fold[:, 1, t:t + 1])
    dve_pre(k, dve, 1, W1, lambda t: k.fold[:, 2, t:t + 1], lambda t: k.mod[:, 24 + t:25 + t])
    dve_ffn(k, dve, 0, M_GU1, M_DOWN1, 1, W1, lambda t: k.fold[:, 3, t:t + 1], (None, None))
    with dve.Fori(0, LAYERS) as l:
        loop = l * (L_PANELS // 2)

        def gain(name):
            return lambda t: vec(k, name, t, l)
        prologue(split_lo, k, dve, M_LAYER, GU_K, loop)
        dve_pre(k, dve, l * 3 + 2, W2, gain("pre1"))
        dve_ffn(k, dve, l * 2 + 1, M_LAYER + L_GUA, M_LAYER + L_DOWNA, l * 3 + 2, W2, gain("post1"),
                (AB_K, AB_K), loop)
        dve_pre(k, dve, l * 3 + 3, W2, gain("pre_mix"))

        def single(i):
            return k.small[:, :].unsqueeze(1) if i == 0 else k.p2[:, i - 1:i, :]
        dve_copy_out(k, dve, M_LAYER + L_SINGLE, SINGLES, 1, single, TOK, AB_K, (IN_K, IN_K), loop)
        dve_copy_out(k, dve, M_LAYER + L_IN, IN2, 2, lambda i: k.p2[:, bass.ds(i * 2 + 2, 2), :], TOK, IN_K,
                     (AB_K, AB_K), loop)
        stage_end(k, dve, l * 4 + 5)
        dve_gates2(k, dve, l)
        stage_end(k, dve, l * 4 + 6)
        dve_fox(k, dve, l)
        stage_end(k, dve, l * 4 + 7)
        dve_gla(k, dve, l)
        stage_end(k, dve, l * 4 + 8)
        dve_merge(k, dve, l + 1, M_LAYER + L_AB, TOK, lambda t: tile(k.p2, t + T_GA), lambda t: tile(k.p2, t + T_GB),
                  W2, (OUT_K, OUT_K), loop)
        dve_products(k, dve, l * 3 + 3, M_LAYER + L_OUT, 2, W2, OUT_K, (GU_K, GU_K), loop)
        dve_post(k, dve, l * 3 + 3, W2, gain("post_mix"))
        dve_pre(k, dve, l * 3 + 4, W2, gain("pre2"))
        dve_ffn(k, dve, l * 2 + 2, M_LAYER + L_GUB, M_LAYER + L_DOWNB, l * 3 + 4, W2, gain("post2"),
                (None, None), loop)


def program_gpsimd(k, pool, d):
    g = k.nc.gpsimd
    g.memset(k.mean_ones[:, :], 1.0 / D)
    g.memset(k.eps[:, 0:1], EPS)
    g.memset(k.eps[:, 1:2], GN_EPS).then_inc(k.const_ready, 1)
    pool.wait_ge(k.ada_products, ADA_FIRST)
    g.memset(k.p_in[:, :, 0:1], 0.0).then_inc(k.const_ready, 1)
    pool_shift(k, pool)
    stage_end(k, pool, 1)
    pool_att(k, pool)
    stage_end(k, pool, 2)
    pool_rwkv(k, pool, d)
    stage_end(k, pool, 3)
    pool_rwkv_zero(k, pool)
    pool_rwkv_pairs(k, pool)
    stage_end(k, pool, 4)
    with pool.Fori(0, LAYERS) as l:
        stage_end(k, pool, l * 4 + 5)
        pool.dma_start(k.wal[:, :], flat(d["wal"], l)).then_inc(k.dec_in, 16)
        pool_fox(k, pool)
        stage_end(k, pool, l * 4 + 6)
        stage_end(k, pool, l * 4 + 7)
        pool_gla(k, pool)
        stage_end(k, pool, l * 4 + 8)


def build(nc, d):
    with ExitStack() as ctx:
        k = Kernel()
        k.nc = nc
        allocate(k, nc, ctx)
        semaphores(k, lambda name: ctx.enter_context(nc.semaphore(name)))
        block = ctx.enter_context(nc.Block())

        @block.sync
        def _(sp):
            program_sync(k, sp, d)

        @block.tensor
        def _(pe):
            program_tensor(k, pe)

        @block.scalar
        def _(act):
            program_scalar(k, act, d)

        @block.vector
        def _(dve):
            program_vector(k, dve)

        @block.gpsimd
        def _(pool):
            program_gpsimd(k, pool, d)



def panels(w, per):
    kt, nt = w.shape[0] // P, w.shape[1] // P
    return w.reshape(kt, P, nt // per, per, P).transpose(2, 1, 3, 0, 4).reshape(nt // per, P, per * kt * P)


def gate_up(w):
    return w.reshape(KT, P, 2, FT, P).transpose(3, 1, 2, 0, 4).reshape(FT, P, GU_K * P)


def columns(v):
    return v.reshape(-1, P).T


def lay_out(x):
    f = {name: np.asarray(a) for name, a in x.items()}
    d = {}
    d["x"] = np.ascontiguousarray(f["x"][0].T.reshape(KT, P, SEQ).transpose(1, 0, 2))
    d["meta"] = np.ascontiguousarray(f["meta_tokens_2"].T.reshape(KT, P, META).transpose(1, 0, 2))
    v = np.zeros((P, VEC_COLS), np.float32)

    def put(name, a, layer=0):
        at, n = VEC[name]
        at += layer * VEC_LAYER
        v[:, at:at + n] = columns(a.reshape(-1))
    for name, src in (("c", "c"), ("b_ada", "b_ada"), ("g_pre_mix",) * 2, ("g_post_mix",) * 2, ("mu", "mu_shift"),
                      ("w0",) * 2, ("a0",) * 2, ("k_k",) * 2, ("k_a",) * 2, ("r_k",) * 2, ("lnx_w",) * 2,
                      ("lnx_b",) * 2, ("g_pre_ffn",) * 2, ("g_post_ffn",) * 2):
        put(name, f[src])
    for l in range(LAYERS):
        for name, src in (("pre1", "g_pre_ffn1_2"), ("post1", "g_post_ffn1_2"), ("pre_mix", "g_pre_mix_2"),
                          ("post_mix", "g_post_mix_2"), ("pre2", "g_pre_ffn2_2"), ("post2", "g_post_ffn2_2"),
                          ("b_alpha", "b_alpha_2"), ("g_gla", "g_gla_out_2")):
            put(name, f[src][l], l)
        v[FF_ROWS, VEC["b_f"][0] + l * VEC_LAYER] = f["b_f_2"][l]
    d["vec"] = v
    d["const"] = constants()
    d["w_ada"] = panels(f["w_ada"][0], 2)
    w = f["w_in"][0]
    d["w_in"] = panels(w, 2)
    d["w_ab"] = panels(np.concatenate([f["w_a"][0], f["w_b"][0]], 0), 1)
    d["w_out"] = panels(f["w_out"][0], 2)
    d["w_gu"] = gate_up(f["w_ffn_in"][0])
    d["w_down"] = panels(f["w_ffn_out"][0], 1)
    low = np.zeros((2, P, RW), np.float32)
    low[0, 0:HD] = f["w2"][0]
    low[1, HD:P] = f["a2"][0]
    d["w2"], d["a2"], d["g2"] = low[0], low[1], f["g2"][0]
    wal = np.zeros((LAYERS, P, 256), np.float32)
    wal[:, 0:16] = f["w_alpha_up_2"]
    d["wal"] = wal

    def layers(fn):
        return np.concatenate([fn(l) for l in range(LAYERS)], 0)
    sizes = (512, 512, 512, 8, 256, 256, 512, 16, 512, 1024, 1024)
    ends = np.cumsum(sizes)

    def split_in(l):
        w = f["w_in_2"][l]
        fq, fk, fv, ff, gq, gk, gv, ga, gr, ma, mb = (w[:, e - s:e] for s, e in zip(sizes, ends))
        small = np.zeros((D, P), np.float32)
        small[:, 0:16] = ga
        small[:, FF_ROWS] = ff
        return small, np.concatenate([fq, fk, fv, gq, gk, gv, gr, ma, mb], 1)
    d["w_in_single_2"] = layers(lambda l: panels(np.concatenate([split_in(l)[0], split_in(l)[1][:, 0:2 * P]], 1), 1))
    d["w_in_2"] = layers(lambda l: panels(split_in(l)[1][:, 2 * P:], 2))
    d["w_ab_2"] = layers(lambda l: panels(np.concatenate([f["w_fox_o_2"][l], f["w_gla_o_2"][l]], 0), 1))
    d["w_out_2"] = layers(lambda l: panels(f["w_out_2"][l], 2))
    for n in ("1", "2"):
        d["w_gu" + n + "_2"] = layers(lambda l: gate_up(f["w_ffn" + n + "_gu_2"][l]))
        d["w_down" + n + "_2"] = layers(lambda l: panels(f["w_ffn" + n + "_down_2"][l], 1))
    return {name: np.ascontiguousarray(a) for name, a in d.items()}


def kernel(**inputs):
    import concourse.bacc as bacc
    from concourse.bass_utils import run_bass_kernel_spmd as run

    nc = bacc.Bacc("TRN2", target_bir_lowering=False, num_devices=1)
    arrays = {f"in_{name}": a for name, a in lay_out(inputs).items()}
    d = {name[3:]: nc.dram_tensor(name, a.shape, F32, kind="ExternalInput").ap() for name, a in arrays.items()}
    d["out"] = nc.dram_tensor("out_x", (P, KT, SEQ), F32, kind="ExternalOutput").ap()
    build(nc, d)
    got = run(nc, [arrays], core_ids=[0]).results[0]["out_x"]
    return np.ascontiguousarray(got.transpose(2, 1, 0).reshape(1, SEQ, D))
```

```python
from contextlib import ExitStack

import numpy as np
import concourse.bass as bass
from concourse import mybir

F32 = mybir.dt.float32
F32R = mybir.dt.float32r
ALU = mybir.AluOpType
ACT = mybir.ActivationFunctionType
AX = mybir.AxisListType.X

P = 128
D = 1024
KT = D // P
SEQ = 256
META = 16
TOK = META + SEQ
HD = 64
EPS = 1e-6
NEG = -1e30

RW = 768
RT = RW // P
SHIFT_TILES = 20
GN_EPS = 64e-5
DECAY = float(np.exp(-0.5))
CHUNK = 64
NCH = SEQ // CHUNK
FF = 2816
FT = FF // P
GROUPS = ((128, 1), (512, 4), (2048, 16))

LAYERS = 2
FOX_PAIRS = 4
GLA_C = 68
GLA_N = TOK // GLA_C
BLOCKS = ((0, 16), (16, 144), (144, 272))

GU_K, DOWN_K, IN_K, AB_K, OUT_K = 16, FT, 16, 8, 16
ADA_FIRST, ADA_MORE = 8, 3
ADA_PRELOADED = ADA_FIRST + ADA_MORE
ADA_LAST = 24 - ADA_PRELOADED
ADA_K = 16
IN1, AB, OUT, GU, DOWN = 27, 8, 4, 22, 8
assert ADA_LAST == IN1 // 2
SINGLES, IN2 = 3, 19
IN2_GATES = 8
M_AB1 = IN1
M_OUT1 = M_AB1 + AB
M_GU1 = M_OUT1 + OUT
M_DOWN1 = M_GU1 + GU
M_LAYER = M_DOWN1 + DOWN
L_GUA, L_DOWNA = 0, GU
L_SINGLE = GU + DOWN
L_IN = L_SINGLE + SINGLES
L_AB = L_IN + IN2
L_OUT = L_AB + AB
L_GUB = L_OUT + OUT
L_DOWNB = L_GUB + GU
L_PANELS = L_DOWNB + DOWN
assert L_PANELS % 2 == 0

T_R, T_K, T_V, T_WA, T_G = 0, 6, 12, 18, 19
T_FQ, T_FK, T_FV, T_GQ, T_GK, T_GV, T_GR, T_GA, T_GB = 0, 4, 8, 12, 14, 16, 20, 24, 32


def vector_table():
    at, cols = {}, 0
    for name, n in (("c", 8), ("b_ada", 48), ("g_pre_mix", 8), ("g_post_mix", 8), ("mu", 20), ("w0", 6), ("a0", 6),
                    ("k_k", 6), ("k_a", 6), ("r_k", 6), ("lnx_w", 6), ("lnx_b", 6), ("g_pre_ffn", 8),
                    ("g_post_ffn", 8)):
        at[name] = (cols, n)
        cols += n
    first = cols
    for name, n in (("pre1", 8), ("post1", 8), ("pre_mix", 8), ("post_mix", 8), ("pre2", 8), ("post2", 8),
                    ("b_alpha", 2), ("b_f", 1), ("g_gla", 4)):
        at[name] = (cols, n)
        cols += n
    per_layer = cols - first
    return at, cols + per_layer * (LAYERS - 1), per_layer


VEC, VEC_COLS, VEC_LAYER = vector_table()
CONST = {}
_at = 0
for _name, _n in (("ident", 128), ("rot", 128), ("mask_att", 768), ("mask_fox", 272), ("up_strict", 64),
                  ("lo_strict", 64), ("up_incl", 64), ("i2", 64), ("pair_ones", 128),
                  ("cos", 256), ("sin", 256), ("gla_mask", 68), ("eye8", 8)):
    CONST[_name] = (_at, _n)
    _at += _n
CONST_COLS = _at


def constants():
    c = np.zeros((P, CONST_COLS), np.float32)

    def put(name, a):
        at, n = CONST[name]
        c[:a.shape[0], at:at + n] = a.reshape(a.shape[0], n)

    i = np.arange(P)
    put("ident", np.eye(P))
    rot = np.zeros((P, P))
    for m in range(P):
        h, o = divmod(m, HD)
        if o < HD // 2:
            rot[h * HD + o + HD // 2, m] = -1.0
        else:
            rot[h * HD + o - HD // 2, m] = 1.0
    put("rot", rot)
    q, k = i[:, None], i[None, :]
    masks = np.zeros((P, 3, 2, P))
    for g, (window, dil) in enumerate(GROUPS):
        before, diag = q + P - k, q - k
        masks[:, g, 0] = np.where((before % dil == 0) & (before <= window), 0.0, NEG)
        masks[:, g, 1] = np.where((diag % dil == 0) & (diag >= 0) & (diag <= window), 0.0, NEG)
    put("mask_att", masks)
    put("mask_fox", np.concatenate([np.zeros((P, 144)), np.where(q >= k, 0.0, NEG)], 1))
    same = (q // CHUNK) == (k // CHUNK)
    s, t = (i % CHUNK)[:, None], np.arange(CHUNK)[None, :]
    put("up_strict", np.where(s < t, 1.0, 0.0))
    put("lo_strict", np.where(s > t, 1.0, 0.0))
    put("up_incl", np.where(s <= t, 1.0, 0.0))
    put("i2", np.where(s == t, 1.0, 0.0))
    put("pair_ones", np.where(same, 1.0, 0.0))
    half = HD // 2
    inv = (10000.0 ** (-np.arange(half, dtype=np.float32) / half)).astype(np.float32)
    ang = np.arange(SEQ, dtype=np.float32)[None, :] * inv[i % half][:, None]
    put("cos", np.cos(ang))
    put("sin", np.sin(ang))
    g = np.arange(GLA_C)
    put("gla_mask", np.where(g[:, None] <= g[None, :], 1.0, 0.0))
    put("eye8", np.eye(8))
    return c


class Panel:

    def __init__(self, half, par):
        self.half, self.par = half, par

    @classmethod
    def of(cls, m, loop=0):
        return cls(m // 2 + loop, m % 2)

    def ahead2(self):
        return Panel(self.half + 1, self.par)

    def count(self, extra):
        return self.half * 2 + (self.par + extra)

    def landed(self):
        return (self.half + 1) * 16


def section(eng, start, count, fn, loop=0, after=(None, None), unrolled=False):
    pairs = 0 if unrolled else (count - 2) // 2
    if pairs > 0:
        with eng.Fori(0, pairs) as i:
            for b in range(2):
                fn(i * 2 + b, Panel.of(start + b, loop + i), "same")
    for t in range(2 * max(pairs, 0), count):
        left = count - 1 - t
        fn(t, Panel.of(start + t, loop), "same" if left >= 2 else after[1 - left])


class Kernel:
    pass


def allocate(k, nc, ctx):
    where = [16512]

    def at(name, shape, dt=F32, offset=None):
        size = 4 * int(np.prod(shape[1:]))
        here = where[0] if offset is None else offset
        t = nc.alloc_sbuf_tensor_at(name, shape, dt, offset=here)
        here += -(-size // 32) * 32
        if offset is None:
            where[0] = here
        return t, here

    def fixed(name, shape, dt=F32):
        return at(name, shape, dt)[0]

    def chain(start, *items):
        out = []
        for name, shape, *dt in items:
            t, start = at(name, shape, dt[0] if dt else F32, offset=start)
            out.append(t)
        return out, start

    k.land = fixed("land", [P, 2, FT * P])
    k.w_hi = fixed("w_hi", [P, 2, FT * P], F32R)
    k.w_lo = fixed("w_lo", [P, 2, FT * P], F32R)
    k.x = fixed("x", [P, KT, TOK])
    k.const = fixed("const", [P, CONST_COLS])
    k.vec = fixed("vec", [P, VEC_COLS])
    k.ssum = fixed("ssum", [P, TOK])
    k.root = fixed("root", [P, TOK])
    k.rstd = fixed("rstd", [P, TOK])
    norm_at = where[0]
    k.sq = fixed("sq", [P, 2, TOK])
    k.sq_post = fixed("sq_post", [P, 4, TOK])
    k.upd = fixed("upd", [P, 2, TOK])
    norm_end = where[0]
    k.mean_ones = fixed("mean_ones", [P, P])
    k.mod = fixed("mod", [P, 48])
    k.fold = fixed("fold", [P, 4, KT])
    k.csil = fixed("csil", [P, KT])
    k.eps = fixed("eps", [P, 2])
    h_at = where[0]
    k.h_hi = fixed("h_hi", [P, KT, TOK], F32R)
    k.h_lo = fixed("h_lo", [P, KT, TOK], F32R)
    k.f = fixed("f", [P, KT, TOK])
    h_end = where[0]
    arena = where[0]
    top = 229344

    (k.a_hi, k.a_lo, k.sig, k.t_ff, k.a_ff), end = chain(
        arena, ("a_hi", [P, FT, TOK], F32R), ("a_lo", [P, FT, TOK], F32R), ("sig", [P, 2, TOK]),
        ("t_ff", [P, 2, TOK]), ("a_ff", [P, 2, TOK]))
    assert end <= top, end

    (k.p_in, k.gates, k.c1), qkv_at = chain(
        arena, ("p_in", [P, SHIFT_TILES, SEQ + 1]), ("gates", [P, 16, SEQ]), ("c1", [P, RT, SEQ]))
    (k.qkv,), late = chain(qkv_at, ("qkv", [P, 18, SEQ]))
    ada_at = top - 4 * ADA_PRELOADED * ADA_K * P
    (k.ada_first,), end = chain(ada_at, ("ada_first", [P, ADA_PRELOADED, ADA_K * P]))
    k.ada_slot = k.ada_first[:, ADA_FIRST, :]
    assert h_end - 4 * KT * TOK <= ada_at and late <= ada_at + 4 * ADA_FIRST * ADA_K * P
    (k.qs, k.kz), end = chain(h_at, ("qs", [P, 3, SEQ]), ("kz", [P, 3, 2, SEQ]),)
    (k.vs, k.vz, k.s_att), end = chain(
        end, ("vs", [P, 3, SEQ]), ("vz", [P, 3, 2, 2, P]), ("s_att", [P, 2, 3, SEQ]))
    (k.rt1, k.rt2), _ = chain(norm_at, ("rt1", [P, 2, SEQ]), ("rt2", [P, 2, SEQ]))
    assert end <= h_end, (end, h_end)
    (k.p_att, k.pt_att, k.st_att), att_end = chain(
        late, ("p_att", [P, 2, 3, SEQ]), ("pt_att", [P, 2, 6, P]), ("st_att", [P, 2, 4]))
    assert att_end <= late + 4 * 2 * RT * SEQ + 96
    (k.bon, k.gate, k.tmp), end = chain(
        qkv_at, ("bon", [P, RT, SEQ]), ("gate", [P, RT, SEQ]), ("tmp", [P, RT, SEQ]))
    assert end <= late
    (k.beta, k.kap), rest = chain(late, ("beta", [P, RT, SEQ]), ("kap", [P, RT, SEQ]))
    (k.sw, k.kk, k.reset, k.w2p, k.a2p), end2 = chain(
        h_at, ("sw", [P, RT, SEQ]), ("kk", [P, RT, SEQ]), ("reset", [P, SEQ]), ("w2p", [P, RW]), ("a2p", [P, RW]))
    (k.g2,), end2 = chain(end2, ("g2", [P, RW]))
    assert end2 <= h_end
    (k.pc, k.yb_keep), rest = chain(rest, ("pc", [P, RT, NCH]), ("yb_keep", [P, 2, SEQ]))
    bd = [P, NCH, P]
    st = [P, NCH, CHUNK]
    names = (("al_bd", bd), ("be_bd", bd), ("ka_bd", bd), ("v_bd", bd), ("xr", bd), ("x_st", st),
             ("x_bd", bd), ("xt_bd", bd), ("rt_bd", bd), ("akt_bd", bd))
    place = h_at
    made = {}
    for name, shape in names:
        (made[name],), place = chain(place, (name, shape))
    assert place <= h_end, (place, h_end)
    h_place = place
    place = rest
    for name, shape in (("qbt", st), ("qkt", st), ("au", bd), ("bet_bd", bd), ("bet_st", st), ("kat_bd", bd),
                        ("vt_bd", bd)):
        (made[name],), place = chain(place, (name, shape))
    assert place <= top, (place, top)
    place = qkv_at + 2 * 4 * RT * SEQ
    for name, shape in (("w_bd", bd), ("u_bd", bd), ("f_st", st), ("n_st", st)):
        (made[name],), place = chain(place, (name, shape))
    assert place <= late, (place, late)
    place = norm_at
    for name, shape in (("vt_st", st), ("u_st", st), ("m_bd", bd), ("s_st", [P, CHUNK]), ("s_bd", [P, 3, P])):
        (made[name],), place = chain(place, (name, shape))
    assert place <= norm_end - 4 * (RT * 32 + SEQ), (place, norm_end)
    place = 16512 + 4 * 2 * FT * P
    second = {}
    for name, t in made.items():
        (second[name],), place = chain(place, (name + "_2nd", list(t.shape)))
    assert place <= 16512 + 4 * 6 * FT * P, place
    k.m = (made, second)
    (k.sel, k.per_head), end = chain(norm_end - 4 * (RT * 32 + SEQ), ("sel", [P, RT * 32]), ("per_head", [32, SEQ]))
    (k.spread,), _ = chain(h_end - 4 * RT * P, ("spread", [32, RT * P]))
    assert end2 <= h_end - 4 * RT * P and h_place <= h_end - 4 * RT * P
    (k.y1_hi, k.y1_lo), end = chain(arena, ("y1_hi", [P, KT, SEQ], F32R), ("y1_lo", [P, KT, SEQ], F32R))
    assert end <= arena + 4 * SHIFT_TILES * (SEQ + 1)

    (k.p2, k.y_hi, k.y_lo), mix_at = chain(
        arena, ("p2", [P, 40, TOK]), ("y_hi", [P, KT, TOK], F32R), ("y_lo", [P, KT, TOK], F32R))
    (k.small, k.wal, k.gcum), end = chain(mix_at, ("small", [P, TOK]), ("wal", [P, 256]), ("gcum", [P, 2, TOK]))
    (k.gst, k.cum, k.lf), end = chain(end, ("gst", [P, 2, 3, GLA_N]), ("cum", [P, TOK]), ("lf", [P, TOK]))
    k.mix_rest = end
    (k.e1, k.e2), end = chain(end, ("e1", [P, 2, TOK]), ("e2", [P, 2, TOK]))
    gr_at = end
    (k.minus8, k.gr_), end = chain(end, ("minus8", [8, P]), ("gr_", [P, 4, TOK]))
    assert end <= top, (end, top)
    (k.fkz, k.fvz, k.fs, k.fp, k.fpt), end = chain(
        h_at, ("fkz", [P, 2, 2, TOK]), ("fvz", [P, 2, 3, 2, P]),
        ("fs", [P, 2, TOK]), ("fp", [P, 2, TOK]), ("fpt", [P, 2, 3, P]))
    (k.cumz,), end2 = chain(norm_at, ("cumz", [8, 8, TOK]))
    assert end2 <= norm_end
    assert end <= h_end, (end, h_end)
    (k.fstat, k.fy), end = chain(
        k.mix_rest, ("fstat", [P, 2, 4]), ("fy", [P, 2, TOK]))
    assert end <= top
    k.g = ({}, {})
    place, place2, place3 = h_at, norm_at, k.mix_rest
    for s in range(2):
        for name, shape in (("kz", [P, 2, TOK]), ("vt", [GLA_C, GLA_N, 2, P]), ("kt", [GLA_C, GLA_N, P]),
                            ("state", [P, P]), ("scaled", [P, 3, 2, P])):
            (k.g[s][name],), place = chain(place, (f"gla_{name}{s}", shape))
        for name, shape in (("at", [GLA_C, GLA_N, 2, GLA_C]), ("o", [P, 2, TOK])):
            (k.g[s][name],), place2 = chain(place2, (f"gla_{name}{s}", shape))
        (k.g[s]["sq"],), place3 = chain(place3, (f"gla_sq{s}", [P, 2, TOK]))
    assert place <= h_end and place2 <= norm_end and place3 <= gr_at, (place, h_end, place2, norm_end, place3, gr_at)

    k.acc = ctx.enter_context(nc.psum_tensor("acc", [P, 4, 512], F32))
    k.mb = ctx.enter_context(nc.psum_tensor("mb", [P, 4, 512], F32))
    k.stat = k.mb[:, 3, 0:TOK]


def semaphores(k, sem):
    k.landed = (sem("landed0"), sem("landed1"))
    k.ada_first_landed = [sem(f"ada_first_landed{i}") for i in range(ADA_PRELOADED)]
    k.ada_landed = sem("ada_landed")
    k.ada_products = sem("ada_products")
    k.ada_done = sem("ada_done")
    k.hi_ready = sem("hi_ready")
    k.lo_ready = sem("lo_ready")
    k.panel_done = sem("panel_done")
    k.acc_free = sem("acc_free")
    k.x_loaded = sem("x_loaded")
    k.vec_loaded = sem("vec_loaded")
    k.lora_loaded = sem("lora_loaded")
    k.const_loaded = sem("const_loaded")
    k.const_ready = sem("const_ready")
    k.csig = sem("csig")
    k.stored = sem("stored")
    k.sq_ready = sem("sq_ready")
    k.sq_used = sem("sq_used")
    k.sq_post_ready = sem("sq_post_ready")
    k.sums_ready = sem("sums_ready")
    k.stat_done = sem("stat_done")
    k.root_ready = sem("root_ready")
    k.n_ready = sem("n_ready")
    k.hh_ready = sem("hh_ready")
    k.hl_ready = sem("hl_ready")
    k.x_ready = sem("x_ready")
    k.sig_ready = sem("sig_ready")
    k.ah_ready = sem("ah_ready")
    k.al_ready = sem("al_ready")
    k.stage = sem("stage")
    k.pin_ready = sem("pin_ready")
    k.gla_zero = sem("gla_zero")
    k.gates_ready = sem("gates_ready")
    k.merged = sem("merged")
    k.yh_ready = sem("yh_ready")
    k.yl_ready = sem("yl_ready")
    k.t_ready = sem("t_ready")
    k.rot_done = sem("rot_done")
    k.q_copied = sem("q_copied")
    k.att_ready = sem("att_ready")
    k.v_tok = sem("v_tok")
    k.v_evac = sem("v_evac")
    k.scored = sem("scored")
    k.masked = sem("masked")
    k.p_ready = sem("p_ready")
    k.p_norm = sem("p_norm")
    k.p_tr = sem("p_tr")
    k.pt_ready = sem("pt_ready")
    k.pv_done = sem("pv_done")
    k.pv_evac = sem("pv_evac")
    k.wg_ready = sem("wg_ready")
    k.lora_mm = sem("lora_mm")
    k.lora_evac = sem("lora_evac")
    k.kk_sq = sem("kk_sq")
    k.kk_sum = sem("kk_sum")
    k.kk_root = sem("kk_root")
    k.kk_inv = sem("kk_inv")
    k.kk_spread = sem("kk_spread")
    k.gn_inv = sem("gn_inv")
    k.gn_spread = sem("gn_spread")
    k.gn_norm = sem("gn_norm")
    k.gn_affine = sem("gn_affine")
    k.c_ready = sem("c_ready")
    k.exp_ready = sem("exp_ready")
    k.arr_ready = sem("arr_ready")
    k.bon_in = sem("bon_in")
    k.bon_sum = sem("bon_sum")
    k.bd_pool = sem("bd_pool")
    k.bd_act = sem("bd_act")
    k.xbd_ready = sem("xbd_ready")
    k.round_act = sem("round_act")
    k.tok_act = sem("tok_act")
    k.max_ready = sem("max_ready")
    k.gram = sem("gram")
    k.gram_evac = sem("gram_evac")
    k.tok_mm = sem("tok_mm")
    k.tok_evac = sem("tok_evac")
    k.round_mm = sem("round_mm")
    k.round_evac = sem("round_evac")
    k.rt_copied = sem("rt_copied")
    k.u0_mm = sem("u0_mm")
    k.u0_evac = sem("u0_evac")
    k.wu_mm = sem("wu_mm")
    k.wu_evac = sem("wu_evac")
    k.mfn_mm = sem("mfn_mm")
    k.mfn_evac = sem("mfn_evac")
    k.chain_mm = sem("chain_mm")
    k.chain_evac = sem("chain_evac")
    k.y_mm = sem("y_mm")
    k.y_evac = sem("y_evac")
    k.gn_in = sem("gn_in")
    k.gn_sum = sem("gn_sum")
    k.gn_root = sem("gn_root")
    k.gn_sq = sem("gn_sq")
    k.dec_in = sem("dec_in")
    k.dec_exp = sem("dec_exp")
    k.dec_abs = sem("dec_abs")
    k.dec_mm = sem("dec_mm")
    k.gz_ready = sem("gz_ready")
    k.gexp_ready = sem("gexp_ready")
    k.gla_copy = sem("gla_copy")
    k.gla_tok = sem("gla_tok")
    k.gla_tok_evac = sem("gla_tok_evac")
    k.gla_att = sem("gla_att")
    k.gla_att_evac = sem("gla_att_evac")
    k.gla_state = sem("gla_state")
    k.gla_state_evac = sem("gla_state_evac")
    k.gla_o = sem("gla_o")
    k.gla_sq = sem("gla_sq")
    k.gla_mean = sem("gla_mean")
    k.gla_root = sem("gla_root")
    k.wh_y = sem("wh_y")
    k.gyh_ready = sem("gyh_ready")
    k.y_ready = sem("y_ready")
    k.settled = sem("settled")
    k.fox_copy = sem("fox_copy")
    k.fox_tok = sem("fox_tok")
    k.fox_tok_evac = sem("fox_tok_evac")
    k.fox_sc = sem("fox_sc")
    k.fox_masked = sem("fox_masked")
    k.fox_p = sem("fox_p")
    k.fox_norm = sem("fox_norm")
    k.fox_tr = sem("fox_tr")
    k.fox_pt = sem("fox_pt")
    k.fox_pv = sem("fox_pv")


def stage_end(k, eng, n):
    eng.drain().then_inc(k.stage, 1)
    eng.wait_ge(k.stage, n * 4)
    settle(k, eng)


def settle(k, eng):
    eng.sem_inc(k.settled, 1)


def const(k, name, rows=slice(0, P)):
    at, n = CONST[name]
    return k.const[rows, at:at + n]


def vec(k, name, t=0, layer=None, n=1, rows=slice(0, P)):
    at = VEC[name][0]
    if layer is None:
        return k.vec[rows, bass.ds(at + t, n)]
    return k.vec[rows, bass.ds(layer * VEC_LAYER + (at + t), n)]



def load(k, sp, par, half, dram, size):
    sp.dma_start(k.land[:, par, 0:size * P], dram).then_inc(k.landed[par], 16)


def load_section(k, sp, start, count, dram, size, loop=0):
    def one(i, p, _):
        sp.wait_ge(k.lo_ready, p.count(1))
        load(k, sp, p.par, p.half, dram(i), size)
    section(sp, start, count, one, loop)


def load_with_ada(k, sp, d):
    def ada(n):
        sp.wait_ge(k.ada_products, n)
        sp.dma_start(k.ada_slot, flat(d["w_ada"], n)).then_inc(k.ada_landed, 16)

    def one(i, p, _):
        if p.par == 0:
            ada(p.half + (ADA_PRELOADED - 2))
        sp.wait_ge(k.lo_ready, p.count(1))
        load(k, sp, p.par, p.half, flat(d["w_in"], i + 4), IN_K)
    for i in range(2, 4):
        sp.wait_ge(k.lo_ready, i + 1)
        load(k, sp, i % 2, None, flat(d["w_in"], i), IN_K)
    section(sp, 4, IN1 - 4, one)
    ada(ADA_PRELOADED + ADA_LAST - 1)


def flat(ap, i):
    return ap[bass.ds(i, 1), :, :].rearrange("a p n -> p (a n)")


def program_sync(k, sp, d):
    W = slice(META, TOK)
    sp.dma_start(k.vec[:, :], d["vec"]).then_inc(k.vec_loaded, 16)
    for i in range(ADA_PRELOADED):
        if i == ADA_FIRST:
            for b in range(2):
                load(k, sp, b, None, flat(d["w_in"], b), IN_K)
        sp.dma_start(k.ada_first[:, i, :], flat(d["w_ada"], i)).then_inc(k.ada_first_landed[i], 16)
    load_with_ada(k, sp, d)
    load_section(k, sp, M_AB1, AB, lambda i: flat(d["w_ab"], i), AB_K)
    load_section(k, sp, M_OUT1, OUT, lambda i: flat(d["w_out"], i), OUT_K)
    load_section(k, sp, M_GU1, GU, lambda i: flat(d["w_gu"], i), GU_K)
    load_section(k, sp, M_DOWN1, DOWN, lambda i: flat(d["w_down"], i), DOWN_K)
    with sp.Fori(0, LAYERS) as l:
        q = l * (L_PANELS // 2)

        def part(start, count, name, size, each=None, first=0):
            n = count if each is None else each
            load_section(k, sp, M_LAYER + start, count, lambda i: flat(d[name], l * n + i + first), size, q)
        part(L_GUA, GU, "w_gu1_2", GU_K)
        part(L_DOWNA, DOWN, "w_down1_2", DOWN_K)
        part(L_SINGLE, SINGLES, "w_in_single_2", AB_K)
        part(L_IN, IN2, "w_in_2", IN_K)
        part(L_AB, AB, "w_ab_2", AB_K)
        part(L_OUT, OUT, "w_out_2", OUT_K)
        part(L_GUB, GU, "w_gu2_2", GU_K)
        part(L_DOWNB, DOWN, "w_down2_2", DOWN_K)
    sp.wait_ge(k.x_ready, KT * (2 + 3 * LAYERS))
    sp.dma_start(d["out"], k.x[:, :, W]).then_inc(k.stored, 16)
    sp.wait_ge(k.stored, 16)



def split_hi(k, act, p, size):
    for par in (0, 1):
        if par == p.par:
            act.wait_ge(k.landed[par], p.landed())
    act.wait_ge(k.panel_done, p.count(1))
    k.nc.scalar.activation(k.w_hi[:, p.par, 0:size * P], k.land[:, p.par, 0:size * P],
                           ACT.Copy).then_inc(k.hi_ready, 1)


def split_lo(k, dve, p, size):
    dve.wait_ge(k.hi_ready, p.count(1))
    k.nc.vector.tensor_tensor(k.w_lo[:, p.par, 0:size * P], k.land[:, p.par, 0:size * P],
                              k.w_hi[:, p.par, 0:size * P].bitcast(F32), ALU.subtract).then_inc(k.lo_ready, 1)


def ahead(fn, k, eng, p, nxt, size):
    if nxt is not None:
        fn(k, eng, p.ahead2(), size if nxt == "same" else nxt)


def panel_begin(k, pe, p):
    pe.wait_ge(k.lo_ready, p.count(3))
    pe.wait_ge(k.acc_free, p.count(1))


def tile_mm(k, out, par, tile, hi, lo, start, stop):
    c = slice(tile * P, (tile + 1) * P)
    mm = k.nc.tensor.matmul
    mm(out, k.w_hi[:, par, c], hi, start=start, stop=False)
    mm(out, k.w_hi[:, par, c], lo, start=False, stop=False)
    return mm(out, k.w_lo[:, par, c], hi, start=False, stop=stop)


def pe_project(k, pe, start, count, tiles, W, loop=0, ada=False, ready=None):
    n = W.stop - W.start

    def one(i, p, _):
        panel_begin(k, pe, p)
        for o in range(tiles):
            for t in range(KT):
                last = tile_mm(k, k.acc[:, 2 * p.par + o, 0:n], p.par, o * KT + t, k.h_hi[:, t, W],
                               k.h_lo[:, t, W], t == 0, t == KT - 1)
        last.then_inc(k.panel_done, 1)
        if ada and p.par == 1:
            pe_ada(k, pe, p.half + (ADA_PRELOADED - 1), 1)
    peeled = 0
    if ready is not None:
        p = Panel.of(start, loop)
        panel_begin(k, pe, p)
        for t in range(KT):
            pe.wait_ge(ready[0], ready[1] + (t + 1))
            for o in range(tiles):
                last = tile_mm(k, k.acc[:, 2 * p.par + o, 0:n], p.par, o * KT + t, k.h_hi[:, t, W],
                               k.h_lo[:, t, W], t == 0, t == KT - 1)
        last.then_inc(k.panel_done, 1)
        peeled = 1
    section(pe, start + peeled, count - peeled, one, loop)



def dve_ada(k, dve, n, slot, src, behind):
    w = src.rearrange("p (o t c) -> p t o c", o=2, t=KT)
    dve.wait_ge(k.ada_done, n + 1 if behind else n + 2)
    sums, more = k.sq_post[:, 2 * slot:2 * slot + 2, 0:2 * P], k.upd[:, :, 0:2 * P]
    for t in range(KT):
        out = (sums if t % 4 < 2 else more)[:, t % 2, :].rearrange("p (o c) -> p o c", o=2)
        c = k.csil[:, t:t + 1]
        if t < 4:
            k.nc.vector.tensor_scalar(out, w[:, t], c, None, ALU.mult)
        else:
            k.nc.vector.scalar_tensor_tensor(out, w[:, t], c, out, ALU.mult, ALU.add)
        if t % 4 == 3:
            dve.drain()
    k.nc.vector.tensor_tensor(sums, sums, more, ALU.add).then_inc(k.ada_products, 1)


def pe_ada(k, pe, n, slot):
    pe.wait_ge(k.ada_products, n + 1)
    for o in range(2):
        for s in range(2):
            last = k.nc.tensor.matmul(k.mb[:, 2, bass.ds(n * 2 + o, 1)],
                                      k.sq_post[:, 2 * slot + s, o * P:(o + 1) * P],
                                      k.mean_ones[:, 0:1], start=s == 0, stop=s == 1)
    last.then_inc(k.ada_done, 1)


def dve_mod(k, dve, first, n):
    k.nc.vector.scalar_tensor_tensor(k.mod[:, first:first + n], k.mb[:, 2, first:first + n], float(D),
                                     vec(k, "b_ada", first, n=n), ALU.mult, ALU.add)
    dve.drain()


def dve_split_with_ada(k, dve, start, count, nxt):
    def one(i, p, ahead_size):
        ahead(split_lo, k, dve, p, ahead_size, IN_K)
        if p.par == 1:
            dve.drain()
            dve.wait_ge(k.ada_landed, p.landed())
            dve_ada(k, dve, p.half + ADA_PRELOADED, 1, k.ada_slot, False)
    section(dve, start, count, one, 0, nxt)


def pe_down(k, pe, start, W, first, loop=0):
    n = W.stop - W.start
    p = Panel.of(start, loop)
    panel_begin(k, pe, p)
    for t in range(FT):
        pe.wait_ge(k.al_ready, first + (t + 1))
        last = tile_mm(k, k.acc[:, 2 * p.par, 0:n], p.par, t, k.a_hi[:, t, W], k.a_lo[:, t, W],
                       t == 0, t == FT - 1)
    last.then_inc(k.panel_done, 1)

    def one(i, p, _):
        panel_begin(k, pe, p)
        for t in range(FT):
            last = tile_mm(k, k.acc[:, 2 * p.par, 0:n], p.par, t, k.a_hi[:, t, W], k.a_lo[:, t, W],
                           t == 0, t == FT - 1)
        last.then_inc(k.panel_done, 1)
    section(pe, start + 1, DOWN - 1, one, loop)


def pe_branches(k, pe, start, n, y_hi, y_lo, first, loop=0):
    def one(i, p, _):
        panel_begin(k, pe, p)
        for t in range(KT):
            b = int(t >= first)
            last = tile_mm(k, k.acc[:, 2 * p.par + b, 0:n], p.par, t, y_hi[:, t, 0:n], y_lo[:, t, 0:n],
                           t in (0, first), t in (first - 1, KT - 1))
        last.then_inc(k.panel_done, 1)
    section(pe, start, AB, one, loop)



def pe_stat(k, pe, i, W):
    pe.wait_ge(k.sums_ready, i + 1)
    k.nc.tensor.matmul(k.mb[:, 3, 0:W.stop - W.start], k.mean_ones[:, :], k.ssum[:, W],
                       start=True, stop=True).then_inc(k.stat_done, 1)


def act_post_root(k, act, i, W):
    act.wait_ge(k.stat_done, i + 1)
    act_root(k, W)


def act_root(k, W):
    k.nc.scalar.activation(k.root[:, W], k.mb[:, 3, 0:W.stop - W.start], ACT.Sqrt,
                           bias=k.eps[:, 0:1]).then_inc(k.root_ready, 1)


def dve_rstd(k, dve, n, W):
    dve.wait_ge(k.root_ready, n + 1)
    k.nc.vector.reciprocal(k.rstd[:, W], k.root[:, W])
    dve.drain()


def act_pre_sums(k, act, i, W, updates=None):
    for t in range(KT):
        if updates is not None:
            act.wait_ge(k.x_ready, updates * KT + (t + 1))
        act.wait_ge(k.sq_used, i * KT + (t + 1))
        k.nc.scalar.activation(k.sq[:, t % 2, W], k.x[:, t, W], ACT.Square).then_inc(k.sq_ready, 1)
    act.wait_ge(k.sq_used, i * KT + (KT + 2))
    act_root(k, W)


def act_pre(k, act, i, W, shift=None, updates=None):
    act_pre_sums(k, act, i, W, updates)
    act_pre_split(k, act, i, W, shift)


def act_pre_split(k, act, i, W, shift=None):
    for t in range(KT):
        act.wait_ge(k.n_ready, i * KT + (t + 1))
        if shift is None:
            r = k.nc.scalar.activation(k.h_hi[:, t, W], k.f[:, t, W], ACT.Copy)
        else:
            r = k.nc.scalar.activation(k.h_hi[:, t, W], k.f[:, t, W], ACT.Identity, bias=shift(t))
        r.then_inc(k.hh_ready, 1)


def dve_pre(k, dve, i, W, gain, shift=None):
    dve_rstd(k, dve, i * 2, W)
    dve_pre_apply(k, dve, i, W, gain, shift)


def dve_pre_apply(k, dve, i, W, gain, shift=None):
    v = k.nc.vector

    def normed(t):
        v.scalar_tensor_tensor(k.f[:, t, W], k.x[:, t, W], gain(t), k.rstd[:, W], ALU.mult,
                               ALU.mult).then_inc(k.n_ready, 1)
    normed(0)
    for t in range(KT):
        if t + 1 < KT:
            normed(t + 1)
        if t == KT - 1:
            dve.drain()
        dve.wait_ge(k.hh_ready, i * KT + (t + 1))
        hh = k.h_hi[:, t, W].bitcast(F32)
        if shift is None:
            r = v.tensor_tensor(k.h_lo[:, t, W], k.f[:, t, W], hh, ALU.subtract)
        else:
            r = v.scalar_tensor_tensor(k.h_lo[:, t, W], k.f[:, t, W], shift(t), hh, ALU.add, ALU.subtract)
        r.then_inc(k.hl_ready, 1)


def pe_pre(k, pe, i, W):
    for t in range(KT):
        pe.wait_ge(k.sq_ready, i * KT + (t + 1))
        k.nc.tensor.matmul(k.mb[:, 3, 0:W.stop - W.start], k.mean_ones[:, :], k.sq[:, t % 2, W],
                           start=t == 0, stop=t == KT - 1).then_inc(k.sq_used, 1)


def act_products(k, act, i, start, tiles, W, size, nxt, loop=0):
    n = W.stop - W.start

    def one(t, p, ahead_size):
        act.wait_ge(k.panel_done, p.count(3))
        for o in range(tiles):
            k.nc.scalar.activation(k.sq_post[:, 2 * p.par + o, W], k.acc[:, 2 * p.par + o, 0:n],
                                   ACT.Square).then_inc(k.sq_post_ready, 1)
        ahead(split_hi, k, act, p, ahead_size, size)
    section(act, start, KT // tiles, one, loop, nxt)


def dve_products(k, dve, i, start, tiles, W, size, nxt, loop=0):
    n = W.stop - W.start
    v = k.nc.vector

    def one(idx, p, ahead_size):
        dve.wait_ge(k.panel_done, p.count(3))
        for o in range(tiles):
            t = idx * tiles + o
            f = k.f[:, bass.ds(t, 1), W].rearrange("p a n -> p (a n)")
            dve.wait_ge(k.sq_post_ready, i * KT + (t + 1))
            v.tensor_copy(f, k.acc[:, 2 * p.par + o, 0:n])
            r = v.tensor_tensor(k.ssum[:, W], k.ssum[:, W], k.sq_post[:, 2 * p.par + o, W], ALU.add)
            if o == tiles - 1:
                r.then_inc(k.acc_free, 1)
            dve.drain()
        ahead(split_lo, k, dve, p, ahead_size, size)
    section(dve, start, KT // tiles, one, loop, (nxt[0], None))


def dve_post(k, dve, i, W, gain, late=None, loop=0):
    v = k.nc.vector
    v.drain().then_inc(k.sums_ready, 1)
    dve_rstd(k, dve, i * 2 + 1, W)
    for t in range(0, KT, 2):
        for u in (t, t + 1):
            v.scalar_tensor_tensor(k.f[:, u, W], k.f[:, u, W], gain(u), k.rstd[:, W], ALU.mult, ALU.mult)
        dve.drain()
        for u in (t, t + 1):
            v.tensor_tensor(k.x[:, u, W], k.x[:, u, W], k.f[:, u, W], ALU.add).then_inc(k.x_ready, 1)
    v.memset(k.ssum[:, :], 0.0)
    if late is not None:
        split_lo(k, dve, Panel.of(late[0], loop), late[1])
    dve.drain()



def act_gate_up(k, act, i, start, W, nxt, loop=0):
    n = W.stop - W.start

    def one(t, p, ahead_size):
        act.wait_ge(k.panel_done, p.count(3))
        k.nc.scalar.activation(k.sig[:, p.par, W], k.acc[:, 2 * p.par, 0:n], ACT.Sigmoid).then_inc(k.sig_ready, 1)
        ahead(split_hi, k, act, p, ahead_size, GU_K)
        act.wait_ge(k.acc_free, p.count(3))
        k.nc.scalar.activation(k.a_hi[:, bass.ds(t, 1), W].rearrange("p a n -> p (a n)"), k.a_ff[:, p.par, W],
                               ACT.Copy).then_inc(k.ah_ready, 1)
    section(act, start, GU, one, loop, nxt)


def dve_gate_up(k, dve, i, start, W, nxt, loop=0):
    n = W.stop - W.start
    v = k.nc.vector

    def one(t, p, ahead_size):
        dve.wait_ge(k.sig_ready, i * FT + (t + 1))
        v.tensor_tensor(k.t_ff[:, p.par, W], k.sig[:, p.par, W], k.acc[:, 2 * p.par, 0:n], ALU.mult)
        dve.drain()
        v.tensor_tensor(k.a_ff[:, p.par, W], k.t_ff[:, p.par, W], k.acc[:, 2 * p.par + 1, 0:n],
                        ALU.mult).then_inc(k.acc_free, 1)
        ahead(split_lo, k, dve, p, ahead_size, GU_K)
        dve.drain()
        dve.wait_ge(k.ah_ready, i * FT + (t + 1))
        a = bass.ds(t, 1)
        v.tensor_tensor(k.a_lo[:, a, W].rearrange("p a n -> p (a n)"), k.a_ff[:, p.par, W],
                        k.a_hi[:, a, W].rearrange("p a n -> p (a n)").bitcast(F32),
                        ALU.subtract).then_inc(k.al_ready, 1)
    section(dve, start, GU, one, loop, nxt)


def act_ffn(k, act, i, gu, down, post, W, nxt, loop=0):
    act_gate_up(k, act, i, gu, W, (DOWN_K, DOWN_K), loop)
    act_products(k, act, post, down, 1, W, DOWN_K, nxt, loop)
    act_post_root(k, act, post, W)


def dve_ffn(k, dve, i, gu, down, post, W, gain, nxt, loop=0):
    dve_gate_up(k, dve, i, gu, W, (DOWN_K, DOWN_K), loop)
    dve_products(k, dve, post, down, 1, W, DOWN_K, nxt, loop)
    late = None if nxt[1] is None else (down + DOWN + 1, nxt[1])
    dve_post(k, dve, post, W, gain, late, loop)


def pe_ffn(k, pe, i, pre, gu, down, W, loop=0):
    pe_pre(k, pe, pre, W)
    pe_project(k, pe, gu, GU, 2, W, loop, ready=(k.hl_ready, pre * KT))
    pe_down(k, pe, down, W, i * FT, loop)
    pe_stat(k, pe, pre, W)



def act_ahead_only(k, act, start, count, size, nxt, loop=0):
    section(act, start, count, lambda t, p, s: ahead(split_hi, k, act, p, s, size), loop, nxt)


def act_copy_out(k, act, start, count, tiles, dst, n, size, nxt, loop=0, signal=None):
    def one(i, p, ahead_size):
        ahead(split_hi, k, act, p, ahead_size, size)
        act.wait_ge(k.panel_done, p.count(3))
        k.nc.scalar.activation(dst(i), k.acc[:, 2 * p.par:2 * p.par + tiles, 0:n], ACT.Copy).then_inc(k.acc_free, 1)
        if signal is not None:
            k.nc.scalar.drain().then_inc(signal, 1)
    section(act, start, count, one, loop, nxt)


def dve_copy_out(k, dve, start, count, tiles, dst, n, size, nxt, loop=0, signal=None):
    def one(i, p, ahead_size):
        dve.wait_ge(k.panel_done, p.count(3))
        k.nc.vector.tensor_copy(dst(i), k.acc[:, 2 * p.par:2 * p.par + tiles, 0:n]).then_inc(k.acc_free, 1)
        if signal is not None:
            k.nc.vector.drain().then_inc(signal, 1)
        ahead(split_lo, k, dve, p, ahead_size, size)
    section(dve, start, count, one, loop, nxt)



def dve_merge(k, dve, i, start, n, ga, gb, W, nxt, loop=0):
    v = k.nc.vector

    def one(t, p, ahead_size):
        dve.wait_ge(k.panel_done, p.count(3))
        v.tensor_tensor(k.upd[:, 0, 0:n], ga(t), k.acc[:, 2 * p.par, 0:n], ALU.mult)
        v.tensor_tensor(k.upd[:, 1, 0:n], gb(t), k.acc[:, 2 * p.par + 1, 0:n], ALU.mult).then_inc(k.acc_free, 1)
        dve.drain()
        v.tensor_tensor(k.sq_post[:, p.par, 0:n], k.upd[:, 0, 0:n], k.upd[:, 1, 0:n],
                        ALU.add).then_inc(k.merged, 1)
        ahead(split_lo, k, dve, p, ahead_size, AB_K)
        dve.drain()
        dve.wait_ge(k.yh_ready, i * KT + (t + 1))
        a = bass.ds(t, 1)
        v.tensor_tensor(k.h_lo[:, a, W].rearrange("p a n -> p (a n)"), k.sq_post[:, p.par, 0:n],
                        k.h_hi[:, a, W].rearrange("p a n -> p (a n)").bitcast(F32),
                        ALU.subtract).then_inc(k.yl_ready, 1)
    section(dve, start, AB, one, loop, nxt)


def act_merge(k, act, i, start, n, W, nxt, loop=0):
    def one(t, p, ahead_size):
        ahead(split_hi, k, act, p, ahead_size, AB_K)
        act.wait_ge(k.merged, i * KT + (t + 1))
        k.nc.scalar.activation(k.h_hi[:, bass.ds(t, 1), W].rearrange("p a n -> p (a n)"),
                               k.sq_post[:, p.par, 0:n], ACT.Copy).then_inc(k.yh_ready, 1)
    section(act, start, AB, one, loop, nxt)


def tile(a, i, cols=slice(None), rows=slice(0, P)):
    return a[rows, bass.ds(i, 1), cols].rearrange("p a n -> p (a n)")


def over(a, n, axis=1):
    return a.unsqueeze(axis).broadcast_to([a.shape[0], n, a.shape[1]])


HALVES = (slice(0, HD), slice(HD, P))




def att_transposed(k, h, i, n):
    if i < 4:
        bank, at = (k.mb[:, 0, :], k.acc[:, 3, :])[h], i * P
    else:
        bank, at = k.mb[:, 3, :], (2 * h + i - 4) * P
    return bank[:, at:at + n * P]


def pool_att(k, pool):
    k.nc.gpsimd.memset(k.kz[:, :, :, :], 0.0)
    k.nc.gpsimd.memset(k.vz[:, :, :, :, :], 0.0).then_inc(k.gates_ready, 1)
    rwkv_zero(k, k.nc.gpsimd, 1, ZEROED_LATE + ZEROED_EARLY)


def pe_att(k, pe):
    nc = k.nc
    ident = const(k, "ident")
    with pe.Fori(0, 2) as hp:
        pe.wait_ge(k.pv_evac, hp + 1)
        for g in range(3):
            for b in range(2):
                last = nc.tensor.matmul(k.mb[:, g, b * SEQ:(b + 1) * SEQ], const(k, "rot"),
                                        tile(k.qkv, hp + (b * 6 + 2 * g)), start=True, stop=True)
        last.then_inc(k.rot_done, 1)
        pe.wait_ge(k.q_copied, hp + 1)
        for g in range(2):
            for b in range(2):
                last = nc.tensor.transpose(k.mb[:, 3, (2 * g + b) * P:(2 * g + b + 1) * P],
                                           k.vs[:, g, b * P:(b + 1) * P], ident)
        last.then_inc(k.v_tok, 1)
        pe.wait_ge(k.att_ready, hp + 1)
        for b in range(2):
            last = nc.tensor.transpose(k.mb[:, 0, b * P:(b + 1) * P], k.vs[:, 2, b * P:(b + 1) * P], ident)
        last.then_inc(k.v_tok, 1)

        def scores(qb):
            n = (qb + 1) * P
            for h in range(2):
                pe.wait_ge(k.masked, hp * 4 + (2 * qb + h + 1))
                for g in range(3):
                    last = nc.tensor.matmul((k.mb, k.acc)[h][:, 1 + g // 2, (g % 2) * SEQ:(g % 2) * SEQ + n],
                                            k.qs[:, g, qb * P:(qb + 1) * P], k.kz[:, g, h, 0:n],
                                            start=True, stop=True)
                last.then_inc(k.scored, 1)
        scores(0)
        pe.wait_ge(k.v_evac, hp * 2 + 2)
        for qb in range(2):
            nb = 3 * (qb + 1)
            for h in range(2):
                pe.wait_ge(k.p_norm, hp * 4 + (2 * qb + h + 1))
                for i in range(nb):
                    g, b = divmod(i, qb + 1)
                    last = nc.tensor.transpose(att_transposed(k, h, i, 1), k.p_att[:, h, g, b * P:(b + 1) * P], ident)
                last.then_inc(k.p_tr, 1)
            if qb == 0:
                scores(1)
            for h in range(2):
                pe.wait_ge(k.pt_ready, hp * 4 + (2 * qb + h + 1))
                for i in range(nb):
                    g, b = divmod(i, qb + 1)
                    last = nc.tensor.matmul(k.acc[:, 0, qb * P:(qb + 1) * P], k.vz[:, g, b, h, :],
                                            k.pt_att[:, h, i, :], start=(h == 0 and i == 0),
                                            stop=(h == 1 and i == nb - 1))
                last.then_inc(k.pv_done, 1)


def act_att(k, act):
    nc = k.nc
    with act.Fori(0, 2) as hp:
        act.wait_ge(k.pv_evac, hp + 1)
        for g in range(3):
            last = nc.scalar.activation(k.vs[:, g, :], tile(k.qkv, hp + (12 + 2 * g)), ACT.Copy)
        last.then_inc(k.q_copied, 1)
        act.wait_ge(k.gates_ready, 1)
        act.wait_ge(k.v_tok, hp * 2 + 1)
        for h in range(2):
            src = k.mb[:, 3, :].rearrange("p (g b c) -> p (g b) c", g=2, b=2)[:, :, HALVES[h]]
            last = nc.scalar.activation(k.vz[:, 0:2, :, h, HALVES[h]].rearrange("p g b c -> p (g b) c"), src, ACT.Copy)
        last.then_inc(k.v_evac, 1)
        act.wait_ge(k.v_tok, hp * 2 + 2)
        for h in range(2):
            src = k.mb[:, 0, 0:2 * P].rearrange("p (b c) -> p b c", b=2)[:, :, HALVES[h]]
            last = nc.scalar.activation(k.vz[:, 2, :, h, HALVES[h]], src, ACT.Copy)
        last.then_inc(k.v_evac, 1)
        for qb in range(2):
            n = (qb + 1) * P
            nb = 3 * (qb + 1)
            for h in range(2):
                act.wait_ge(k.max_ready, hp * 4 + (2 * qb + h + 1))
                act.wait_ge(k.p_tr, hp * 4 + (2 * qb + h + 1))
                nc.scalar.activation(k.p_att[:, h, :, 0:n], k.s_att[:, h, :, 0:n], ACT.Exp,
                                     bias=k.st_att[:, h, 0:1], accum_out=k.st_att[:, h, 1:2]).then_inc(k.p_ready, 1)
            act.wait_ge(k.p_tr, hp * 4 + (2 * qb + 4))
            for h in range(2):
                act.wait_ge(k.pv_done, hp * 4 + (2 * qb + h + 1))
                last = nc.scalar.activation(k.pt_att[:, h, 0:min(nb, 4), :],
                                            att_transposed(k, h, 0, min(nb, 4)).rearrange("p (i c) -> p i c", c=P),
                                            ACT.Copy)
                if nb > 4:
                    last = nc.scalar.activation(k.pt_att[:, h, 4:nb, :],
                                                att_transposed(k, h, 4, nb - 4).rearrange("p (i c) -> p i c", c=P),
                                                ACT.Copy)
                last.then_inc(k.pt_ready, 1)


def dve_att(k, dve):
    v = k.nc.vector
    mask = const(k, "mask_att").rearrange("p (g n) -> p g n", g=3)
    dve.wait_ge(k.gates_ready, 1)
    with dve.Fori(0, 2) as hp:
        dve.drain()
        dve.wait_ge(k.rot_done, hp + 1)
        for g in range(3):
            for b in range(2):
                rt1, rt2 = k.rt1[:, b, :], k.rt2[:, b, :]
                v.tensor_tensor(rt1, tile(k.qkv, hp + (b * 6 + 2 * g)), const(k, "cos"), ALU.mult)
                v.tensor_tensor(rt2, k.mb[:, g, b * SEQ:(b + 1) * SEQ], const(k, "sin"), ALU.mult)
                dve.drain()
                if b == 0:
                    last = v.tensor_tensor(k.qs[:, g, :], rt1, rt2, ALU.add)
                else:
                    for h, rows in enumerate(HALVES):
                        last = v.tensor_tensor(k.kz[rows, g, h, :], rt1[rows], rt2[rows], ALU.add)
        last.then_inc(k.att_ready, 1)
        for qb in range(2):
            n = (qb + 1) * P
            cols = slice((1 - qb) * P, 2 * P)
            for h in range(2):
                bank = (k.mb, k.acc)[h]
                dve.wait_ge(k.scored, hp * 4 + (2 * qb + h + 1))
                v.scalar_tensor_tensor(k.s_att[:, h, 0:2, 0:n],
                                       bank[:, 1, :].rearrange("p (g n) -> p g n", g=2)[:, :, 0:n], HD ** -0.5,
                                       mask[:, 0:2, cols], ALU.mult, ALU.add)
                v.scalar_tensor_tensor(k.s_att[:, h, 2, 0:n], bank[:, 2, 0:n], HD ** -0.5, mask[:, 2, cols],
                                       ALU.mult, ALU.add).then_inc(k.masked, 1)
                dve.drain()
                v.tensor_reduce(k.st_att[:, h, 0:1], k.s_att[:, h, :, 0:n], mybir.AxisListType.XY, ALU.max,
                                negate=True).then_inc(k.max_ready, 1)
            for h in range(2):
                dve.wait_ge(k.p_ready, hp * 4 + (2 * qb + h + 1))
                v.reciprocal(k.st_att[:, h, 2:3], k.st_att[:, h, 1:2])
                dve.drain()
                v.tensor_scalar(k.p_att[:, h, :, 0:n], k.p_att[:, h, :, 0:n], k.st_att[:, h, 2:3], None,
                                ALU.mult).then_inc(k.p_norm, 1)
        dve.wait_ge(k.pv_done, hp * 4 + 6)
        v.tensor_copy(tile(k.yb_keep, hp), k.acc[:, 0, 0:SEQ]).then_inc(k.pv_evac, 1)



def pool_shift(k, pool):
    g = k.nc.gpsimd
    with pool.Fori(0, SHIFT_TILES // 2) as i:
        pool.wait_ge(k.pin_ready, i + 1)
        two = bass.ds(i * 2, 2)
        g.tensor_tensor(k.c1[:, 0:2, :], k.p_in[:, two, 0:SEQ], k.p_in[:, two, 1:SEQ + 1], ALU.subtract)
        pool.drain()
        mu = k.vec[:, bass.ds(i * 2 + VEC["mu"][0], 2)].unsqueeze(2).broadcast_to([P, 2, SEQ])
        g.tensor_tensor(k.c1[:, 0:2, :], k.c1[:, 0:2, :], mu, ALU.mult)
        pool.drain()
        g.tensor_tensor(k.p_in[:, two, 1:SEQ + 1], k.p_in[:, two, 1:SEQ + 1], k.c1[:, 0:2, :], ALU.add)
        pool.drain()


def pool_rwkv(k, pool, d):
    g = k.nc.gpsimd
    g.dma_start(k.w2p[:, :], d["w2"]).then_inc(k.lora_loaded, 16)
    g.dma_start(k.a2p[:, :], d["a2"]).then_inc(k.lora_loaded, 16)
    g.dma_start(k.g2[:, :], d["g2"]).then_inc(k.lora_loaded, 16)
    g.dma_start(k.sel[:, :], d["sel"]).then_inc(k.lora_loaded, 16)
    g.dma_start(k.spread[:, :], d["spread"]).then_inc(k.lora_loaded, 16)
    rwkv_zero(k, g, 0, ZEROED_EARLY)
    g.memset(k.reset[:, :], 1.0)
    pool.drain()
    g.memset(k.reset[:, 0:SEQ:CHUNK], 0.0).then_inc(k.t_ready, 1)


def pe_pair_sums(k, pe, ready, src, done):
    pe.wait_ge(ready, 1)
    s = src[:, :, :].rearrange("p t n -> p (t n)")
    for b in range(3):
        last = k.nc.tensor.matmul(k.mb[:, b, :], const(k, "pair_ones"), s[:, b * 512:(b + 1) * 512],
                                  start=True, stop=True)
    last.then_inc(done, 1)


def pe_head_sums(k, pe, ready, src, done):
    pe.wait_ge(ready, 1)
    for c in range(RT):
        last = k.nc.tensor.matmul(k.acc[0:32, 3, 0:SEQ], k.sel[:, c * 32:(c + 1) * 32], src[:, c, :],
                                  start=c == 0, stop=c == RT - 1)
    last.then_inc(done, 1)


def pe_head_spread(k, pe, ready, done):
    pe.wait_ge(ready, 1)
    for c in range(RT):
        last = k.nc.tensor.matmul(k.acc[:, c // 2, (c % 2) * SEQ:(c % 2 + 1) * SEQ],
                                  k.spread[:, c * P:(c + 1) * P], k.per_head[:, :], start=True, stop=True)
    last.then_inc(done, 1)


def three_banks(bank):
    return bank[:, 0:3, :].rearrange("p b (t n) -> p b t n", t=2)


def pe_rwkv_prep(k, pe):
    mm = k.nc.tensor.matmul
    x = slice(1, SEQ + 1)
    pe.wait_ge(k.lora_loaded, 80)
    pe_head_sums(k, pe, k.kk_sq, k.tmp, k.kk_sum)
    pe.wait_ge(k.wg_ready, 1)
    for c in range(RT):
        b, cols = 2 * (c % 2), slice(c * P, (c + 1) * P)
        if c >= 2:
            pe.wait_ge(k.lora_evac, c - 1)
        mm(k.mb[:, b, 0:SEQ], k.w2p[:, cols], k.p_in[:, T_WA, x], start=True, stop=True)
        mm(k.mb[:, b, SEQ:2 * SEQ], k.a2p[:, cols], k.p_in[:, T_WA, x], start=True, stop=True)
        mm(k.mb[:, b + 1, 0:SEQ], k.g2[:, cols], k.p_in[:, T_G, x], start=True, stop=True).then_inc(k.lora_mm, 1)
    pe_head_spread(k, pe, k.kk_inv, k.kk_spread)
    pe.wait_ge(k.lora_evac, RT)
    pe_pair_sums(k, pe, k.bon_in, k.c1, k.bon_sum)


def act_rwkv_prep(k, act):
    a = k.nc.scalar.activation
    x = slice(1, SEQ + 1)
    for t in range(RT):
        last = a(k.tmp[:, t, :], k.p_in[:, T_K + t, x], ACT.Square, scale=vec(k, "k_k", t))
    last.then_inc(k.kk_sq, 1)
    a(k.p_in[0:HD, T_WA, x], k.p_in[0:HD, T_WA, x], ACT.Tanh)
    for t in range(RT):
        a(k.kk[:, t, :], k.p_in[:, T_K + t, x], ACT.Copy, scale=vec(k, "k_k", t))
    act.wait_ge(k.kk_sum, 1)
    a(k.per_head[:, :], k.acc[0:32, 3, 0:SEQ], ACT.Sqrt).then_inc(k.kk_root, 1)
    a(k.p_in[:, T_G, x], k.p_in[:, T_G, x], ACT.Sigmoid).then_inc(k.wg_ready, 1)
    for c in range(RT):
        b = 2 * (c % 2)
        act.wait_ge(k.lora_mm, c + 1)
        a(k.sw[:, c, :], k.mb[:, b, 0:SEQ], ACT.Sigmoid, bias=vec(k, "w0", c))
        a(k.beta[:, c, :], k.mb[:, b, SEQ:2 * SEQ], ACT.Sigmoid, bias=vec(k, "a0", c))
        a(k.gate[:, c, :], k.mb[:, b + 1, 0:SEQ], ACT.Copy).then_inc(k.lora_evac, 1)
    act.wait_ge(k.c_ready, 1)
    a(k.bon[:, :, :], k.c1[:, :, :], ACT.Exp, scale=DECAY).then_inc(k.exp_ready, 1)
    a(k.tmp[:, :, :], k.c1[:, :, :], ACT.Exp, scale=-DECAY).then_inc(k.exp_ready, 1)
    a(k.sw[:, :, :], k.sw[:, :, :], ACT.Exp, scale=-DECAY).then_inc(k.exp_ready, 1)


def dve_rwkv_prep(k, dve):
    v = k.nc.vector
    x = slice(1, SEQ + 1)
    tt = v.tensor_tensor
    pk, pr, pv = (k.p_in[:, t:t + RT, x] for t in (T_K, T_R, T_V))
    kk, tmp, kap, a, c1, sw = (b[:, :, :] for b in (k.kk, k.tmp, k.kap, k.beta, k.c1, k.sw))
    dve.wait_ge(k.kk_root, 1)
    v.tensor_scalar_max(k.per_head[:, :], k.per_head[:, :], 1e-12)
    dve.drain()
    v.reciprocal(k.per_head[:, :], k.per_head[:, :]).then_inc(k.kk_inv, 1)
    dve.wait_ge(k.lora_evac, RT)
    dve.wait_ge(k.t_ready, 1)
    for t in range(RT):
        v.tensor_tensor_scan(k.c1[:, t, :], k.reset[:, :], k.sw[:, t, :], 0.0, ALU.mult, ALU.add)
    for t in range(RT):
        v.tensor_scalar(k.kap[:, t, :], k.beta[:, t, :], -1.0, vec(k, "k_a", t), ALU.add, ALU.mult)
    dve.drain()
    tt(sw, c1, sw, ALU.subtract).then_inc(k.c_ready, 1)
    dve.wait_ge(k.kk_spread, 1)
    kk4 = kk.rearrange("p (b t) n -> p b t n", b=3)
    tt(kk4, kk4, three_banks(k.acc), ALU.mult)
    for t in range(RT):
        v.scalar_tensor_tensor(k.kap[:, t, :], k.kap[:, t, :], 1.0, k.p_in[:, T_K + t, x], ALU.add, ALU.mult)
    dve.drain()
    tt(a, a, kk, ALU.mult)
    dve.drain()
    dve.wait_ge(k.exp_ready, 1)
    tt(a, a, k.bon[:, :, :], ALU.mult)
    dve.wait_ge(k.exp_ready, 2)
    for t in range(RT):
        last = v.scalar_tensor_tensor(k.c1[:, t, :], k.p_in[:, T_R + t, x], vec(k, "r_k", t), k.kap[:, t, :],
                                      ALU.mult, ALU.mult)
    last.then_inc(k.bon_in, 1)
    v.tensor_copy(k.pc[:, :, :], k.tmp[:, :, CHUNK - 1:SEQ:CHUNK])
    dve.wait_ge(k.exp_ready, 3)
    tt(pk, kk, sw, ALU.mult)
    dve.drain()
    tt(kap, kap, k.bon[:, :, :], ALU.mult)
    tt(pr, pr, tmp, ALU.mult)
    dve.drain()
    dve.wait_ge(k.bon_sum, 1)
    for b in range(3):
        tt(k.bon[:, 2 * b:2 * b + 2, :], k.p_in[:, T_V + 2 * b:T_V + 2 * b + 2, x],
           k.mb[:, b, :].rearrange("p (t n) -> p t n", t=2), ALU.mult)
    dve.drain()



STREAMS = (0, 1)


def nth(j, per, idx, s):
    return j * (2 * per) + (2 * idx + s + 1)


ZEROED_EARLY = ("m_bd", "s_bd")
ZEROED_LATE = ("al_bd", "be_bd", "ka_bd", "v_bd", "x_bd", "xt_bd", "rt_bd", "akt_bd", "w_bd", "u_bd")
ZEROED_BY_POOL = 5


def rwkv_zero(k, engine, s, names):
    for name in names:
        last = engine.memset(k.m[s][name][:, :, :], 0.0)
    last.then_inc(k.arr_ready, 1)


def chunks(a):
    return a.rearrange("p (c t) -> p c t", c=NCH)


def pool_rwkv_pairs(k, pool):
    with pool.Fori(0, RT // 2) as j:
        for s in STREAMS:
            pair = j * 2 + s
            pool.wait_ge(k.tok_mm, nth(j, 4, 3, s))
            x = slice(1, SEQ + 1)
            for h, rows in enumerate(HALVES):
                for name, src in (("al_bd", tile(k.p_in, pair + T_K, x, rows)),
                                  ("be_bd", tile(k.beta, pair, rows=rows))):
                    last = k.nc.gpsimd.tensor_copy(k.m[s][name][rows, :, HALVES[h]], chunks(src))
            last.then_inc(k.bd_pool, 1)


ROUNDS = 6


def pe_rwkv_pairs(k, pe):
    nc = k.nc
    mm = nc.tensor.matmul
    ident = const(k, "ident")
    half = CHUNK
    banks = (k.mb, k.acc)

    def c_(c, n=P):
        return slice(c * n, (c + 1) * n)
    with pe.Fori(0, RT // 2) as j:
        for s in STREAMS:
            m, bank, pair = k.m[s], banks[s], j * 2 + s
            pe.wait_ge(k.bd_pool, nth(j, 1, 0, s))
            pe.wait_ge(k.bd_act, nth(j, 1, 0, s))
            pe.wait_ge(k.y_evac, nth(j, 1, 0, s))
            for c in range(NCH):
                both = k.p_in[:, bass.ds(pair, 2, 6), 1 + c * half:1 + (c + 1) * half]
                mm(bank[:, 0, c_(c)], m["be_bd"][:, c, :], both, start=True, stop=True)
                mm(bank[:, 1, c_(c)], m["ka_bd"][:, c, :], both, start=True, stop=True)
                last = mm(bank[:, 2, c_(c, half)], m["al_bd"][:, c, :], tile(k.beta, pair, c_(c, half)),
                          start=True, stop=True)
            last.then_inc(k.gram, 1)
        for i, name in enumerate(("al_bd", "be_bd", "ka_bd", "v_bd")):
            for s in STREAMS:
                if i == 1:
                    pe.wait_ge(k.gram_evac, nth(j, 1, 0, s))
                for c in range(NCH):
                    last = nc.tensor.transpose(banks[s][:, (3, 0, 1, 2)[i], c_(c)], k.m[s][name][:, c, :], ident)
                last.then_inc(k.tok_mm, 1)
        for s in STREAMS:
            m, bank = k.m[s], banks[s]
            pe.wait_ge(k.tok_evac, nth(j, 1, 0, s))
            pe.wait_ge(k.tok_act, nth(j, 1, 0, s))
            for c in range(NCH):
                last = mm(bank[:, 3, c_(c, half)], m["akt_bd"][:, c, :], m["vt_st"][:, c, :], start=True, stop=True)
            last.then_inc(k.u0_mm, 1)
        for r in range(ROUNDS):
            for s in STREAMS:
                m, bank = k.m[s], banks[s]
                if r == 0:
                    pe.wait_ge(k.xbd_ready, nth(j, 1, 0, s))
                else:
                    pe.wait_ge(k.round_act, nth(j, ROUNDS - 1, r - 1, s))
                    pe.wait_ge(k.round_evac, nth(j, ROUNDS, r - 1, s))
                for c in range(NCH):
                    if r < ROUNDS - 1:
                        mm(bank[:, 0, c_(c, half)], m["xt_bd"][:, c, :], m["x_st"][:, c, :], start=True, stop=True)
                    lo = half if r == ROUNDS - 1 else 0
                    hi = half if r == 0 else P
                    last = mm(bank[:, 1, c * P + lo:c * P + hi], m["x_bd"][:, c, :], m["xr"][:, c, lo:hi],
                              start=True, stop=True)
                last.then_inc(k.round_mm, 1)
        for s in STREAMS:
            m, bank = k.m[s], banks[s]
            pe.wait_ge(k.round_evac, nth(j, ROUNDS, ROUNDS - 1, s))
            pe.wait_ge(k.u0_evac, nth(j, 1, 0, s))
            for c in range(NCH):
                mm(bank[:, 2, c_(c, half)], m["rt_bd"][:, c, :], m["au"][:, c, 0:half], start=True, stop=True)
                last = mm(bank[:, 3, c_(c, half)], m["rt_bd"][:, c, :], m["au"][:, c, half:P], start=True, stop=True)
            last.then_inc(k.wu_mm, 1)
        for s in STREAMS:
            m, bank = k.m[s], banks[s]
            pe.wait_ge(k.wu_evac, nth(j, 1, 0, s))
            pe.wait_ge(k.rt_copied, nth(j, 1, 0, s))
            for c in range(NCH):
                if c < NCH - 1:
                    mm(bank[:, 0, c_(c, half)], m["w_bd"][:, c, :], m["bet_st"][:, c, :], start=True, stop=True)
                    mm(bank[:, 2, c_(c, half)], m["kat_bd"][:, c, :], m["vt_st"][:, c, :], start=True, stop=False)
                    mm(bank[:, 2, c_(c, half)], m["bet_bd"][:, c, :], m["u_st"][:, c, :], start=False, stop=True)
                last = mm(bank[:, 1, c_(c, half)], m["w_bd"][:, c, :], m["qbt"][:, c, :], start=True, stop=True)
            last.then_inc(k.mfn_mm, 1)
        for c in range(2):
            for s in STREAMS:
                m, bank = k.m[s], banks[s]
                if c == 0:
                    pe.wait_ge(k.mfn_evac, nth(j, 1, 0, s))
                pe.wait_ge(k.chain_evac, nth(j, 3, c, s))
                before = m["n_st"][:, 0, :] if c == 0 else m["s_st"][:, :]
                mm(bank[:, 3, 0:half], m["m_bd"][:, c + 1, :], before, start=True, stop=True).then_inc(k.chain_mm, 1)
        for s in STREAMS:
            m, bank = k.m[s], banks[s]
            pe.wait_ge(k.chain_evac, nth(j, 3, 2, s))
            for c in range(NCH):
                out = bank[:, 0, c_(c, half)]
                mm(out, m["u_bd"][:, c, :], m["qbt"][:, c, :], start=True, stop=False)
                last = mm(out, m["vt_bd"][:, c, :], m["qkt"][:, c, :], start=False, stop=c == 0)
                if c > 0:
                    last = mm(out, m["s_bd"][:, c - 1, :], m["f_st"][:, c, :], start=False, stop=True)
            last.then_inc(k.y_mm, 1)


def act_rwkv_pairs(k, act):
    a = k.nc.scalar.activation
    half = CHUNK
    banks = (k.mb, k.acc)

    def blocks(s, bank, n):
        return banks[s][:, bank, 0:NCH * n].rearrange("p (c n) -> p c n", c=NCH)

    def bd(s, name, src):
        for h, rows in enumerate(HALVES):
            r = a(k.m[s][name][rows, :, HALVES[h]], src[rows, :, 0:half], ACT.Copy)
        return r

    def st(dst, src, scale=1.0):
        for h, rows in enumerate(HALVES):
            r = a(dst[rows], src[rows, :, HALVES[h]], ACT.Copy, scale=scale)
        return r
    act.wait_ge(k.arr_ready, 4)
    with act.Fori(0, RT // 2) as j:
        for s in STREAMS:
            m, pair = k.m[s], j * 2 + s
            act.wait_ge(k.tok_mm, nth(j, 4, 3, s))
            for h, rows in enumerate(HALVES):
                a(m["ka_bd"][rows, :, HALVES[h]], chunks(tile(k.kap, pair, rows=rows)), ACT.Copy)
                last = a(m["v_bd"][rows, :, HALVES[h]], chunks(tile(k.p_in, pair + T_V, slice(1, SEQ + 1), rows)),
                         ACT.Copy)
            last.then_inc(k.bd_act, 1)
        for s in STREAMS:
            m = k.m[s]
            act.wait_ge(k.tok_mm, nth(j, 4, 0, s) + 8)
            st(m["au"][:, :, 0:half], blocks(s, 3, P), scale=-1.0)
            act.wait_ge(k.gram_evac, nth(j, 1, 0, s))
            bd(s, "x_bd", m["x_st"])
            bd(s, "xt_bd", m["xr"]).then_inc(k.xbd_ready, 1)
        for s in STREAMS:
            m = k.m[s]
            act.wait_ge(k.tok_mm, nth(j, 4, 1, s) + 8)
            a(m["bet_bd"][:, :, :], blocks(s, 0, P), ACT.Copy)
            st(m["bet_st"][:, :, :], blocks(s, 0, P)).then_inc(k.tok_act, 1)
        for r in range(ROUNDS - 1):
            for s in STREAMS:
                act.wait_ge(k.round_mm, nth(j, ROUNDS, r, s))
                if r < ROUNDS - 2:
                    a(k.m[s]["x_st"][:, :, :], blocks(s, 0, half), ACT.Copy)
                bd(s, "x_bd", blocks(s, 0, half)).then_inc(k.round_act, 1)
        for s in STREAMS:
            act.wait_ge(k.wu_mm, nth(j, 1, 0, s))
            bd(s, "w_bd", blocks(s, 2, half)).then_inc(k.wu_evac, 1)
        for s in STREAMS:
            pair = j * 2 + s
            act.wait_ge(k.mfn_mm, nth(j, 1, 0, s))
            for c in range(NCH - 1):
                last = a(k.m[s]["n_st"][:, c, :], banks[s][:, 2, c * half:(c + 1) * half], ACT.Copy,
                         scale=k.pc[:, bass.ds(pair, 1), c:c + 1].rearrange("p a n -> p (a n)"))
            last.then_inc(k.mfn_evac, 1)


def dve_rwkv_pairs(k, dve):
    v = k.nc.vector
    half = CHUNK
    banks = (k.mb, k.acc)
    ui, us, ls, i2 = (const(k, n) for n in ("up_incl", "up_strict", "lo_strict", "i2"))
    stt, tt = v.scalar_tensor_tensor, v.tensor_tensor

    def blocks(s, bank, n):
        return banks[s][:, bank, 0:NCH * n].rearrange("p (c n) -> p c n", c=NCH)

    def st(dst, src):
        for h, rows in enumerate(HALVES):
            r = v.tensor_copy(dst[rows], src[rows, :, HALVES[h]])
        return r
    rwkv_zero(k, v, 0, ZEROED_LATE[ZEROED_BY_POOL:])
    dve.drain()
    dve.wait_ge(k.arr_ready, 4)
    with dve.Fori(0, RT // 2) as j:
        for s in STREAMS:
            m = k.m[s]
            dve.wait_ge(k.gram, nth(j, 1, 0, s))
            stt(m["xr"][:, :, 0:half], blocks(s, 0, P)[:, :, half:P], -1.0, over(us, NCH), ALU.mult, ALU.mult)
            stt(m["x_st"][:, :, :], blocks(s, 2, half), -1.0, over(ls, NCH), ALU.mult, ALU.mult)
            tt(m["qbt"][:, :, :], blocks(s, 0, P)[:, :, 0:half], over(ui, NCH), ALU.mult)
            tt(m["qkt"][:, :, :], blocks(s, 1, P)[:, :, 0:half], over(ui, NCH), ALU.mult)
            for h, rows in enumerate(HALVES):
                last = tt(m["akt_bd"][rows, :, HALVES[h]], blocks(s, 1, P)[rows, :, half:P], over(us[rows], NCH),
                          ALU.mult)
            last.then_inc(k.gram_evac, 1)
        dve.drain()
        for s in STREAMS:
            m = k.m[s]
            tt(m["xr"][:, :, half:P], m["xr"][:, :, 0:half], over(i2, NCH), ALU.add)
        for s in STREAMS:
            m = k.m[s]
            dve.wait_ge(k.tok_mm, nth(j, 4, 3, s) + 8)
            st(m["vt_st"][:, :, :], blocks(s, 2, P))
            v.tensor_copy(m["kat_bd"][:, :, :], blocks(s, 1, P))
            v.tensor_copy(m["vt_bd"][:, :, :], blocks(s, 2, P)).then_inc(k.tok_evac, 1)
        for s in STREAMS:
            dve.wait_ge(k.u0_mm, nth(j, 1, 0, s))
            v.tensor_scalar(k.m[s]["au"][:, :, half:P], blocks(s, 3, half), -1.0, None,
                            ALU.mult).then_inc(k.u0_evac, 1)
        for r in range(ROUNDS):
            for s in STREAMS:
                m = k.m[s]
                dve.wait_ge(k.round_mm, nth(j, ROUNDS, r, s))
                src = blocks(s, 1, P)
                if r < ROUNDS - 1:
                    if r < ROUNDS - 2:
                        v.tensor_copy(m["xr"][:, :, 0:half], src[:, :, 0:half])
                        for h, rows in enumerate(HALVES):
                            last = v.tensor_copy(m["xt_bd"][rows, :, HALVES[h]], src[rows, :, 0:half])
                    if r > 0:
                        last = tt(m["xr"][:, :, half:P], m["xr"][:, :, half:P], src[:, :, half:P], ALU.add)
                else:
                    for h, rows in enumerate(HALVES):
                        last = tt(m["rt_bd"][rows, :, HALVES[h]], m["xr"][rows, :, half:P], src[rows, :, half:P],
                                  ALU.add)
                last.then_inc(k.round_evac, 1)
            dve.drain()
        for s in STREAMS:
            m = k.m[s]
            dve.wait_ge(k.wu_mm, nth(j, 1, 0, s))
            v.tensor_copy(m["u_st"][:, :, :], blocks(s, 3, half))
            for h, rows in enumerate(HALVES):
                last = v.tensor_copy(m["u_bd"][rows, :, HALVES[h]], blocks(s, 3, half)[rows])
            last.then_inc(k.rt_copied, 1)
        for s in STREAMS:
            m, pair = k.m[s], j * 2 + s
            dve.wait_ge(k.mfn_mm, nth(j, 1, 0, s))
            for h, rows in enumerate(HALVES):
                tt(m["m_bd"][rows, 0:NCH - 1, HALVES[h]], blocks(s, 0, half)[rows, 0:NCH - 1],
                   over(i2[rows], NCH - 1), ALU.add)
            tt(m["f_st"][:, :, :], blocks(s, 1, half), chunks(tile(k.p_in, pair + T_R, slice(1, SEQ + 1))),
               ALU.add).then_inc(k.chain_evac, 1)

        def state(s, c, src):
            for h, rows in enumerate(HALVES):
                r = v.tensor_copy(k.m[s]["s_bd"][rows, c, HALVES[h]], src[rows])
            return r
        for s in STREAMS:
            dve.wait_ge(k.mfn_evac, nth(j, 1, 0, s))
            state(s, 0, k.m[s]["n_st"][:, 0, :])
        for c in (1, 2):
            for s in STREAMS:
                m, pair = k.m[s], j * 2 + s
                dve.wait_ge(k.chain_mm, nth(j, 2, c - 1, s))
                stt(m["s_st"][:, :], banks[s][:, 3, 0:half],
                    k.pc[:, bass.ds(pair, 1), c:c + 1].rearrange("p a n -> p (a n)"), m["n_st"][:, c, :],
                    ALU.mult, ALU.add)
            dve.drain()
            for s in STREAMS:
                state(s, c, k.m[s]["s_st"][:, :]).then_inc(k.chain_evac, 1)
        for s in STREAMS:
            dve.wait_ge(k.y_mm, nth(j, 1, 0, s))
            v.tensor_copy(tile(k.c1, j * 2 + s), banks[s][:, 0, 0:SEQ]).then_inc(k.y_evac, 1)


def pe_rwkv_out(k, pe):
    pe_pair_sums(k, pe, k.gn_in, k.c1, k.gn_sum)
    pe_head_sums(k, pe, k.gn_sq, k.tmp, k.gn_sum)
    pe_head_spread(k, pe, k.gn_inv, k.gn_spread)


def act_rwkv_out(k, act):
    a = k.nc.scalar.activation
    act.wait_ge(k.y_evac, RT + 2)
    prologue(split_hi, k, act, M_AB1, AB_K)
    act.wait_ge(k.gn_sum, 2)
    a(k.per_head[:, :], k.acc[0:32, 3, 0:SEQ], ACT.Sqrt, bias=k.eps[0:32, 1:2],
      scale=1.0 / HD).then_inc(k.gn_root, 1)
    act.wait_ge(k.gn_norm, 1)
    for t in range(RT):
        last = a(k.c1[:, t, :], k.c1[:, t, :], ACT.Identity, bias=vec(k, "lnx_b", t), scale=vec(k, "lnx_w", t))
    last.then_inc(k.gn_affine, 1)
    act.wait_ge(k.gn_root, 2)
    a(k.y1_hi[:, 0:RT, :], k.c1[:, :, :], ACT.Copy)
    a(k.y1_hi[:, RT:KT, :], k.yb_keep[:, :, :], ACT.Copy).then_inc(k.gn_root, 1)


def dve_rwkv_out(k, dve):
    v = k.nc.vector
    tt = v.tensor_tensor
    c1 = k.c1[:, :, :]
    v.drain().then_inc(k.gn_in, 1)
    prologue(split_lo, k, dve, M_AB1, AB_K)
    dve.wait_ge(k.gn_sum, 1)
    flat3 = c1.rearrange("p t n -> p (t n)").rearrange("p (b n) -> p b n", b=3)
    v.scalar_tensor_tensor(flat3, k.mb[:, 0:3, :], -1.0 / HD, flat3, ALU.mult, ALU.add)
    dve.drain()
    tt(k.tmp[:, :, :], c1, c1, ALU.mult).then_inc(k.gn_sq, 1)
    dve.wait_ge(k.gn_root, 1)
    v.reciprocal(k.per_head[:, :], k.per_head[:, :]).then_inc(k.gn_inv, 1)
    dve.wait_ge(k.gn_spread, 1)
    c4 = c1.rearrange("p (b t) n -> p b t n", b=3)
    tt(c4, c4, three_banks(k.acc), ALU.mult).then_inc(k.gn_norm, 1)
    dve.wait_ge(k.gn_affine, 1)
    tt(c1, c1, k.bon[:, :, :], ALU.add)
    dve.drain()
    tt(c1, c1, k.gate[:, :, :], ALU.mult)
    dve.drain().then_inc(k.gn_root, 1)
    dve.wait_ge(k.gn_root, 3)
    tt(k.y1_lo[:, 0:RT, :], c1, k.y1_hi[:, 0:RT, :].bitcast(F32), ALU.subtract)
    tt(k.y1_lo[:, RT:KT, :], k.yb_keep[:, :, :], k.y1_hi[:, RT:KT, :].bitcast(F32), ALU.subtract)
    dve.drain()



FF_ROWS = slice(32, 40)


def pe_gates2(k, pe, l):
    pe.wait_ge(k.dec_in, l * 16 + 16)
    for t in range(2):
        last = k.nc.tensor.matmul(k.mb[:, t, 0:TOK], k.wal[:, t * P:(t + 1) * P], k.small[:, :], start=True, stop=True)
    last.then_inc(k.dec_mm, 1)



def act_gates2_step(k, act, l, step):
    a = k.nc.scalar.activation
    s = 1.0 / 16.0
    if step == 0:
        a(k.lf[0:8, :], k.small[FF_ROWS, :], ACT.Abs, bias=vec(k, "b_f", layer=l, rows=FF_ROWS))
        act.wait_ge(k.dec_mm, l + 1)
        for t in range(2):
            a(k.e1[:, t, :], k.mb[:, t, 0:TOK], ACT.Abs, bias=vec(k, "b_alpha", t, l))
        act.drain().then_inc(k.dec_abs, 1)
    elif step == 1:
        a(k.lf[0:8, :], k.lf[0:8, :], ACT.Exp, scale=-1.0)
        a(k.e1[:, :, :], k.e1[:, :, :], ACT.Exp, scale=-1.0)
        act.drain()
    elif step == 2:
        a(k.lf[0:8, :], k.lf[0:8, :], ACT.Ln, bias=1.0)
        a(k.e1[:, :, :], k.e1[:, :, :], ACT.Ln, bias=1.0).then_inc(k.dec_exp, 1)
    elif step == 3:
        a(k.gr_[:, :, :], k.p2[:, T_GR:T_GR + 4, :], ACT.Sigmoid)
    elif step == 6:
        act.wait_ge(k.gz_ready, l + 1)
        a(k.e1[:, :, :], k.e2[:, :, :], ACT.Exp, scale=s)
        a(k.gst[:, :, :, :], k.gst[:, :, :, :], ACT.Exp, scale=s)
        act.drain()
        a(k.e2[:, :, :], k.e2[:, :, :], ACT.Exp, scale=-s).then_inc(k.gexp_ready, 1)


def dve_gates2_step(k, dve, l, step):
    v = k.nc.vector
    if step == 1:
        v.tensor_scalar(k.cum[0:8, :], k.small[FF_ROWS, :], vec(k, "b_f", layer=l, rows=FF_ROWS), 0.0, ALU.add,
                        ALU.min)
        dve.wait_ge(k.dec_abs, l + 1)
        for t in range(2):
            v.tensor_scalar(k.gcum[:, t, :], k.mb[:, t, 0:TOK], vec(k, "b_alpha", t, l), 0.0, ALU.add, ALU.min)
        v.memset(k.e2[:, :, :], 1.0)
        dve.drain()
    elif step == 3:
        dve.wait_ge(k.dec_exp, l + 1)
        v.tensor_tensor(k.lf[0:8, :], k.cum[0:8, :], k.lf[0:8, :], ALU.subtract)
        v.tensor_tensor(k.e1[:, :, :], k.gcum[:, :, :], k.e1[:, :, :], ALU.subtract)
        dve.drain()
        v.tensor_tensor_scan(k.cum[0:8, :], k.e2[0:8, 0, :], k.lf[0:8, :], 0.0, ALU.mult, ALU.add)
        dve.drain()
        v.memset(k.e2[:, :, 0:TOK:GLA_C], 0.0)
        dve.drain()
    elif step == 4:
        for t in range(2):
            v.tensor_tensor_scan(k.gcum[:, t, :], k.e2[:, t, :], k.e1[:, t, :], 0.0, ALU.mult, ALU.add)
        dve.drain()
    elif step == 5:
        for t in range(2):
            g = k.gcum[:, t, :].rearrange("p (n c) -> p n c", n=GLA_N)
            mid = g[:, :, GLA_C // 2:GLA_C // 2 + 1]
            v.tensor_tensor(k.e2[:, t, :].rearrange("p (n c) -> p n c", n=GLA_N), g,
                            mid.broadcast_to([P, GLA_N, GLA_C]), ALU.subtract)
            v.tensor_copy(k.gst[:, t, 0, :], mid.rearrange("p n c -> p (n c)"))
            v.tensor_copy(k.gst[:, t, 1, :], g[:, :, GLA_C - 1:GLA_C].rearrange("p n c -> p (n c)"))
            v.tensor_tensor(k.gst[:, t, 2, :], g[:, :, GLA_C - 1:GLA_C].rearrange("p n c -> p (n c)"),
                            mid.rearrange("p n c -> p (n c)"), ALU.subtract)
        dve.drain()
        v.tensor_scalar(k.e2[:, :, :], k.e2[:, :, :], 80.0 * 16, -80.0 * 16, ALU.min, ALU.max).then_inc(k.gz_ready, 1)
    elif step == 6:
        eye = const(k, "eye8", slice(0, 8))
        v.memset(k.minus8[:, :], -float(HD) ** 0.5)
        v.tensor_tensor(k.cumz[:, :, :], over(k.cum[0:8, :], 8), eye.unsqueeze(2).broadcast_to([8, 8, TOK]),
                        ALU.mult)
    elif step == 7:
        dve.wait_ge(k.gexp_ready, l + 1)
        q, kk = k.p2[:, T_GQ:T_GQ + 2, :], k.p2[:, T_GK:T_GK + 2, :]
        v.scalar_tensor_tensor(q, q, HD ** -0.5, k.e1[:, :, :], ALU.mult, ALU.mult)
        v.tensor_tensor(kk, kk, k.e2[:, :, :], ALU.mult)


def act_branch_gates(k, act, l, start, loop):
    def one(i, p, ahead_size):
        ahead(split_hi, k, act, p, ahead_size, IN_K)
        if i == 0:
            act.wait_ge(k.acc_free, p.count(2))
        act.wait_ge(k.panel_done, p.count(3))
        at = T_GA + 2 * i
        k.nc.scalar.activation(k.p2[:, at:at + 2, :], k.acc[:, 2 * p.par:2 * p.par + 2, 0:TOK],
                               ACT.Sigmoid).then_inc(k.acc_free, 1)
        act_gates2_step(k, act, l, i)
    section(act, start, IN2_GATES, one, loop, (AB_K, AB_K), unrolled=True)


def dve_branch_gates(k, dve, l, start, loop):
    def one(i, p, ahead_size):
        ahead(split_lo, k, dve, p, ahead_size, IN_K)
        dve_gates2_step(k, dve, l, i)
    section(dve, start, IN2_GATES, one, loop, (AB_K, AB_K), unrolled=True)




FOX_STEPS = [(i, b) for i in range(FOX_PAIRS) for b in range(3)]


def fox_nth(l, q, h):
    return l * (2 * len(FOX_STEPS)) + (2 * q + h + 1)


def pool_fox(k, pool):
    k.nc.gpsimd.memset(k.fkz[:, :, :, :], 0.0)
    k.nc.gpsimd.memset(k.fvz[:, :, :, :, :], 0.0)
    pool.drain()


def pe_fox(k, pe, l):
    nc = k.nc
    ident = const(k, "ident")

    def token_major(i):
        for b, (lo, hi) in enumerate(BLOCKS):
            last = nc.tensor.transpose(k.mb[0:hi - lo, 3, b * P:(b + 1) * P], k.p2[:, T_FV + i, lo:hi], ident)
        last.then_inc(k.fox_tok, 1)

    def scores(q):
        i, b = FOX_STEPS[q]
        lo, hi = BLOCKS[b]
        for h in range(2):
            if b == 0:
                pe.wait_ge(k.fox_copy, l * FOX_PAIRS + (i + 1))
            if q > 0:
                pe.wait_ge(k.fox_masked, fox_nth(l, q - 1, h))
            out = k.mb[:, h, 0:hi]
            nc.tensor.matmul(out, k.p2[:, T_FQ + i, lo:lo + P], k.fkz[:, i % 2, h, 0:hi], start=True, stop=False)
            nc.tensor.matmul(out, k.minus8[:, :], k.cumz[:, i * 2 + h, 0:hi],
                             start=False, stop=True).then_inc(k.fox_sc, 1)
    token_major(0)
    scores(0)
    for q, (i, b) in enumerate(FOX_STEPS):
        lo, hi = BLOCKS[b]
        n = hi - lo
        for h in range(2):
            pe.wait_ge(k.fox_norm, fox_nth(l, q, h))
            settle(k, pe)
            tr = (k.mb[:, 2, :], k.acc[:, 2, :])[h]
            for c in range(b + 1):
                clo, chi = BLOCKS[c]
                last = nc.tensor.transpose(tr[0:chi - clo, c * P:c * P + n], k.fp[0:n, h, clo:chi],
                                           ident[0:n, 0:n])
            last.then_inc(k.fox_tr, 1)
        if q + 1 < len(FOX_STEPS):
            scores(q + 1)
        if b == 1 and i + 1 < FOX_PAIRS:
            token_major(i + 1)
        pe.wait_ge(k.fox_tok_evac, l * FOX_PAIRS + (i + 1))
        if b == 0 and i > 1:
            pe.wait_ge(k.t_ready, l * FOX_PAIRS + i)
        for h in range(2):
            pe.wait_ge(k.fox_pt, fox_nth(l, q, h))
            settle(k, pe)
            for c in range(b + 1):
                clo, chi = BLOCKS[c]
                last = nc.tensor.matmul(k.acc[:, i % 2, lo:hi], k.fvz[0:chi - clo, i % 2, c, h, :],
                                        k.fpt[0:chi - clo, h, c, 0:n],
                                        start=(h == 0 and c == 0), stop=(h == 1 and c == b))
            last.then_inc(k.fox_pv, 1)


def act_fox(k, act, l):
    a = k.nc.scalar.activation

    def keys(i):
        for h, rows in enumerate(HALVES):
            last = a(k.fkz[rows, i % 2, h, :], k.p2[rows, T_FK + i, :], ACT.Copy)
        last.then_inc(k.fox_copy, 1)

    def values(i):
        act.wait_ge(k.fox_tok, l * FOX_PAIRS + (i + 1))
        for h in range(2):
            src = k.mb[:, 3, 0:3 * P].rearrange("p (c n) -> p c n", c=3)[:, :, HALVES[h]]
            a(k.fvz[0:META, i % 2, 0, h, HALVES[h]], src[0:META, 0], ACT.Copy)
            last = a(k.fvz[:, i % 2, 1:3, h, HALVES[h]], src[:, 1:3], ACT.Copy)
        last.then_inc(k.fox_tok_evac, 1)

    def output(i):
        act.wait_ge(k.t_ready, l * FOX_PAIRS + (i + 2))
        a(k.y_hi[:, i, :], k.fy[:, i % 2, :], ACT.Copy).then_inc(k.y_ready, 1)
    keys(0)
    values(0)
    for q, (i, b) in enumerate(FOX_STEPS):
        lo, hi = BLOCKS[b]
        n = hi - lo
        for h in range(2):
            act.wait_ge(k.max_ready, fox_nth(l, q, h) + 8)
            if q > 0:
                act.wait_ge(k.fox_tr, fox_nth(l, q - 1, h))
            a(k.fp[0:n, h, 0:hi], k.fs[0:n, h, 0:hi], ACT.Exp, bias=k.fstat[0:n, h, 0:1],
              accum_out=k.fstat[0:n, h, 1:2]).then_inc(k.fox_p, 1)
        if b == 0 and i + 1 < FOX_PAIRS:
            keys(i + 1)
        for h in range(2):
            act.wait_ge(k.fox_tr, fox_nth(l, q, h))
            if q > 0:
                act.wait_ge(k.fox_pv, fox_nth(l, q - 1, h))
            tr = (k.mb[:, 2, :], k.acc[:, 2, :])[h]
            for c in range(b + 1):
                clo, chi = BLOCKS[c]
                last = a(k.fpt[0:chi - clo, h, c, 0:n], tr[0:chi - clo, c * P:c * P + n], ACT.Copy)
            last.then_inc(k.fox_pt, 1)
        if b == 1 and i + 1 < FOX_PAIRS:
            values(i + 1)
        if b == 0 and i > 0:
            output(i - 1)
    output(FOX_PAIRS - 1)


def dve_fox(k, dve, l):
    v = k.nc.vector
    mask = const(k, "mask_fox")

    def output(i):
        dve.wait_ge(k.fox_pv, fox_nth(l, 3 * i + 2, 1))
        v.tensor_copy(k.fy[:, i % 2, :], k.acc[:, i % 2, 0:TOK]).then_inc(k.t_ready, 1)

    def output_lo(i):
        dve.wait_ge(k.y_ready, l * FOX_PAIRS + (i + 1))
        v.tensor_tensor(k.y_lo[:, i, :], k.fy[:, i % 2, :], k.y_hi[:, i, :].bitcast(F32), ALU.subtract)
    for q, (i, b) in enumerate(FOX_STEPS):
        lo, hi = BLOCKS[b]
        n = hi - lo
        at = (TOK - P) - lo
        for h in range(2):
            dve.wait_ge(k.fox_sc, fox_nth(l, q, h))
            v.scalar_tensor_tensor(k.fs[0:n, h, 0:hi], k.mb[0:n, h, 0:hi], HD ** -0.5, mask[0:n, at:at + hi],
                                   ALU.mult, ALU.add).then_inc(k.fox_masked, 1)
            dve.drain()
            v.tensor_reduce(k.fstat[0:n, h, 0:1], k.fs[0:n, h, 0:hi], AX, ALU.max, negate=True).then_inc(k.max_ready, 1)
        if b == 0 and i > 0:
            output(i - 1)
        for h in range(2):
            dve.wait_ge(k.fox_p, fox_nth(l, q, h))
            v.reciprocal(k.fstat[0:n, h, 2:3], k.fstat[0:n, h, 1:2])
            dve.drain()
            v.tensor_scalar(k.fp[0:n, h, 0:hi], k.fp[0:n, h, 0:hi], k.fstat[0:n, h, 2:3], None,
                            ALU.mult).then_inc(k.fox_norm, 1)
        if b == 1 and i > 0:
            output_lo(i - 1)
    output(FOX_PAIRS - 1)
    dve.drain()
    output_lo(FOX_PAIRS - 1)




def pool_gla(k, pool):
    for s in STREAMS:
        k.nc.gpsimd.memset(k.g[s]["kz"][:, :, :], 0.0)
        k.nc.gpsimd.memset(k.g[s]["scaled"][:, :, :, :], 0.0).then_inc(k.gla_zero, 1)


def gla_chunk(n):
    return slice(n * GLA_C, (n + 1) * GLA_C)


def pe_gla(k, pe, l):
    nc = k.nc
    mm = nc.tensor.matmul
    ident = const(k, "ident")
    banks = (k.mb, k.acc)
    for s in STREAMS:
        for n in range(GLA_N):
            nc.tensor.transpose(banks[s][0:GLA_C, 2, n * P:(n + 1) * P], k.p2[:, T_GK + s, gla_chunk(n)], ident)
            for h in range(2):
                last = nc.tensor.transpose(banks[s][0:GLA_C, h, n * P:(n + 1) * P],
                                           k.p2[:, T_GV + 2 * s + h, gla_chunk(n)], ident)
        last.then_inc(k.gla_tok, 1)
    for s in STREAMS:
        pe.wait_ge(k.gla_copy, nth(l, 1, 0, s))
        for h in range(2):
            if h == 1:
                pe.wait_ge(k.gla_tok_evac, nth(l, 1, 0, s))
            for n in range(GLA_N):
                c = gla_chunk(n)
                last = mm(banks[s][0:GLA_C, 3 - h, c], k.g[s]["kz"][:, h, c], k.p2[:, T_GQ + s, c],
                          start=True, stop=True)
        last.then_inc(k.gla_att, 1)
    for s in STREAMS:
        for h in range(2):
            for n in range(GLA_N - 1):
                last = mm(banks[s][:, h, n * P:(n + 1) * P], k.g[s]["kt"][:, n, :], k.g[s]["vt"][:, n, h, :],
                          start=True, stop=True)
        last.then_inc(k.gla_state, 1)
    for s in STREAMS:
        pe.wait_ge(k.gla_att_evac, nth(l, 1, 0, s))
        pe.wait_ge(k.gla_state_evac, l + 1)
        for h in range(2):
            for n in range(GLA_N):
                c = gla_chunk(n)
                out = banks[s][:, 3 - h, c]
                last = mm(out, k.g[s]["vt"][:, n, h, :], k.g[s]["at"][:, n, h, :], start=True, stop=n == 0)
                if n > 0:
                    last = mm(out, k.g[s]["scaled"][:, n - 1, h, :], k.p2[:, T_GQ + s, c], start=False, stop=True)
        last.then_inc(k.gla_o, 1)
    for s in STREAMS:
        pe.wait_ge(k.gla_sq, nth(l, 1, 0, s))
        for h in range(2):
            last = mm(banks[s][:, h, 0:TOK], k.mean_ones[:, :], k.g[s]["sq"][:, h, :], start=True, stop=True)
        last.then_inc(k.gla_mean, 1)


def act_gla(k, act, l):
    a = k.nc.scalar.activation
    banks = (k.mb, k.acc)
    act.wait_ge(k.gla_zero, l * 2 + 2)
    settle(k, act)
    for s in STREAMS:
        for h, rows in enumerate(HALVES):
            last = a(k.g[s]["kz"][rows, h, :], k.p2[rows, T_GK + s, :], ACT.Copy)
        last.then_inc(k.gla_copy, 1)
    for s in STREAMS:
        act.wait_ge(k.gla_tok, nth(l, 1, 0, s))
        a(k.g[s]["kt"][:, :, :], banks[s][0:GLA_C, 2, :].rearrange("p (n c) -> p n c", n=GLA_N), ACT.Copy)
        for h in range(2):
            last = a(k.g[s]["vt"][:, :, h, :], banks[s][0:GLA_C, h, :].rearrange("p (n c) -> p n c", n=GLA_N),
                     ACT.Copy)
        last.then_inc(k.gla_tok_evac, 1)
    for s in STREAMS:
        act.wait_ge(k.gla_o, nth(l, 1, 0, s))
        for h in range(2):
            last = a(k.g[s]["sq"][:, h, :], banks[s][:, 3 - h, 0:TOK], ACT.Square)
        last.then_inc(k.gla_sq, 1)
    for s in STREAMS:
        for h in range(2):
            last = a(k.g[s]["o"][:, h, :], banks[s][:, 3 - h, 0:TOK], ACT.Copy)
    for s in STREAMS:
        act.wait_ge(k.gla_mean, nth(l, 1, 0, s))
        last = a(k.g[s]["sq"][:, :, :], banks[s][:, 0:2, 0:TOK], ACT.Sqrt, bias=k.eps[:, 0:1], scale=float(D) / P)
        last.then_inc(k.gla_root, 1)
    for s in STREAMS:
        act.wait_ge(k.wh_y, nth(l, 1, 0, s))
        at = 4 + 2 * s
        a(k.y_hi[:, at:at + 2, :], k.g[s]["o"][:, :, :], ACT.Copy).then_inc(k.gyh_ready, 1)


def dve_gla(k, dve, l):
    v = k.nc.vector
    gm = const(k, "gla_mask", slice(0, GLA_C))
    banks = (k.mb, k.acc)
    dve.wait_ge(k.gla_zero, l * 2 + 2)
    settle(k, dve)
    for s in STREAMS:
        dve.wait_ge(k.gla_att, nth(l, 1, 0, s))
        for h in range(2):
            last = v.tensor_tensor(k.g[s]["at"][:, :, h, :],
                                   banks[s][0:GLA_C, 3 - h, 0:TOK].rearrange("p (n c) -> p n c", n=GLA_N),
                                   over(gm, GLA_N), ALU.mult)
        last.then_inc(k.gla_att_evac, 1)
    dve.wait_ge(k.gla_state, l * 2 + 2)
    heads = [(s, h, rows) for s in STREAMS for h, rows in enumerate(HALVES)]
    for n in range(GLA_N - 1):
        for s, h, rows in heads:
            state = k.g[s]["state"][rows, :]
            if n > 0:
                v.tensor_scalar(state, state, k.gst[rows, s, 1, n:n + 1], None, ALU.mult)
        if n > 0:
            dve.drain()
        for s, h, rows in heads:
            state = k.g[s]["state"][rows, :]
            add = banks[s][rows, h, n * P:(n + 1) * P]
            if n > 0:
                v.scalar_tensor_tensor(state, add, k.gst[rows, s, 2, n:n + 1], state, ALU.mult, ALU.add)
            else:
                v.tensor_scalar(state, add, k.gst[rows, s, 2, n:n + 1], None, ALU.mult)
        dve.drain()
        for s, h, rows in heads:
            last = v.tensor_scalar(k.g[s]["scaled"][rows, n, h, :], k.g[s]["state"][rows, :],
                                   k.gst[rows, s, 0, n + 1:n + 2], None, ALU.mult)
    last.then_inc(k.gla_state_evac, 1)
    v.tensor_tensor(k.gr_[:, :, :], k.gr_[:, :, :], k.p2[:, T_GR:T_GR + 4, :], ALU.mult)
    for s in STREAMS:
        sq, o = k.g[s]["sq"], k.g[s]["o"]
        dve.wait_ge(k.gla_root, nth(l, 1, 0, s))
        v.reciprocal(sq[:, :, :], sq[:, :, :])
        dve.drain()
        for h in range(2):
            v.scalar_tensor_tensor(o[:, h, :], o[:, h, :], vec(k, "g_gla", 2 * s + h, l), sq[:, h, :], ALU.mult,
                                   ALU.mult)
        dve.drain()
        v.tensor_tensor(o[:, :, :], o[:, :, :], k.gr_[:, 2 * s:2 * s + 2, :], ALU.mult).then_inc(k.wh_y, 1)
    dve.drain()
    for s in STREAMS:
        at = 4 + 2 * s
        dve.wait_ge(k.gyh_ready, nth(l, 1, 0, s))
        v.tensor_tensor(k.y_lo[:, at:at + 2, :], k.g[s]["o"][:, :, :], k.y_hi[:, at:at + 2, :].bitcast(F32),
                        ALU.subtract)



W1 = slice(META, TOK)
W2 = slice(0, TOK)


def program_tensor(k, pe):
    pe.sem_inc(k.ada_done, 2)
    pe.sem_inc(k.tok_mm, 8)
    pe.sem_inc(k.panel_done, 2)
    pe.sem_inc(k.p_tr, 2)
    pe.sem_inc(k.pv_done, 2)
    pe.wait_ge(k.const_ready, 1)
    pe_pre(k, pe, 0, W1)
    with pe.Fori(0, ADA_FIRST // 2) as i:
        for b in range(2):
            pe_ada(k, pe, i * 2 + b, b)
    for i in range(ADA_MORE):
        pe_project(k, pe, i, 1, 2, W1, ready=(k.hl_ready, 0) if i == 0 else None)
        pe_ada(k, pe, ADA_FIRST + i, i % 2)
    pe_project(k, pe, ADA_MORE, IN1 - ADA_MORE, 2, W1, ada=True)
    pe_ada(k, pe, ADA_PRELOADED + ADA_LAST - 1, 1)
    stage_end(k, pe, 1)
    pe_att(k, pe)
    stage_end(k, pe, 2)
    pe_rwkv_prep(k, pe)
    stage_end(k, pe, 3)
    pe_rwkv_pairs(k, pe)
    pe_rwkv_out(k, pe)
    stage_end(k, pe, 4)
    pe_branches(k, pe, M_AB1, SEQ, k.y1_hi, k.y1_lo, RT)
    pe_project(k, pe, M_OUT1, OUT, 2, W1, ready=(k.yl_ready, 0))
    pe_stat(k, pe, 0, W1)
    pe_ffn(k, pe, 0, 1, M_GU1, M_DOWN1, W1)
    with pe.Fori(0, LAYERS) as l:
        loop = l * (L_PANELS // 2)
        pe_ffn(k, pe, l * 2 + 1, l * 3 + 2, M_LAYER + L_GUA, M_LAYER + L_DOWNA, W2, loop)
        pe_pre(k, pe, l * 3 + 3, W2)
        pe_project(k, pe, M_LAYER + L_SINGLE, SINGLES, 1, W2, loop, ready=(k.hl_ready, (l * 3 + 3) * KT))
        pe_project(k, pe, M_LAYER + L_IN, IN2 - IN2_GATES, 2, W2, loop)
        pe_gates2(k, pe, l)
        pe_project(k, pe, M_LAYER + L_IN + IN2 - IN2_GATES, IN2_GATES, 2, W2, loop)
        stage_end(k, pe, l * 4 + 5)
        stage_end(k, pe, l * 4 + 6)
        pe_fox(k, pe, l)
        stage_end(k, pe, l * 4 + 7)
        pe_gla(k, pe, l)
        stage_end(k, pe, l * 4 + 8)
        pe_branches(k, pe, M_LAYER + L_AB, TOK, k.y_hi, k.y_lo, 4, loop)
        pe_project(k, pe, M_LAYER + L_OUT, OUT, 2, W2, loop, ready=(k.yl_ready, (l + 1) * KT))
        pe_stat(k, pe, l * 3 + 3, W2)
        pe_ffn(k, pe, l * 2 + 2, l * 3 + 4, M_LAYER + L_GUB, M_LAYER + L_DOWNB, W2, loop)


def prologue(fn, k, eng, start, size, loop=0):
    for b in range(2):
        fn(k, eng, Panel.of(start + b, loop), size)


def program_scalar(k, act, d):
    nc = k.nc
    act.dma_start(k.x[:, :, W1], d["x"]).then_inc(k.x_loaded, 16)
    act.dma_start(k.x[:, :, 0:META], d["meta"]).then_inc(k.x_loaded, 16)
    act.dma_start(k.const[:, :], d["const"]).then_inc(k.const_loaded, 16)
    act.wait_ge(k.vec_loaded, 16)
    nc.scalar.activation(k.csil[:, :], vec(k, "c", n=KT), ACT.Sigmoid).then_inc(k.csig, 1)
    act.wait_ge(k.const_ready, 1)
    act.wait_ge(k.x_loaded, 32)
    act_pre_sums(k, act, 0, W1)
    prologue(split_hi, k, act, 0, IN_K)
    act_pre_split(k, act, 0, W1, lambda t: k.mod[:, t:t + 1])
    act.wait_ge(k.const_ready, 2)
    act_copy_out(k, act, 0, 10, 2, lambda i: k.p_in[:, bass.ds(i * 2, 2), 1:SEQ + 1], SEQ, IN_K, (IN_K, IN_K),
                 signal=k.pin_ready)
    act_copy_out(k, act, 10, 9, 2, lambda i: k.qkv[:, bass.ds(i * 2, 2), :], SEQ, IN_K, (IN_K, IN_K))
    act_copy_out(k, act, 19, 8, 2, lambda i: k.gates[:, bass.ds(i * 2, 2), :], SEQ, IN_K, (None, None))
    act.wait_ge(k.const_loaded, 16)
    stage_end(k, act, 1)
    act_att(k, act)
    stage_end(k, act, 2)
    act_rwkv_prep(k, act)
    nc.scalar.activation(k.gates[:, :, :], k.gates[:, :, :], ACT.Sigmoid)
    stage_end(k, act, 3)
    act_rwkv_pairs(k, act)
    act_rwkv_out(k, act)
    stage_end(k, act, 4)
    act_merge(k, act, 0, M_AB1, SEQ, W1, (OUT_K, OUT_K))
    act_products(k, act, 0, M_OUT1, 2, W1, OUT_K, (GU_K, GU_K))
    act_post_root(k, act, 0, W1)
    act_pre(k, act, 1, W1, lambda t: k.mod[:, 24 + t:25 + t], updates=0)
    act_ffn(k, act, 0, M_GU1, M_DOWN1, 1, W1, (None, None))
    with act.Fori(0, LAYERS) as l:
        loop = l * (L_PANELS // 2)
        prologue(split_hi, k, act, M_LAYER, GU_K, loop)
        act_pre(k, act, l * 3 + 2, W2, updates=l * 3 + 1)
        act_ffn(k, act, l * 2 + 1, M_LAYER + L_GUA, M_LAYER + L_DOWNA, l * 3 + 2, W2, (AB_K, AB_K), loop)
        act_pre(k, act, l * 3 + 3, W2, updates=l * 3 + 2)
        act_ahead_only(k, act, M_LAYER + L_SINGLE, SINGLES, AB_K, (IN_K, IN_K), loop)
        act_ahead_only(k, act, M_LAYER + L_IN, IN2 - IN2_GATES, IN_K, (IN_K, IN_K), loop)
        act_branch_gates(k, act, l, M_LAYER + L_IN + IN2 - IN2_GATES, loop)
        stage_end(k, act, l * 4 + 5)
        stage_end(k, act, l * 4 + 6)
        act_fox(k, act, l)
        stage_end(k, act, l * 4 + 7)
        act_gla(k, act, l)
        stage_end(k, act, l * 4 + 8)
        act_merge(k, act, l + 1, M_LAYER + L_AB, TOK, W2, (OUT_K, OUT_K), loop)
        act_products(k, act, l * 3 + 3, M_LAYER + L_OUT, 2, W2, OUT_K, (GU_K, GU_K), loop)
        act_post_root(k, act, l * 3 + 3, W2)
        act_pre(k, act, l * 3 + 4, W2, updates=l * 3 + 3)
        act_ffn(k, act, l * 2 + 2, M_LAYER + L_GUB, M_LAYER + L_DOWNB, l * 3 + 4, W2, (None, None), loop)


def program_vector(k, dve):
    v = k.nc.vector
    dve.sem_inc(k.lo_ready, 2)
    dve.sem_inc(k.acc_free, 2)
    dve.sem_inc(k.sq_used, 2)
    dve.sem_inc(k.pv_evac, 1)
    dve.sem_inc(k.masked, 2)
    dve.sem_inc(k.y_evac, 2)
    v.memset(k.ssum[:, :], 0.0)
    dve.wait_ge(k.csig, 1)
    v.tensor_tensor(k.csil[:, :], k.csil[:, :], vec(k, "c", n=KT), ALU.mult)
    for l in range(LAYERS):
        for name in ("post1", "post2"):
            p = vec(k, name, l * VEC_LAYER, n=KT)
            v.tensor_scalar(p, p, 0.5, None, ALU.mult)
    dve.drain()
    for i in range(ADA_FIRST):
        dve.drain()
        dve.wait_ge(k.ada_first_landed[i], 16)
        dve_ada(k, dve, i, i % 2, k.ada_first[:, i, :], True)
    dve_rstd(k, dve, 0, W1)
    dve.wait_ge(k.ada_done, ADA_FIRST + 2)
    dve_mod(k, dve, 0, 16)
    v.scalar_tensor_tensor(k.fold[:, 0, :], k.mod[:, 8:16], 1.0, vec(k, "g_pre_mix", n=KT), ALU.add, ALU.mult)
    dve.drain()
    dve_pre_apply(k, dve, 0, W1, lambda t: k.fold[:, 0, t:t + 1], lambda t: k.mod[:, t:t + 1])
    prologue(split_lo, k, dve, 0, IN_K)
    for i in range(ADA_FIRST, ADA_PRELOADED):
        dve.drain()
        dve.wait_ge(k.ada_first_landed[i], 16)
        dve_ada(k, dve, i, i % 2, k.ada_first[:, i, :], True)
    dve_split_with_ada(k, dve, 0, IN1, (None, None))
    dve.wait_ge(k.ada_done, ADA_PRELOADED + ADA_LAST + 2)
    dve_mod(k, dve, 16, 32)
    v.tensor_tensor(k.fold[:, 1, :], k.mod[:, 16:24], vec(k, "g_post_mix", n=KT), ALU.mult)
    v.scalar_tensor_tensor(k.fold[:, 2, :], k.mod[:, 32:40], 1.0, vec(k, "g_pre_ffn", n=KT), ALU.add, ALU.mult)
    v.tensor_tensor(k.fold[:, 3, :], k.mod[:, 40:48], vec(k, "g_post_ffn", n=KT), ALU.mult)
    stage_end(k, dve, 1)
    dve_att(k, dve)
    stage_end(k, dve, 2)
    dve_rwkv_prep(k, dve)
    stage_end(k, dve, 3)
    dve_rwkv_pairs(k, dve)
    dve_rwkv_out(k, dve)
    stage_end(k, dve, 4)
    dve_merge(k, dve, 0, M_AB1, SEQ, lambda t: tile(k.gates, t), lambda t: tile(k.gates, t + 8), W1, (OUT_K, OUT_K))
    dve_products(k, dve, 0, M_OUT1, 2, W1, OUT_K, (GU_K, GU_K))
    dve_post(k, dve, 0, W1, lambda t: k.fold[:, 1, t:t + 1], (M_GU1 + 1, GU_K))
    dve_pre(k, dve, 1, W1, lambda t: k.fold[:, 2, t:t + 1], lambda t: k.mod[:, 24 + t:25 + t])
    dve_ffn(k, dve, 0, M_GU1, M_DOWN1, 1, W1, lambda t: k.fold[:, 3, t:t + 1], (None, None))
    with dve.Fori(0, LAYERS) as l:
        loop = l * (L_PANELS // 2)

        def gain(name):
            return lambda t: vec(k, name, t, l)
        prologue(split_lo, k, dve, M_LAYER, GU_K, loop)
        dve_pre(k, dve, l * 3 + 2, W2, gain("pre1"))
        dve_ffn(k, dve, l * 2 + 1, M_LAYER + L_GUA, M_LAYER + L_DOWNA, l * 3 + 2, W2, gain("post1"),
                (AB_K, AB_K), loop)
        dve_pre(k, dve, l * 3 + 3, W2, gain("pre_mix"))

        def single(i):
            return k.small[:, :].unsqueeze(1) if i == 0 else k.p2[:, i - 1:i, :]
        dve_copy_out(k, dve, M_LAYER + L_SINGLE, SINGLES, 1, single, TOK, AB_K, (IN_K, IN_K), loop)
        dve_copy_out(k, dve, M_LAYER + L_IN, IN2 - IN2_GATES, 2, lambda i: k.p2[:, bass.ds(i * 2 + 2, 2), :], TOK,
                     IN_K, (IN_K, IN_K), loop)
        dve.drain()
        dve_branch_gates(k, dve, l, M_LAYER + L_IN + IN2 - IN2_GATES, loop)
        stage_end(k, dve, l * 4 + 5)
        stage_end(k, dve, l * 4 + 6)
        dve_fox(k, dve, l)
        stage_end(k, dve, l * 4 + 7)
        dve_gla(k, dve, l)
        stage_end(k, dve, l * 4 + 8)
        dve_merge(k, dve, l + 1, M_LAYER + L_AB, TOK, lambda t: tile(k.p2, t + T_GA), lambda t: tile(k.p2, t + T_GB),
                  W2, (OUT_K, OUT_K), loop)
        dve_products(k, dve, l * 3 + 3, M_LAYER + L_OUT, 2, W2, OUT_K, (GU_K, GU_K), loop)
        dve_post(k, dve, l * 3 + 3, W2, gain("post_mix"), (M_LAYER + L_GUB + 1, GU_K), loop)
        dve_pre(k, dve, l * 3 + 4, W2, gain("pre2"))
        dve_ffn(k, dve, l * 2 + 2, M_LAYER + L_GUB, M_LAYER + L_DOWNB, l * 3 + 4, W2, gain("post2"),
                (None, None), loop)


def program_gpsimd(k, pool, d):
    g = k.nc.gpsimd
    g.memset(k.mean_ones[:, :], 1.0 / D)
    g.memset(k.eps[:, 0:1], EPS)
    g.memset(k.eps[:, 1:2], GN_EPS).then_inc(k.const_ready, 1)
    pool.wait_ge(k.ada_products, ADA_FIRST)
    g.memset(k.p_in[:, :, 0:1], 0.0).then_inc(k.const_ready, 1)
    pool_shift(k, pool)
    stage_end(k, pool, 1)
    pool_att(k, pool)
    stage_end(k, pool, 2)
    pool_rwkv(k, pool, d)
    stage_end(k, pool, 3)
    rwkv_zero(k, g, 0, ZEROED_LATE[:ZEROED_BY_POOL])
    pool.drain()
    pool_rwkv_pairs(k, pool)
    stage_end(k, pool, 4)
    with pool.Fori(0, LAYERS) as l:
        pool.dma_start(k.wal[:, :], flat(d["wal"], l)).then_inc(k.dec_in, 16)
        stage_end(k, pool, l * 4 + 5)
        pool_fox(k, pool)
        stage_end(k, pool, l * 4 + 6)
        stage_end(k, pool, l * 4 + 7)
        pool_gla(k, pool)
        stage_end(k, pool, l * 4 + 8)


def build(nc, d):
    with ExitStack() as ctx:
        k = Kernel()
        k.nc = nc
        allocate(k, nc, ctx)
        semaphores(k, lambda name: ctx.enter_context(nc.semaphore(name)))
        block = ctx.enter_context(nc.Block())

        @block.sync
        def _(sp):
            program_sync(k, sp, d)

        @block.tensor
        def _(pe):
            program_tensor(k, pe)

        @block.scalar
        def _(act):
            program_scalar(k, act, d)

        @block.vector
        def _(dve):
            program_vector(k, dve)

        @block.gpsimd
        def _(pool):
            program_gpsimd(k, pool, d)



def panels(w, per):
    kt, nt = w.shape[0] // P, w.shape[1] // P
    return w.reshape(kt, P, nt // per, per, P).transpose(2, 1, 3, 0, 4).reshape(nt // per, P, per * kt * P)


def gate_up(w):
    return w.reshape(KT, P, 2, FT, P).transpose(3, 1, 2, 0, 4).reshape(FT, P, GU_K * P)


def columns(v):
    return v.reshape(-1, P).T


def lay_out(x):
    f = {name: np.asarray(a) for name, a in x.items()}
    d = {}
    d["x"] = np.ascontiguousarray(f["x"][0].T.reshape(KT, P, SEQ).transpose(1, 0, 2))
    d["meta"] = np.ascontiguousarray(f["meta_tokens_2"].T.reshape(KT, P, META).transpose(1, 0, 2))
    v = np.zeros((P, VEC_COLS), np.float32)

    def put(name, a, layer=0):
        at, n = VEC[name]
        at += layer * VEC_LAYER
        v[:, at:at + n] = columns(a.reshape(-1))
    for name, src in (("c", "c"), ("b_ada", "b_ada"), ("g_pre_mix",) * 2, ("g_post_mix",) * 2, ("mu", "mu_shift"),
                      ("w0",) * 2, ("a0",) * 2, ("k_k",) * 2, ("k_a",) * 2, ("r_k",) * 2, ("lnx_w",) * 2,
                      ("lnx_b",) * 2, ("g_pre_ffn",) * 2, ("g_post_ffn",) * 2):
        put(name, f[src])
    for l in range(LAYERS):
        for name, src in (("pre1", "g_pre_ffn1_2"), ("post1", "g_post_ffn1_2"), ("pre_mix", "g_pre_mix_2"),
                          ("post_mix", "g_post_mix_2"), ("pre2", "g_pre_ffn2_2"), ("post2", "g_post_ffn2_2"),
                          ("b_alpha", "b_alpha_2"), ("g_gla", "g_gla_out_2")):
            put(name, f[src][l], l)
        v[FF_ROWS, VEC["b_f"][0] + l * VEC_LAYER] = f["b_f_2"][l]
    d["vec"] = v
    d["const"] = constants()
    d["w_ada"] = panels(f["w_ada"][0], 2)
    w = f["w_in"][0]
    d["w_in"] = panels(w, 2)
    d["w_ab"] = panels(np.concatenate([f["w_a"][0], f["w_b"][0]], 0), 1)
    d["w_out"] = panels(f["w_out"][0], 2)
    d["w_gu"] = gate_up(f["w_ffn_in"][0])
    d["w_down"] = panels(f["w_ffn_out"][0], 1)
    low = np.zeros((2, P, RW), np.float32)
    low[0, 0:HD] = f["w2"][0]
    low[1, HD:P] = f["a2"][0]
    d["w2"], d["a2"], d["g2"] = low[0], low[1], f["g2"][0]
    c = np.arange(RW)
    heads = (c[:, None] // HD == np.arange(32)[None, :]).astype(np.float32)
    d["sel"] = heads.reshape(RT, P, 32).transpose(1, 0, 2).reshape(P, RT * 32)
    d["spread"] = heads.T
    wal = np.zeros((LAYERS, P, 256), np.float32)
    wal[:, 0:16] = f["w_alpha_up_2"]
    d["wal"] = wal

    def layers(fn):
        return np.concatenate([fn(l) for l in range(LAYERS)], 0)
    sizes = (512, 512, 512, 8, 256, 256, 512, 16, 512, 1024, 1024)
    ends = np.cumsum(sizes)

    def split_in(l):
        w = f["w_in_2"][l]
        fq, fk, fv, ff, gq, gk, gv, ga, gr, ma, mb = (w[:, e - s:e] for s, e in zip(sizes, ends))
        small = np.zeros((D, P), np.float32)
        small[:, 0:16] = ga
        small[:, FF_ROWS] = ff
        return small, np.concatenate([fq, fk, fv, gq, gk, gv, gr, ma, mb], 1)
    d["w_in_single_2"] = layers(lambda l: panels(np.concatenate([split_in(l)[0], split_in(l)[1][:, 0:2 * P]], 1), 1))
    d["w_in_2"] = layers(lambda l: panels(split_in(l)[1][:, 2 * P:], 2))
    d["w_ab_2"] = layers(lambda l: panels(np.concatenate([f["w_fox_o_2"][l], f["w_gla_o_2"][l]], 0), 1))
    d["w_out_2"] = layers(lambda l: panels(f["w_out_2"][l], 2))
    for n in ("1", "2"):
        d["w_gu" + n + "_2"] = layers(lambda l: gate_up(f["w_ffn" + n + "_gu_2"][l]))
        d["w_down" + n + "_2"] = layers(lambda l: panels(f["w_ffn" + n + "_down_2"][l], 1))
    return {name: np.ascontiguousarray(a) for name, a in d.items()}


def kernel(**inputs):
    import concourse.bacc as bacc
    from concourse.bass_utils import run_bass_kernel_spmd as run

    nc = bacc.Bacc("TRN2", target_bir_lowering=False, num_devices=1)
    arrays = {f"in_{name}": a for name, a in lay_out(inputs).items()}
    d = {name[3:]: nc.dram_tensor(name, a.shape, F32, kind="ExternalInput").ap() for name, a in arrays.items()}
    d["out"] = nc.dram_tensor("out_x", (P, KT, SEQ), F32, kind="ExternalOutput").ap()
    build(nc, d)
    got = run(nc, [arrays], core_ids=[0]).results[0]["out_x"]
    return np.ascontiguousarray(got.transpose(2, 1, 0).reshape(1, SEQ, D))
```
